# Optimizing a Trainium2 kernel written in Bass

```python
import math
import jax, jax.numpy as jnp
from jax import lax
import numpy as np

D_MODEL = 1024
BATCH = 1
SEQ = 512
DEPTH = 2

N_MEM = 256
BLOCK_Q = 128
MIX_WIDTH = D_MODEL
MEM_WIDTH = D_MODEL // 4
MAIN_WIDTH = MIX_WIDTH - MEM_WIDTH
MEM_HEADS = 4
MEM_DIM = MEM_WIDTH // MEM_HEADS
MLA_V = 64
MLA_HEADS = MAIN_WIDTH // MLA_V
MLA_NOPE = 64
MLA_ROPE = 32
MLA_QK = MLA_NOPE + MLA_ROPE
Q_LORA = 384
KV_LORA = 256
ROPE_THETA = 10000.0
MAX_POS_OFFSET = 4096
FOX_DIM = 64
FOX_HEADS = MAIN_WIDTH // FOX_DIM
EPS = 1e-6
N_A = (DEPTH + 1) // 2
N_B = DEPTH // 2
A_IN = Q_LORA + KV_LORA + MLA_ROPE + MEM_WIDTH + MIX_WIDTH
B_IN = 3 * MAIN_WIDTH + FOX_HEADS + MEM_WIDTH + MIX_WIDTH


def rms_norm(x, g):
    xf = x.astype(jnp.float32)
    y = xf * lax.rsqrt(jnp.mean(xf * xf, axis=-1, keepdims=True) + EPS)
    return (y * g.astype(jnp.float32)).astype(x.dtype)

def split_cols(a, sizes):
    idx = np.cumsum(sizes)[:-1].tolist()
    return jnp.split(a, idx, axis=-1)

def rope(x, pos):
    half = x.shape[-1] // 2
    inv = ROPE_THETA ** (-jnp.arange(half, dtype=jnp.float32) / half)
    ang = pos.astype(jnp.float32)[..., None] * inv
    if x.ndim == 4:
        ang = ang[:, :, None, :]
    cos, sin = jnp.cos(ang), jnp.sin(ang)
    x1 = x[..., :half].astype(jnp.float32)
    x2 = x[..., half:].astype(jnp.float32)
    return jnp.concatenate([x1 * cos - x2 * sin, x2 * cos + x1 * sin], axis=-1).astype(x.dtype)

def causal_block_attention(q, k, v, scale, log_f_cum=None):
    B, S, H, Dk = q.shape
    nb = S // BLOCK_Q
    qb = q.reshape(B, nb, BLOCK_Q, H, Dk).swapaxes(0, 1)
    blk = jnp.arange(nb)
    key_pos = jnp.arange(S)
    if log_f_cum is not None:
        f_t = log_f_cum.transpose(0, 2, 1)
        fb = jnp.moveaxis(f_t.reshape(B, H, nb, BLOCK_Q), 2, 0)
        xs = (blk, qb, fb)
    else:
        xs = (blk, qb)

    def one_block(args):
        i, q_i = args[0], args[1]
        s = jnp.einsum('bqhd,bkhd->bhqk', q_i, k,
                       preferred_element_type=jnp.float32) * scale
        if log_f_cum is not None:
            s = s + (args[2][..., None].astype(jnp.float32) - f_t[:, :, None, :].astype(jnp.float32))
        q_pos = i * BLOCK_Q + jnp.arange(BLOCK_Q)
        mask = key_pos[None, :] <= q_pos[:, None]
        s = jnp.where(mask, s, -jnp.inf)
        p = jax.nn.softmax(s, axis=-1)
        return jnp.einsum('bhqk,bkhd->bqhd', p.astype(v.dtype), v)

    out = lax.map(one_block, xs)
    return out.swapaxes(0, 1).reshape(B, S, H, v.shape[-1])

def memory_attention(q, k, v):
    s = jnp.einsum('bshd,bmhd->bhsm', q, k,
                   preferred_element_type=jnp.float32) * (MEM_DIM ** -0.5)
    p = jax.nn.softmax(s, axis=-1)
    return jnp.einsum('bhsm,bmhd->bshd', p.astype(v.dtype), v)

def mla_mixer(c_q, c_kv, k_r, pos, q_norm, kv_norm, w_q_up, w_kv_up):
    B, S, _ = c_q.shape
    q = (rms_norm(c_q, q_norm) @ w_q_up).reshape(B, S, MLA_HEADS, MLA_QK)
    q_nope, q_rope = q[..., :MLA_NOPE], rope(q[..., MLA_NOPE:], pos)
    kv = (rms_norm(c_kv, kv_norm) @ w_kv_up).reshape(B, S, MLA_HEADS, MLA_NOPE + MLA_V)
    k_nope, v = kv[..., :MLA_NOPE], kv[..., MLA_NOPE:]
    k_rope = jnp.broadcast_to(rope(k_r, pos)[:, :, None, :], (B, S, MLA_HEADS, MLA_ROPE))
    qf = jnp.concatenate([q_nope, q_rope], axis=-1)
    kf = jnp.concatenate([k_nope, k_rope], axis=-1)
    out = causal_block_attention(qf, kf, v, MLA_QK ** -0.5)
    return out.reshape(B, S, MAIN_WIDTH)

def fox_mixer(q, k, v, f_logit, b_f):
    B, S, _ = q.shape
    log_f = jax.nn.log_sigmoid(f_logit.astype(jnp.float32) + b_f.astype(jnp.float32))
    log_f_cum = jnp.cumsum(log_f, axis=1)
    qh = q.reshape(B, S, FOX_HEADS, FOX_DIM)
    kh = k.reshape(B, S, FOX_HEADS, FOX_DIM)
    vh = v.reshape(B, S, FOX_HEADS, FOX_DIM)
    out = causal_block_attention(qh, kh, vh, FOX_DIM ** -0.5, log_f_cum)
    return out.reshape(B, S, MAIN_WIDTH)

def first_inputs(seed: int = 0) -> dict:
    key = jax.random.key(seed)
    ks = jax.random.split(key, 16)
    f32 = jnp.float32

    def nrm(k, shape, fan_in):
        return jax.random.normal(k, shape, f32) * (fan_in ** -0.5)

    def gain(k, shape):
        return 1.0 + 0.01 * jax.random.normal(k, shape, f32)

    x = jax.random.normal(ks[0], (BATCH, SEQ, D_MODEL), f32)
    mem = jax.random.normal(ks[1], (BATCH, N_MEM, D_MODEL), f32)
    positions = (jax.random.randint(ks[2], (BATCH, 1), 0, MAX_POS_OFFSET, dtype=jnp.int32)
                 + jnp.arange(SEQ, dtype=jnp.int32)[None, :])
    return {
        "x": x,
        "mem": mem,
        "positions": positions,
        "norm_pre": gain(ks[3], (DEPTH, D_MODEL)),
        "norm_post": gain(ks[4], (DEPTH, D_MODEL)),
        "mem_norm": gain(ks[5], (D_MODEL,)),
        "w_mem_kv": nrm(ks[6], (DEPTH, D_MODEL, 2 * MEM_WIDTH), D_MODEL),
        "w_out": nrm(ks[7], (DEPTH, MIX_WIDTH, D_MODEL), MIX_WIDTH),
        "w_in_a": nrm(ks[8], (N_A, D_MODEL, A_IN), D_MODEL),
        "q_norm_a": gain(ks[9], (N_A, Q_LORA)),
        "kv_norm_a": gain(ks[10], (N_A, KV_LORA)),
        "w_q_up_a": nrm(ks[11], (N_A, Q_LORA, MLA_HEADS * MLA_QK), Q_LORA),
        "w_kv_up_a": nrm(ks[12], (N_A, KV_LORA, MLA_HEADS * (MLA_NOPE + MLA_V)), KV_LORA),
        "w_in_b": nrm(ks[13], (N_B, D_MODEL, B_IN), D_MODEL),
        "b_f": jax.random.uniform(ks[14], (N_B, FOX_HEADS), f32, 1.0, 4.0),
    }

def first_block(x, mem, positions, norm_pre, norm_post, mem_norm, w_mem_kv, w_out,
              w_in_a, q_norm_a, kv_norm_a, w_q_up_a, w_kv_up_a, w_in_b, b_f):
    B, S, _ = x.shape
    M = mem.shape[1]
    mem_n = rms_norm(mem, mem_norm)
    h = x
    for i in range(DEPTH):
        j = i // 2
        hn = rms_norm(h, norm_pre[i])
        mkv = (mem_n @ w_mem_kv[i]).reshape(M, 2, MEM_HEADS, MEM_DIM) if False else \
            (mem_n @ w_mem_kv[i]).reshape(B, M, 2, MEM_HEADS, MEM_DIM)
        k_m, v_m = mkv[:, :, 0], mkv[:, :, 1]
        if i % 2 == 0:
            proj = hn @ w_in_a[j]
            c_q, c_kv, k_r, q_m, gate = split_cols(
                proj, [Q_LORA, KV_LORA, MLA_ROPE, MEM_WIDTH, MIX_WIDTH])
            main = mla_mixer(c_q, c_kv, k_r, positions, q_norm_a[j], kv_norm_a[j],
                             w_q_up_a[j], w_kv_up_a[j])
        else:
            proj = hn @ w_in_b[j]
            q, k, v, f_logit, q_m, gate = split_cols(
                proj, [MAIN_WIDTH, MAIN_WIDTH, MAIN_WIDTH, FOX_HEADS, MEM_WIDTH, MIX_WIDTH])
            main = fox_mixer(q, k, v, f_logit, b_f[j])
        mem_out = memory_attention(q_m.reshape(B, S, MEM_HEADS, MEM_DIM), k_m, v_m)
        y = jnp.concatenate([main, mem_out.reshape(B, S, MEM_WIDTH)], axis=-1) * jax.nn.silu(gate)
        h = h + rms_norm(y @ w_out[i], norm_post[i])
    return h


DEPTH_2 = 1

CHUNK = 64
SSD_HEADS = 16
SSD_HEAD_DIM = 64
SSD_INNER = SSD_HEADS * SSD_HEAD_DIM
SSD_GROUPS = 2
SSD_STATE = 128
SSD_CONV = 4
SSD_SCAN_CHUNK = CHUNK
CONV_DIM = SSD_INNER + 2 * SSD_GROUPS * SSD_STATE
SB_HEADS = 16
SB_HEAD_DIM = 64
SB_INNER = SB_HEADS * SB_HEAD_DIM
SB_BLOCK = 128
N_BRANCH = 2
IN_SIZES = (SSD_INNER, CONV_DIM, SSD_HEADS, SB_INNER, SB_INNER, SB_INNER, SB_INNER, N_BRANCH * D_MODEL)
IN_COLS = sum(IN_SIZES)


def _split_points():
    pts, acc = [], 0
    for s in IN_SIZES[:-1]:
        acc += s
        pts.append(acc)
    return pts

def rmsnorm(x, w):
    xf = x.astype(jnp.float32)
    y = xf * lax.rsqrt(jnp.mean(xf * xf, axis=-1, keepdims=True) + EPS)
    return (y * w.astype(jnp.float32)).astype(x.dtype)

def gated_group_rmsnorm(y, z, w, groups):
    g = (y.astype(jnp.float32) * jax.nn.silu(z.astype(jnp.float32)))
    g = g.reshape(y.shape[:-1] + (groups, y.shape[-1] // groups))
    g = g * lax.rsqrt(jnp.mean(g * g, axis=-1, keepdims=True) + EPS)
    return (g.reshape(y.shape) * w.astype(jnp.float32)).astype(y.dtype)

def ssd_scan(xh, dt, a, bmat, cmat, d_skip):
    bsz, L, H, P = xh.shape
    G, N = bmat.shape[2], bmat.shape[3]
    R = H // G
    T = SSD_SCAN_CHUNK
    NC = L // T
    x_dt = (xh * dt[..., None]).reshape(bsz, NC, T, G, R, P)
    a_dt = jnp.transpose((dt * a).reshape(bsz, NC, T, G, R), (0, 3, 4, 1, 2))
    a_cs = jnp.cumsum(a_dt, axis=-1)
    bc = bmat.reshape(bsz, NC, T, G, N)
    cc = cmat.reshape(bsz, NC, T, G, N)
    seg = a_cs[..., :, None] - a_cs[..., None, :]
    causal = jnp.tril(jnp.ones((T, T), dtype=bool))
    decay = jnp.exp(jnp.where(causal, seg, -jnp.inf))
    scores = jnp.einsum('bclgn,bcsgn->bgcls', cc, bc)
    attn = scores[:, :, None] * decay
    y_diag = jnp.einsum('bgrcls,bcsgrp->bclgrp', attn, x_dt)
    decay_states = jnp.exp(a_cs[..., -1:] - a_cs)
    states = jnp.einsum('bclgn,bgrcl,bclgrp->bcgrpn', bc, decay_states, x_dt)
    chunk_decay = jnp.exp(a_cs[..., -1])

    def step(carry, inp):
        st, dec = inp
        new = carry * dec[..., None, None] + st
        return new, carry

    init = jnp.zeros((bsz, G, R, P, N), dtype=xh.dtype)
    _, prev = lax.scan(step, init, (jnp.moveaxis(states, 1, 0), jnp.moveaxis(chunk_decay, -1, 0)))
    prev = jnp.moveaxis(prev, 0, 1)
    y_off = jnp.einsum('bclgn,bcgrpn,bgrcl->bclgrp', cc, prev, jnp.exp(a_cs))
    y = (y_diag + y_off).reshape(bsz, L, H, P)
    return y + xh * d_skip[:, None]

def stick_breaking(q, k, v):
    bsz, L, H, Dh = q.shape
    scale = Dh ** -0.5
    outs = []
    for blk in range(L // SB_BLOCK):
        q0 = blk * SB_BLOCK
        kend = q0 + SB_BLOCK
        logits = jnp.einsum('bqhd,bkhd->bhqk', q[:, q0:kend], k[:, :kend]).astype(jnp.float32) * scale
        qi = q0 + jnp.arange(SB_BLOCK)[:, None]
        ki = jnp.arange(kend)[None, :]
        mask = ki < qi
        log_fail = jnp.where(mask, jax.nn.log_sigmoid(-logits), 0.0)
        between = lax.cumsum(log_fail, axis=3, reverse=True) - log_fail
        w = jnp.where(mask, jnp.exp(jax.nn.log_sigmoid(logits) + between), 0.0)
        outs.append(jnp.einsum('bhqk,bkhd->bqhd', w.astype(v.dtype), v[:, :kend]))
    return jnp.concatenate(outs, axis=1)

def hybrid_layer(x, norm_pre, w_in, b_gate, conv_w, conv_b, dt_bias, a_log, d_skip,
                 ssd_norm, w_ssd_proj, w_sb_proj, w_out, norm_post):
    bsz, L, _ = x.shape
    h = rmsnorm(x, norm_pre)
    proj = jnp.einsum('bld,de->ble', h, w_in)
    z_ssd, xbc, dt_raw, q, k, v, z_sb, gates = jnp.split(proj, _split_points(), axis=-1)

    xbc = lax.conv_general_dilated(
        xbc, conv_w[:, None, :], window_strides=(1,), padding=[(SSD_CONV - 1, 0)],
        dimension_numbers=('NWC', 'WIO', 'NWC'), feature_group_count=CONV_DIM) + conv_b
    xbc = jax.nn.silu(xbc)
    xs, bm, cm = jnp.split(xbc, [SSD_INNER, SSD_INNER + SSD_GROUPS * SSD_STATE], axis=-1)
    dt = jax.nn.softplus(dt_raw.astype(jnp.float32) + dt_bias.astype(jnp.float32))
    a = -jnp.exp(a_log.astype(jnp.float32))
    y = ssd_scan(xs.reshape(bsz, L, SSD_HEADS, SSD_HEAD_DIM).astype(jnp.float32), dt, a,
                 bm.reshape(bsz, L, SSD_GROUPS, SSD_STATE).astype(jnp.float32),
                 cm.reshape(bsz, L, SSD_GROUPS, SSD_STATE).astype(jnp.float32),
                 d_skip.astype(jnp.float32))
    y = y.reshape(bsz, L, SSD_INNER).astype(x.dtype)
    y = gated_group_rmsnorm(y, z_ssd, ssd_norm, SSD_GROUPS)
    y_ssd = jnp.einsum('ble,ed->bld', y, w_ssd_proj)

    o = stick_breaking(q.reshape(bsz, L, SB_HEADS, SB_HEAD_DIM),
                       k.reshape(bsz, L, SB_HEADS, SB_HEAD_DIM),
                       v.reshape(bsz, L, SB_HEADS, SB_HEAD_DIM)).reshape(bsz, L, SB_INNER)
    y_sb = jnp.einsum('ble,ed->bld', o * jax.nn.silu(z_sb), w_sb_proj)

    g = jax.nn.sigmoid(gates + b_gate)
    g_ssd, g_sb = jnp.split(g, [D_MODEL], axis=-1)
    merged = g_ssd * y_ssd + g_sb * y_sb
    out = jnp.einsum('bld,de->ble', merged, w_out)
    return x + rmsnorm(out, norm_post)

def second_inputs(seed: int = 0) -> dict:
    key = jax.random.key(seed)
    ks = jax.random.split(key, 16)
    f32 = jnp.float32
    x = jax.random.normal(ks[0], (BATCH, SEQ, D_MODEL), f32)
    norm_pre = 1.0 + 0.05 * jax.random.normal(ks[1], (DEPTH_2, D_MODEL), f32)
    w_in = jax.random.normal(ks[2], (DEPTH_2, D_MODEL, IN_COLS), f32) * D_MODEL ** -0.5
    b_gate = 0.02 * jax.random.normal(ks[3], (DEPTH_2, N_BRANCH * D_MODEL), f32)
    conv_w = jax.random.normal(ks[4], (DEPTH_2, SSD_CONV, CONV_DIM), f32) * SSD_CONV ** -0.5
    conv_b = 0.02 * jax.random.normal(ks[5], (DEPTH_2, CONV_DIM), f32)
    u = jax.random.uniform(ks[6], (DEPTH_2, SSD_HEADS), f32)
    dt0 = jnp.exp(u * (math.log(0.1) - math.log(0.001)) + math.log(0.001))
    dt_bias = dt0 + jnp.log(-jnp.expm1(-dt0))
    a_log = jnp.log(jax.random.uniform(ks[7], (DEPTH_2, SSD_HEADS), f32, 1.0, 16.0))
    d_skip = 1.0 + 0.05 * jax.random.normal(ks[8], (DEPTH_2, SSD_HEADS), f32)
    ssd_norm = 1.0 + 0.05 * jax.random.normal(ks[9], (DEPTH_2, SSD_INNER), f32)
    w_ssd_proj = jax.random.normal(ks[10], (DEPTH_2, SSD_INNER, D_MODEL), f32) * SSD_INNER ** -0.5
    w_sb_proj = jax.random.normal(ks[11], (DEPTH_2, SB_INNER, D_MODEL), f32) * SB_INNER ** -0.5
    w_out = jax.random.normal(ks[12], (DEPTH_2, D_MODEL, D_MODEL), f32) * D_MODEL ** -0.5
    norm_post = 1.0 + 0.05 * jax.random.normal(ks[13], (DEPTH_2, D_MODEL), f32)
    return {"x": x, "norm_pre": norm_pre, "w_in": w_in, "b_gate": b_gate,
            "conv_w": conv_w, "conv_b": conv_b, "dt_bias": dt_bias, "a_log": a_log,
            "d_skip": d_skip, "ssd_norm": ssd_norm, "w_ssd_proj": w_ssd_proj,
            "w_sb_proj": w_sb_proj, "w_out": w_out, "norm_post": norm_post}

def second_block(x, norm_pre, w_in, b_gate, conv_w, conv_b, dt_bias, a_log, d_skip,
              ssd_norm, w_ssd_proj, w_sb_proj, w_out, norm_post):
    for layer in range(DEPTH_2):
        x = hybrid_layer(x, norm_pre[layer], w_in[layer], b_gate[layer], conv_w[layer],
                         conv_b[layer], dt_bias[layer], a_log[layer], d_skip[layer],
                         ssd_norm[layer], w_ssd_proj[layer], w_sb_proj[layer],
                         w_out[layer], norm_post[layer])
    return x


def setup_inputs(seed=0):
    out = dict(first_inputs(seed))
    for name, value in second_inputs(seed + 1).items():
        if name != "x":
            out[name + "_2"] = value
    return out


def reference(
    x, mem, positions, norm_pre, norm_post, mem_norm, w_mem_kv, w_out, w_in_a, q_norm_a,
    kv_norm_a, w_q_up_a, w_kv_up_a, w_in_b, b_f, norm_pre_2, w_in_2, b_gate_2, conv_w_2,
    conv_b_2, dt_bias_2, a_log_2, d_skip_2, ssd_norm_2, w_ssd_proj_2, w_sb_proj_2, w_out_2,
    norm_post_2,
):
    x = first_block(
        x, mem, positions, norm_pre, norm_post, mem_norm, w_mem_kv, w_out, w_in_a, q_norm_a,
        kv_norm_a, w_q_up_a, w_kv_up_a, w_in_b, b_f,
    )
    return second_block(
        x, norm_pre_2, w_in_2, b_gate_2, conv_w_2, conv_b_2, dt_bias_2, a_log_2, d_skip_2,
        ssd_norm_2, w_ssd_proj_2, w_sb_proj_2, w_out_2, norm_post_2,
    )


_drawn_inputs = setup_inputs


def setup_inputs(seed=0):
    import zlib

    import numpy as np

    out = dict(_drawn_inputs(seed))
    spreads = {}
    factors = {'norm_post': 4.422,
     'mem_norm': 7.424,
     'q_norm_a': 6.038,
     'kv_norm_a': 3.917,
     'b_gate_2': 46.847,
     'conv_b_2': 17.932,
     'd_skip_2': 139.691,
     'norm_pre_2': 4.692,
     'dt_bias_2': 2.819,
     'a_log_2': 3.979,
     'ssd_norm_2': 23.935,
     'norm_post_2': 7.132}
    for name, (base, spread) in spreads.items():
        noise = np.random.default_rng([zlib.crc32(name.encode()), seed]).standard_normal(out[name].shape)
        drawn = base * np.exp(spread * noise) if base else spread * noise
        out[name] = __import__('jax').numpy.asarray(drawn.astype(out[name].dtype))
    for name, factor in factors.items():
        out[name] = (out[name] * factor).astype(out[name].dtype)
    return out
```

```python
from contextlib import ExitStack

import numpy as np
import concourse.bass as bass
from concourse import mybir

P = 128
F32 = mybir.dt.float32
I32 = mybir.dt.int32
BF16 = mybir.dt.bfloat16
ALU = mybir.AluOpType
ACT = mybir.ActivationFunctionType
AX = mybir.AxisListType
ds = bass.ds

D = 1024
T = 512
MB = T // P
KD = D // P
N_MEM = 256
MEMB = N_MEM // P
MEM_W, MAIN_W = D // 4, D - D // 4
HD = 64
MEM_H, A_H, B_H = MEM_W // HD, MAIN_W // HD, MAIN_W // HD
NOPE, ROPE = 64, 32
QK_A = NOPE + ROPE
HALF = ROPE // 2
Q_LORA, KV_LORA = 384, 256
LAT = Q_LORA + KV_LORA + ROPE
EPS = 1e-6
MASKED = -1e30
C_H, C_G, C_N, TAPS = 16, 2, 128, 4
INNER = C_H * HD
CONV = INNER + 2 * C_G * C_N
CONVC = CONV // P
XC = INNER // P
GH = C_H // C_G
ROPE_THETA = 10000.0
ARENA = 27136
SOFT_MAX = 40.0


class Count:

    def __init__(self, sem):
        self.sem, self.total = sem, 0

    def take(self, n):
        mark = Mark(self.sem, self.total)
        self.total += n
        return mark


class Mark:

    def __init__(self, sem, base):
        self.sem, self.base = sem, base

    def __call__(self, n):
        return self.sem, n + self.base


class Projection:

    def __init__(self, first, n, groups, k, width, src, product, dst, func, loop, w, c0, banks, done, evac):
        self.first = first
        self.n = n
        self.groups = groups
        self.k = k
        self.width = width
        self.src = src
        self.product = product
        self.dst = dst
        self.func = func
        self.loop = loop
        self.w = w
        self.c0 = c0
        self.banks = banks
        self.done = done
        self.evac = evac


class Norm:

    def __init__(self, src, dst, blocks, norms, parts, gain, stat, sq, root, rinv, scaled, turned, normed):
        self.src = src
        self.dst = dst
        self.blocks = blocks
        self.norms = norms
        self.parts = parts
        self.gain = gain
        self.stat = stat
        self.sq = sq
        self.root = root
        self.rinv = rinv
        self.scaled = scaled
        self.turned = turned
        self.normed = normed


class PostNorm:

    def __init__(self, sq, sum, root, out, add):
        self.sq = sq
        self.sum = sum
        self.root = root
        self.out = out
        self.add = add


class Attend:

    def __init__(self, heads, width, keys, causal, scale, q, k, v, y0, extra_q, extra_k, staged, headT,
                 headT_out, scores, neg_max, exped, probT, probT_out, attended, weighed):
        self.heads = heads
        self.width = width
        self.keys = keys
        self.causal = causal
        self.scale = scale
        self.q = q
        self.k = k
        self.v = v
        self.y0 = y0
        self.extra_q = extra_q
        self.extra_k = extra_k
        self.staged = staged
        self.headT = headT
        self.headT_out = headT_out
        self.scores = scores
        self.neg_max = neg_max
        self.exped = exped
        self.probT = probT
        self.probT_out = probT_out
        self.attended = attended
        self.weighed = weighed


class Staging:

    def __init__(self, staged, headT, headT_out):
        self.staged = staged
        self.headT = headT
        self.headT_out = headT_out


def reached(k, n, least):
    return not isinstance(k, int) or k > 0 or n >= least


def turns(eng, n, emit):
    emit(0, False)
    if n > 2:
        with eng.Fori(1, n - 1) as k:
            emit(k, False)
    if n > 1:
        emit(n - 1, True)


def build(nc, i, out):
    ctx = ExitStack()
    with ctx:
        def sb(name, shape, dt=F32):
            return ctx.enter_context(nc.sbuf_tensor(name, shape, dt))

        def count(name):
            return Count(ctx.enter_context(nc.semaphore(name)))

        bank = [ctx.enter_context(nc.psum_tensor(f"bank{n}", [P, 512], F32)) for n in range(8)]

        h = sb("h", [P, MB, D])
        hT = sb("hT", [P, KD, T])
        yT_t = sb("yT_t", [P, KD * T])
        yT = yT_t[:, :].rearrange("p (k t) -> p k t", k=KD)
        wslot = [sb(f"wslot{n}", [P, 4096]) for n in range(2)]
        hn = sb("hn", [P, 2, D])
        junk = sb("junk", [P, D])
        row = sb("row", [P, D])
        ident, tri_le, tri_gt, ones = (sb(n, [P, P]) for n in ("ident", "tri_le", "tri_gt", "ones"))
        neg_ge, neg_ones = (sb(n, [P, P]) for n in ("neg_ge", "neg_ones"))
        ident_b, later_keys, not_before = (sb(n, [P, P], BF16) for n in ("ident_b", "later_keys", "not_before"))
        gains = sb("gains", [P, 48])
        conv_k = sb("conv_k", [P, TAPS, CONVC])
        conv_b = sb("conv_b", [P, CONVC])
        small = sb("small", [P, 64])
        eps_t = sb("eps_t", [P, 1])
        one_t = sb("one_t", [P, 1])
        stat = sb("stat", [P, 40])
        norm_stat = sb("norm_stat", [P, 3, 24])
        inv = sb("inv", [P, HALF])
        pos_i = sb("pos_i", [P, MB], I32)
        pos_f = sb("pos_f", [P, MB])
        done_t = sb("done_t", [P, 1])
        arena = sb("arena", [P, ARENA])

        def view(flat, at, *shape):
            v = flat[:, at:at + int(np.prod(shape))]
            if len(shape) == 2:
                return v.rearrange("p (a b) -> p a b", a=shape[0])
            if len(shape) == 3:
                return v.rearrange("p (a b c) -> p a b c", a=shape[0], b=shape[1])
            return v

        def cut(at, *shape):
            assert at + int(np.prod(shape)) <= ARENA, (at, shape)
            return view(arena, at, *shape)

        q_in = [cut(a * 384, MB, QK_A) for a in range(2)]
        k_in = [cut(768 + a * 384, MB, QK_A) for a in range(2)]
        qT = [cut(1536 + a * 512, T) for a in range(2)]
        kT = [cut(2560 + a * 512, T) for a in range(2)]
        probs = [cut(3584 + a * 512, T) for a in range(4)]
        probsT = [cut(5632 + a * 512, T) for a in range(2)]
        W0 = 6656
        gate = cut(W0, MB, D)
        L0 = W0 + MB * D
        memkv = cut(ARENA - 2048, 2, MEMB, 2 * MEM_W)
        q_mem = cut(ARENA - 3072, MB, MEM_W)
        lat = view(yT_t, 0, MB, LAT)
        trig = view(yT_t, 2688, 2, MB, HALF)
        turns_n = view(yT_t, 2816, 2, MB, HALF)
        turned = view(yT_t, 2944, 2, MB, HALF)
        rot_k = [view(yT_t, 3072 + n * 64, MB, HALF) for n in range(4)]
        latT = cut(L0, 5, T)
        a_q = cut(L0 + 2560, MB, A_H * QK_A)
        a_kv = cut(L0 + 2560 + 4608, MB, A_H * 2 * HD)
        rot = [cut(3584 + n * 768, MB * A_H, HALF) for n in range(4)]
        mem_in = cut(L0 + 2560, MEMB, D)
        memT = cut(L0 + 2560 + 4608, KD, N_MEM)
        b_qkv = cut(L0, MB, 3 * MAIN_W)
        b_f, b_F, b_8F, b_t, b_u = (cut(L0 + 9216 + n * 48, MB, B_H) for n in range(5))
        x_in = [view(yT_t, n * 516, 516) for n in range(2)]
        acc = [view(yT_t, 1032 + n * 512, T) for n in range(2)]
        xcT = cut(0, CONVC, T)
        c_xd = cut(0, MB, D)
        c_x = cut(6144, MB, D)
        c_xdt = cut(10240, MB, D)
        c_y = cut(14336, MB, D)
        c_B = cut(18432, C_G, MB, C_N)
        c_sc = cut(19456, C_G, MB, P)
        prev = cut(20480, MB - 1, D)
        c_dt, c_u, dtA, acs, tot, eacs, etot, eend = (cut(23552 + n * 64, MB, C_H) for n in range(8))
        segD = [cut(24064 + n * 512, MB, P) for n in range(2)]
        att = [cut(25088 + n * 512, MB, P) for n in range(2)]
        off = cut(26112, T)
        a_neg = sb("a_neg", [P, C_H])
        s_qkv = cut(L0, MB, 3 * D)
        y_ssd = cut(L0 + 3 * MB * D, MB, D)
        y_sb = gate
        b_gate = cut(L0, 2 * D)
        g_tmp = [cut(L0 + 2048 + n * 512, T) for n in range(4)]

        G_PRE = [0, 8, 16]
        G_MEM, G_SSD, G_Q, G_KV = 24, 32, 40, 43
        bf_row, dtb_row = small[:, 0:B_H], small[:, 12:28]
        alog_row, dskip_row = small[:, 28:44], small[:, 44:60]

        loaded_x = count("loaded_x")
        params = count("params")
        row_in = count("row_in")
        w_in = [count("w_in0"), count("w_in1")]
        consts = count("consts")
        stored = count("stored")
        C = {n: count(n) for n in (
            "product", "evac", "sq", "root", "rinv", "scaled", "turned", "normed",
            "post_sq", "post_sum", "post_root", "post_out", "post_add",
            "staged", "headT", "headT_out", "scores", "neg_max", "exped", "probT",
            "probT_out", "attended", "weighed")}

        chunks = []

        def weight(w, c0, width):
            chunks.append((w.rearrange("(k p) n -> p k n", p=P)[:, :, c0:c0 + width],
                           w.shape[0] // P, width))

        product_before = [0]

        def project(w, c0, width, n, groups, product, src, dst, func=ACT.Copy, loop=False,
                    banks=None, evac=True):
            first = len(chunks)
            for c in range(n):
                weight(w, c0 + c * width, width)
                product_before.append(product_before[-1] + groups)
            return Projection(first=first, n=n, groups=groups, k=w.shape[0] // P, width=width, src=src,
                         product=product, dst=dst, func=func, loop=loop, w=w, c0=c0,
                         banks=banks or (lambda g: bank[g % 4]),
                         done=C["product"].take(n * groups), evac=C["evac"].take(n * groups) if evac else None)

        def slot_of(S, s):
            return wslot[(S.first + s) % 2][:, 0:S.k * S.width].rearrange("p (k n) -> p k n", k=S.k)

        def pairs(eng, S, emit):
            if S.loop:
                assert S.n % 2 == 0 and S.n > 2
                emit(0, 0)
                emit(0, 1)
                with eng.Fori(1, S.n // 2) as k:
                    emit(k, 0)
                    emit(k, 1)
            else:
                for c in range(S.n):
                    emit(0, c)

        def tokens_by(src):
            def product(S, s, g, kk):
                return src[:, kk, g * P:(g + 1) * P], slot_of(S, s)[:, kk, :]
            return product

        def by_tokens(S, s, g, kk):
            return slot_of(S, s)[:, kk, g * P:(g + 1) * P], hT[:, kk, :]

        def to_columns(dst, c0=0):
            def place(S, k, s, g):
                return dst[:, g, ds((2 * k + s) * S.width + c0, S.width)]
            return place

        def project_sp(sp, S):
            def emit(k, s):
                c = S.first + s
                if c >= 2:
                    before = product_before[c - 1] if isinstance(k, int) else \
                        product_before[S.first] + (s - 1) * S.groups + 2 * k * S.groups
                    sp.wait_ge(C["product"].sem, before)
                at = S.c0 + (2 * k + s) * S.width
                src = S.w.rearrange("(k p) n -> p k n", p=P)[:, :, ds(at, S.width)]
                sp.dma_start(slot_of(S, s), src).then_inc(w_in[c % 2].sem, 16)
            pairs(sp, S, emit)

        def project_pe(pe, S):
            def emit(k, s):
                c = S.first + s
                pe.wait_ge(w_in[c % 2].sem, 16 * (c // 2 + 1) + 16 * k)
                for g in range(S.groups):
                    n = s * S.groups + g
                    if S.evac and reached(k, n, 4):
                        pe.wait_ge(*S.evac(n - 3 + 2 * S.groups * k))
                    to = S.banks(n)
                    for kk in range(S.k):
                        lhs, rhs = S.product(S, s, g, kk)
                        mm = nc.tensor.matmul(to[0:lhs.shape[1], 0:rhs.shape[1]], lhs, rhs,
                                              start=kk == 0, stop=kk == S.k - 1)
                    mm.then_inc(S.done.sem, 1)
            pairs(pe, S, emit)

        def project_act(act, S):
            def emit(k, s):
                for g in range(S.groups):
                    n = s * S.groups + g
                    act.wait_ge(*S.done(n + 1 + 2 * S.groups * k))
                    to = S.dst(S, k, s, g)
                    nc.scalar.activation(to, S.banks(n)[:, 0:to.shape[1]], S.func).then_inc(S.evac.sem, 1)
            pairs(act, S, emit)

        norm_stages = []

        def norm_stage(src, dst, blocks, norms, parts, gain):
            nn, np_ = len(norms), len(parts)
            norm_stages.append(1)
            return Norm(src=src, dst=dst, blocks=blocks, norms=norms, parts=parts, gain=gain,
                         stat=norm_stat[:, len(norm_stages) % 3],
                         sq=C["sq"].take(blocks * nn), root=C["root"].take(blocks * nn),
                         rinv=C["rinv"].take(blocks * nn), scaled=C["scaled"].take(blocks * nn),
                         turned=C["turned"].take(blocks * np_), normed=C["normed"].take(blocks * np_))

        def norm_act(act, N, ready=None):
            for m in range(N.blocks):
                if ready:
                    act.wait_ge(*ready(m))
                for a, (c0, width) in enumerate(N.norms):
                    n = m * len(N.norms) + a
                    if n:
                        act.wait_ge(*N.sq(n))
                    nc.scalar.activation(junk[:, 0:width], N.src[:, m, c0:c0 + width], ACT.Square,
                                         accum_out=N.stat[:, n:n + 1]).then_inc(N.sq.sem, 1)
                    act.wait_ge(*N.sq(n + 1))
                    nc.scalar.activation(N.stat[:, 8 + n:9 + n], N.stat[:, n:n + 1], ACT.Sqrt,
                                         bias=eps_t[:, :], scale=1.0 / width).then_inc(N.root.sem, 1)

        def norm_pe(pe, N, ready=None):
            for m in range(N.blocks):
                if ready:
                    pe.wait_ge(*ready(m))
                for p, (a, c0, n, _, b0) in enumerate(N.parts):
                    if N.norms:
                        pe.wait_ge(*N.scaled(m * len(N.norms) + a + 1))
                        rows = hn[:, m % 2, :]
                    else:
                        rows = N.src[:, m, :]
                    for c in range(n):
                        mm = nc.tensor.transpose(bank[b0 + m][:, c * P:(c + 1) * P],
                                                 rows[:, c0 + c * P:c0 + (c + 1) * P], ident[:, :])
                    mm.then_inc(N.turned.sem, 1)

        def norm_dve(dve, N):
            def scale(m):
                for a, (c0, width) in enumerate(N.norms):
                    n = m * len(N.norms) + a
                    dve.wait_ge(*N.root(n + 1))
                    nc.vector.reciprocal(N.stat[:, 16 + n:17 + n], N.stat[:, 8 + n:9 + n]).then_inc(N.rinv.sem, 1)
                if m >= 2:
                    dve.wait_ge(*N.turned((m - 1) * len(N.parts)))
                for a, (c0, width) in enumerate(N.norms):
                    n = m * len(N.norms) + a
                    dve.wait_ge(*N.rinv(n + 1))
                    nc.vector.tensor_scalar(hn[:, m % 2, c0:c0 + width], N.src[:, m, c0:c0 + width],
                                            N.stat[:, 16 + n:17 + n], None, ALU.mult).then_inc(N.scaled.sem, 1)

            def collect(m):
                for p, (a, c0, n, k0, b0) in enumerate(N.parts):
                    dve.wait_ge(*N.turned(m * len(N.parts) + p + 1))
                    to = N.dst[:, k0:k0 + n, m * P:(m + 1) * P]
                    of = bank[b0 + m][:, 0:n * P].rearrange("p (c t) -> p c t", c=n)
                    if N.gain is None:
                        nc.vector.tensor_copy(to, of).then_inc(N.normed.sem, 1)
                    else:
                        g = gains[:, N.gain + k0:N.gain + k0 + n].unsqueeze(2).to_broadcast([P, n, P])
                        nc.vector.tensor_tensor(to, of, g, ALU.mult).then_inc(N.normed.sem, 1)

            for m in range(N.blocks + 1):
                if m < N.blocks:
                    scale(m)
                if m:
                    collect(m - 1)

        whole = [(0, D)]
        whole_parts = [(0, 0, 4, 0, 0), (0, 512, 4, 4, 4)]

        def post_stage():
            return PostNorm(sq=C["post_sq"].take(2 * MB), sum=C["post_sum"].take(MB),
                         root=C["post_root"].take(MB), out=C["post_out"].take(3 * MB),
                         add=C["post_add"].take(MB))

        def post_act(act, O, S, before):
            act.wait_ge(*before)
            for m in range(MB):
                act.wait_ge(*S.done(MB + m + 1))
                for half in range(2):
                    n = 2 * m + half
                    if n:
                        act.wait_ge(*O.sq(n))
                    nc.scalar.activation(junk[:, 0:512], bank[4 * half + m][:, :], ACT.Square,
                                         accum_out=stat[:, 24 + n:25 + n]).then_inc(O.sq.sem, 1)
                act.wait_ge(*O.sum(m + 1))
                nc.scalar.activation(stat[:, 32 + m:33 + m], stat[:, 32 + m:33 + m], ACT.Sqrt,
                                     bias=eps_t[:, :], scale=1.0 / D).then_inc(O.root.sem, 1)

        def post_dve(dve, O, row_ready):
            dve.wait_ge(*row_ready)
            for m in range(MB):
                dve.wait_ge(*O.sq(2 * m + 2))
                nc.vector.tensor_tensor(stat[:, 32 + m:33 + m], stat[:, 24 + 2 * m:25 + 2 * m],
                                        stat[:, 25 + 2 * m:26 + 2 * m], ALU.add).then_inc(O.sum.sem, 1)
                dve.wait_ge(*O.root(m + 1))
                nc.vector.reciprocal(stat[:, 36 + m:37 + m], stat[:, 32 + m:33 + m]).then_inc(O.out.sem, 1)
                dve.wait_ge(*O.out(3 * m + 1))
                for half in range(2):
                    c0 = 512 * half
                    nc.vector.scalar_tensor_tensor(
                        gate[:, m, c0:c0 + 512], bank[4 * half + m][:, :], stat[:, 36 + m:37 + m],
                        row[:, c0:c0 + 512], ALU.mult, ALU.mult).then_inc(O.out.sem, 1)

        def post_pool(pool, O):
            for m in range(MB):
                pool.wait_ge(*O.out(3 * m + 3))
                nc.gpsimd.tensor_tensor(h[:, m, :], h[:, m, :], gate[:, m, :], ALU.add).then_inc(O.add.sem, 1)

        def attend_stage(heads, width, keys, causal_, scale, q, k, v, extra_q, extra_k, y0):
            s = 4 * heads
            return Attend(heads=heads, width=width, keys=keys, causal=causal_, scale=scale, q=q, k=k,
                         v=v, y0=y0, extra_q=extra_q, extra_k=extra_k,
                         staged=C["staged"].take(2 * heads), headT=C["headT"].take(2 * heads),
                         headT_out=C["headT_out"].take(2 * heads), scores=C["scores"].take(s),
                         neg_max=C["neg_max"].take(s),
                         exped=C["exped"].take(s), probT=C["probT"].take(s),
                         probT_out=C["probT_out"].take(s), attended=C["attended"].take(s),
                         weighed=C["weighed"].take(s))

        def n_keys(A, b):
            return b + 1 if A.causal else A.keys

        def attend_pool(pool, A):
            def emit(k, last):
                for a in range(2):
                    if reached(k, a, 2):
                        pool.wait_ge(*A.headT(2 * a - 2 + 4 * k))
                    parts_q = [A.q(k, a)] + A.extra_q(k, a)
                    parts_k = [A.k(k, a)] + A.extra_k(k, a)
                    for parts, buf, n in ((parts_q, q_in[a], MB), (parts_k, k_in[a], A.keys)):
                        for c0, src in parts:
                            ins = nc.gpsimd.tensor_copy(buf[:, 0:n, c0:c0 + src.shape[2]], src)
                        ins.then_inc(A.staged.sem, 1)
            turns(pool, A.heads // 2, emit)

        def attend_pe(pe, A):
            def turn(k, a, which):
                pe.wait_ge(*A.staged(2 * a + which + 1 + 4 * k))
                buf, n = ((q_in, MB), (k_in, A.keys))[which]
                for b in range(n):
                    mm = nc.tensor.transpose(bank[which][0:A.width, b * P:(b + 1) * P],
                                             buf[a % 2][:, b, 0:A.width], ident[:, :])
                mm.then_inc(A.headT.sem, 1)

            def score(k, j):
                a, b = j // 4 % 2, j % 4
                if b == 0:
                    pe.wait_ge(*A.headT_out(2 * (j // 4) + 2 + 4 * k))
                if reached(k, j, 4):
                    pe.wait_ge(*A.exped(j - 3 + 8 * k))
                n = n_keys(A, b) * P
                mm = nc.tensor.matmul(bank[2 + b][:, 0:n], qT[a][0:A.width, b * P:(b + 1) * P],
                                 kT[a][0:A.width, 0:n], start=True, stop=not A.causal)
                if A.causal:
                    mm = nc.tensor.matmul(bank[2 + b][:, n - P:n], ident_b[:, :], later_keys[:, :],
                                          start=False, stop=True)
                mm.then_inc(A.scores.sem, 1)

            def turn_probs(k, j):
                if not reached(k, j, 0):
                    return
                b = j % 4
                pe.wait_ge(*A.exped(j + 1 + 8 * k))
                if reached(k, j, 1):
                    pe.wait_ge(*A.probT_out(j + 8 * k))
                for c in range(n_keys(A, b)):
                    mm = nc.tensor.transpose(bank[6][:, c * P:(c + 1) * P],
                                             probs[b][:, c * P:(c + 1) * P], ident[:, :])
                mm.then_inc(A.probT.sem, 1)

            def values(k, j):
                if not reached(k, j, 0):
                    return
                b = j % 4
                pe.wait_ge(*A.probT_out(j + 1 + 8 * k))
                if reached(k, j, 1):
                    pe.wait_ge(*A.weighed(j + 8 * k))
                n = n_keys(A, b)
                for c in range(n):
                    mm = nc.tensor.matmul(bank[7][:, 0:HD], probsT[j % 2][:, c * P:(c + 1) * P],
                                          A.v(k, j // 4, c), start=c == 0, stop=c == n - 1)
                mm.then_inc(A.attended.sem, 1)

            def emit(k, last):
                if isinstance(k, int) and k == 0:
                    turn(0, 0, 0)
                    turn(0, 0, 1)
                for j in range(8):
                    score(k, j)
                    if j % 4 in (0, 2) and not (last and j >= 4):
                        turn(k, j // 4 + 1, j % 4 // 2)
                    turn_probs(k, j - 2)
                    values(k, j - 3)
                if last:
                    turn_probs(k, 6)
                    turn_probs(k, 7)
                    for j in (5, 6, 7):
                        values(k, j)
            turns(pe, A.heads // 2, emit)

        def attend_act(act, A):
            def collect(k, a, which):
                n = (MB, A.keys)[which] * P
                act.wait_ge(*A.headT(2 * a + which + 1 + 4 * k))
                nc.scalar.activation((qT, kT)[which][a % 2][0:A.width, 0:n], bank[which][0:A.width, 0:n],
                                     ACT.Copy, scale=(A.scale, 1.0)[which]).then_inc(A.headT_out.sem, 1)

            def emit(k, last):
                if isinstance(k, int) and k == 0:
                    collect(0, 0, 0)
                    collect(0, 0, 1)
                for j in range(8):
                    b = j % 4
                    n = n_keys(A, b) * P
                    act.wait_ge(*A.neg_max(j + 1 + 8 * k))
                    if reached(k, j, 4):
                        act.wait_ge(*A.probT(j - 3 + 8 * k))
                    nc.scalar.activation(probs[b][:, 0:n], bank[2 + b][:, 0:n], ACT.Exp,
                                         bias=stat[:, j:j + 1], accum_out=stat[:, 8 + j:9 + j]
                                         ).then_inc(A.exped.sem, 1)
                    if b in (0, 2) and not (last and j >= 4):
                        collect(k, j // 4 + 1, b // 2)
            turns(act, A.heads // 2, emit)

        def attend_dve(dve, A):
            def maximum(k, j):
                b = j % 4
                n = n_keys(A, b) * P
                dve.wait_ge(*A.scores(j + 1 + 8 * k))
                nc.vector.tensor_reduce(stat[:, j:j + 1], bank[2 + b][:, 0:n], AX.X, ALU.max,
                                        negate=True).then_inc(A.neg_max.sem, 1)

            def collect(k, j):
                if not reached(k, j, 0):
                    return
                b = j % 4
                n = n_keys(A, b) * P
                dve.wait_ge(*A.probT(j + 1 + 8 * k))
                nc.vector.reciprocal(stat[:, 16 + j % 8:17 + j % 8], stat[:, 8 + j % 8:9 + j % 8])
                if reached(k, j, 2):
                    dve.wait_ge(*A.attended(j - 1 + 8 * k))
                nc.vector.tensor_copy(probsT[j % 2][:, 0:n], bank[6][:, 0:n]).then_inc(A.probT_out.sem, 1)

            def weigh(k, j):
                if not reached(k, j, 0):
                    return
                dve.wait_ge(*A.attended(j + 1 + 8 * k))
                y = gate[:, j % 4, ds((2 * k + j // 4) * HD + A.y0, HD)]
                nc.vector.scalar_tensor_tensor(y, bank[7][:, 0:HD], stat[:, 16 + j % 8:17 + j % 8], y,
                                               ALU.mult, ALU.mult).then_inc(A.weighed.sem, 1)

            def emit(k, last):
                for j in range(8):
                    maximum(k, j)
                    collect(k, j - 2)
                    weigh(k, j - 3)
                if last:
                    collect(k, 6)
                    weigh(k, 5)
                    collect(k, 7)
                    weigh(k, 6)
                    weigh(k, 7)
            turns(dve, A.heads // 2, emit)

        def head_of(src, stride, c0=0, width=HD, at=0):
            def pick(k, a):
                return at, src[:, :, ds((2 * k + a) * stride + c0, width)]
            return pick

        def rows_of(src, stride, c0=0):
            def pick(k, a, c):
                return src[:, c, ds((2 * k + a) * stride + c0, HD)]
            return pick

        def none(k, a):
            return []

        pre = [norm_stage(h, hT, MB, whole, whole_parts, G_PRE[0])]
        pre_mem = norm_stage(mem_in, memT, MEMB, whole, whole_parts, G_MEM)
        tb = tokens_by(hT)
        pA_lat = project(i["w_in_a"][0], 0, LAT // 2, 2, MB, tb, hT, to_columns(lat))
        pA_qm = project(i["w_in_a"][0], LAT, MEM_W, 1, MB, tb, hT, to_columns(q_mem))
        pA_gate = project(i["w_in_a"][0], LAT + MEM_W, 512, 2, MB, tb, hT, to_columns(gate), ACT.Silu)

        def mem_product(S, s, g, kk):
            m, half = g // 2, g % 2
            return memT[:, kk, m * P:(m + 1) * P], slot_of(S, s)[:, kk, half * MEM_W:(half + 1) * MEM_W]

        def mem_place(layer):
            def place(S, k, s, g):
                return memkv[:, layer, g // 2, (g % 2) * MEM_W:(g % 2 + 1) * MEM_W]
            return place

        p_mem = [project(i["w_mem_kv"][n], 0, 2 * MEM_W, 1, 4, mem_product, memT, mem_place(n)) for n in range(2)]
        latent = norm_stage(lat, latT, MB, [(0, Q_LORA), (Q_LORA, KV_LORA)],
                            [(0, 0, 3, 0, 0), (1, Q_LORA, 2, 3, 4)], G_Q)

        def up_product(k0, parts, width):
            def product(S, s, g, kk):
                m, n = g // parts, g % parts
                return latT[:, k0 + kk, m * P:(m + 1) * P], slot_of(S, s)[:, kk, n * width:(n + 1) * width]
            return product

        def up_place(dst, parts, width):
            def place(S, k, s, g):
                return dst[:, g // parts, (g % parts) * width:(g % parts + 1) * width]
            return place

        pA_q = project(i["w_q_up_a"][0], 0, A_H * QK_A, 1, 3 * MB, up_product(0, 3, 384), latT, up_place(a_q, 3, 384))
        pA_kv = project(i["w_kv_up_a"][0], 0, A_H * 2 * HD, 1, 3 * MB, up_product(3, 3, 512), latT, up_place(a_kv, 3, 512))
        attA = attend_stage(A_H, QK_A, MB, True, QK_A ** -0.5, head_of(a_q, QK_A, 0, QK_A),
                            head_of(a_kv, 2 * HD), rows_of(a_kv, 2 * HD, HD), none, none, 0)

        def mem_attend(layer):
            return attend_stage(MEM_H, HD, MEMB, False, HD ** -0.5, head_of(q_mem, HD),
                                head_of(memkv[:, layer], HD), rows_of(memkv[:, layer], HD, MEM_W),
                                none, none, MAIN_W)

        attAm = mem_attend(0)
        no_norm = [(0, 0, 4, 0, 0), (0, 512, 4, 4, 4)]
        ytA = norm_stage(gate, yT, MB, [], no_norm, None)
        yb = tokens_by(yT)
        all_banks = lambda n: bank[n]
        pA_out = project(i["w_out"][0], 0, 512, 2, MB, yb, yT, None, banks=all_banks, evac=False)
        post = [post_stage()]

        pre.append(norm_stage(h, hT, MB, whole, whole_parts, G_PRE[1]))
        wb = i["w_in_b"][0]
        pB_qkv = project(wb, 0, 384, 6, MB, tb, hT, to_columns(b_qkv), loop=True)
        pB_f = project(wb, 3 * MAIN_W, B_H, 1, MB, tb, hT, to_columns(b_f))
        pB_qm = project(wb, 3 * MAIN_W + B_H, MEM_W, 1, MB, tb, hT, to_columns(q_mem))
        pB_gate = project(wb, 3 * MAIN_W + B_H + MEM_W, 512, 2, MB, tb, hT, to_columns(gate), ACT.Silu)
        attB = attend_stage(
            B_H, HD + 2, MB, True, HD ** -0.5, head_of(b_qkv, HD), head_of(b_qkv, HD, MAIN_W),
            rows_of(b_qkv, HD, 2 * MAIN_W),
            lambda k, a: [(HD + 1, b_8F[:, :, ds(2 * k + a, 1)])],
            lambda k, a: [(HD, b_F[:, :, ds(2 * k + a, 1)])], 0)
        attBm = mem_attend(1)
        ytB = norm_stage(gate, yT, MB, [], no_norm, None)
        pB_out = project(i["w_out"][1], 0, 512, 2, MB, yb, yT, None, banks=all_banks, evac=False)
        post.append(post_stage())

        pre.append(norm_stage(h, hT, MB, whole, whole_parts, G_PRE[2]))
        wc = i["w_in_2"][0]
        Z0, X0, DT0, Q0 = 0, INNER, INNER + CONV, INNER + CONV + C_H
        ZS0, G0 = Q0 + 3 * D, Q0 + 4 * D
        pC_x = project(wc, X0, 256, 6, 2, by_tokens, hT, None, loop=True)
        pC_dt = project(wc, DT0, C_H, 1, MB, tb, hT, to_columns(c_dt))
        pC_z = project(wc, Z0, 512, 2, MB, tb, hT, to_columns(c_x), ACT.Silu)
        ssd_norm = norm_stage(c_y, yT, MB, [(0, 512), (512, 512)], [(0, 0, 4, 0, 0), (1, 512, 4, 4, 4)], G_SSD)
        pC_ssd = project(i["w_ssd_proj_2"][0], 0, 512, 2, MB, yb, yT, to_columns(y_ssd))
        pC_qkv = project(wc, Q0, 512, 6, MB, tb, hT, to_columns(s_qkv), loop=True)
        pC_zs = project(wc, ZS0, 512, 2, MB, tb, hT, to_columns(gate), ACT.Silu)
        ytC = norm_stage(gate, yT, MB, [], no_norm, None)
        pC_sb = project(i["w_sb_proj_2"][0], 0, 512, 2, MB, yb, yT, to_columns(y_sb))

        def gate_place(S, k, s, g):
            return g_tmp[g]

        pC_gate = project(wc, G0, 512, 4, MB, tb, hT, gate_place)
        ytM = norm_stage(y_ssd, yT, MB, [], no_norm, None)
        pC_out = project(i["w_out_2"][0], 0, 512, 2, MB, yb, yT, None, banks=all_banks, evac=False)
        post.append(post_stage())

        misc = {n: count(n) for n in (
            "pool_self", "dve_self", "act_self", "rope_ang", "rope_trig", "rope_done", "kr_done",
            "gates_in", "gates_exp", "gates_log", "sums", "sums_out",
            "conv_in", "conv_acc", "conv_out", "xT_turned", "xT_out", "ssd_dt", "ssd_sc", "ssd_sc_out",
            "ssd_seg", "ssd_seg_in", "ssd_exp", "ssd_att", "ssd_diag", "ssd_y", "ssd_state",
            "ssd_prev", "ssd_off", "ssd_off_out", "ssd_ready", "ssd_gated",
            "z", "z_min", "soft", "sp", "remain", "w_exp", "s_out", "s_y",
            "g_biased", "g_sig", "g_merge", "g_done")}
        started = {}
        sem = {n: c.sem for n, c in misc.items()}

        def chain(eng, name):
            def link(ins):
                misc[name].total += 1
                ins.then_inc(sem[name], 1)
                eng.wait_ge(sem[name], misc[name].total)
            return link

        XT = 2 * MB + C_G

        def conv_taps(c):
            return [conv_k[:, t, ds(c, 1)] for t in range(TAPS)]

        def ssd_act(act):
            S = pC_x

            def silu(k, n):
                act.wait_ge(sem["conv_acc"], n + 1 + 4 * k)
                nc.scalar.activation(xcT[:, ds(4 * k + n, 1), :].rearrange("p o t -> p (o t)"),
                                     acc[n % 2], ACT.Silu).then_inc(sem["conv_out"], 1)

            def emit(k, s):
                for g in range(S.groups):
                    n = s * S.groups + g
                    act.wait_ge(*S.done(n + 1 + 4 * k))
                    if reached(k, n, 2):
                        act.wait_ge(sem["conv_acc"], n - 1 + 4 * k)
                    nc.scalar.activation(x_in[n % 2][:, TAPS - 1:TAPS - 1 + T], S.banks(n)[:, :],
                                         ACT.Copy).then_inc(S.evac.sem, 1)
                    if reached(k, n, 1):
                        silu(k, n - 1)
            act.wait_ge(*pre[2].normed(1))
            pairs(act, S, emit)
            silu(S.n // 2 - 1, 3)
            project_act(act, pC_dt)
            for f in range(XT):
                act.wait_ge(sem["xT_turned"], f + 1)
                to = c_x[:, f // 2, f % 2 * 512:f % 2 * 512 + 512] if f < 2 * MB else \
                    c_B[:, f - 2 * MB].rearrange("p m n -> p (m n)")
                nc.scalar.activation(to, bank[4 + f % 4][:, :], ACT.Copy).then_inc(sem["xT_out"], 1)
            act.wait_ge(sem["ssd_dt"], 1)
            nc.scalar.activation(acs, acs, ACT.Exp).then_inc(sem["ssd_ready"], 1)
            act.wait_ge(sem["ssd_ready"], 1)
            nc.scalar.activation(acs, acs, ACT.Ln, bias=one_t[:, :]).then_inc(sem["ssd_ready"], 1)
            nc.scalar.activation(a_neg[:, :], alog_row, ACT.Exp).then_inc(sem["ssd_ready"], 1)
            act.wait_ge(sem["sums"], 2)
            nc.scalar.activation(cut(23552 + 5 * 64, 3 * MB * C_H), bank[2][:, 0:3 * MB * C_H],
                                 ACT.Exp).then_inc(sem["ssd_ready"], 1)
            for g in range(C_G):
                def emit_heads(k, last, g=g):
                    for a in range(2):
                        n = GH * g + a
                        act.wait_ge(sem["ssd_seg"], n + 1 + 2 * k)
                        if g or reached(k, a, 2):
                            act.wait_ge(sem["ssd_diag"], n - 1 + 2 * k)
                        nc.scalar.activation(att[a].rearrange("p m l -> p (m l)"), bank[4 + a][:, :],
                                             ACT.Exp).then_inc(sem["ssd_exp"], 1)
                turns(act, GH // 2, emit_heads)
            act.wait_ge(sem["ssd_y"], C_H)
            project_act(act, pC_z)
            norm_act(act, ssd_norm, lambda m: (sem["ssd_gated"], m + 1))
            project_act(act, pC_ssd)

        def ssd_pe(pe):
            project_pe(pe, pC_x)
            pe.wait_ge(*pC_x.evac(12))
            project_pe(pe, pC_dt)
            pe.wait_ge(sem["conv_out"], CONVC)
            for f in range(XT):
                if f >= 4:
                    pe.wait_ge(sem["xT_out"], f - 3)
                for c in range(4):
                    src = xcT[:, 4 * (f % 2) + c, f // 2 * P:(f // 2 + 1) * P] if f < 2 * MB else \
                        xcT[:, XC + f - 2 * MB, c * P:(c + 1) * P]
                    mm = nc.tensor.transpose(bank[4 + f % 4][:, c * P:(c + 1) * P], src, ident[:, :])
                mm.then_inc(sem["xT_turned"], 1)
            pe.wait_ge(*pC_dt.evac(MB))
            for g in range(C_G):
                for m in range(MB):
                    mm = nc.tensor.matmul(bank[g][:, m * P:(m + 1) * P], xcT[:, XC + g, m * P:(m + 1) * P],
                                          xcT[:, XC + C_G + g, m * P:(m + 1) * P], start=True, stop=True)
                mm.then_inc(sem["ssd_sc"], 1)
            pe.wait_ge(sem["ssd_dt"], 2)
            for n, w in enumerate((tri_le, ones, tri_gt)):
                mm = nc.tensor.matmul(bank[2][:, n * 64:(n + 1) * 64], w[:, :],
                                      dtA.rearrange("p m h -> p (m h)"), start=True, stop=True)
            mm.then_inc(sem["sums"], 1)
            pe.wait_ge(sem["xT_out"], XT)
            for g in range(C_G):
                def seg(k, a, g=g):
                    n = GH * g + a
                    pe.wait_ge(sem["ssd_seg_in"], n + 1 + 2 * k)
                    if g or reached(k, a, 2):
                        pe.wait_ge(sem["ssd_exp"], n - 1 + 2 * k)
                    nc.tensor.matmul(bank[4 + a][:, :], tri_gt[:, :], segD[a].rearrange("p m l -> p (m l)"),
                                     start=True, stop=True).then_inc(sem["ssd_seg"], 1)

                def diag(k, a, g=g):
                    n = GH * g + a
                    b = a % 2
                    pe.wait_ge(sem["ssd_att"], n + 1 + 2 * k)
                    if g or reached(k, a, 2):
                        pe.wait_ge(sem["ssd_y"], n - 1 + 2 * k)
                    for m in range(MB):
                        mm = nc.tensor.matmul(bank[6 + b][:, m * HD:(m + 1) * HD], att[b][:, m, :],
                                              c_xdt[:, m, ds((n + 2 * k) * HD, HD)], start=True, stop=True)
                    mm.then_inc(sem["ssd_diag"], 1)

                def emit(k, last):
                    seg(k, 0)
                    if reached(k, 0, 1):
                        diag(k, -1)
                    seg(k, 1)
                    diag(k, 0)
                    if last:
                        diag(k, 1)
                turns(pe, GH // 2, emit)
            pe.wait_ge(sem["ssd_sc_out"], C_G)
            pe.wait_ge(sem["ssd_ready"], 5)
            for n in range(2 * (MB - 1)):
                m, g = n // 2, n % 2
                if n >= 4:
                    pe.wait_ge(sem["ssd_prev"], n - 3)
                nc.tensor.matmul(bank[n % 4][:, :], c_B[:, g, m, :], c_xd[:, m, g * 512:(g + 1) * 512],
                                 start=True, stop=True).then_inc(sem["ssd_state"], 1)
            for n in range(2 * (MB - 1)):
                m, g = n // 2 + 1, n % 2
                pe.wait_ge(sem["ssd_prev"], max(n + 1, 2 * (MB - 1)) if n < 4 else 2 * (MB - 1))
                if n >= 4:
                    pe.wait_ge(sem["ssd_off_out"], 2 * (n - 3))
                nc.tensor.matmul(bank[n % 4][:, :], xcT[:, XC + C_G + g, m * P:(m + 1) * P],
                                 prev[:, m - 1, g * 512:(g + 1) * 512],
                                 start=True, stop=True).then_inc(sem["ssd_off"], 1)
            pe.wait_ge(sem["ssd_off_out"], 4 * (MB - 1))
            project_pe(pe, pC_z)
            pe.wait_ge(*pC_z.evac(2 * MB))
            norm_pe(pe, ssd_norm)
            pe.wait_ge(*ssd_norm.normed(2 * MB))
            project_pe(pe, pC_ssd)
            pe.wait_ge(*pC_ssd.evac(2 * MB))

        def ssd_pool(pool, link):
            pool.wait_ge(sem["xT_out"], 2 * MB)
            skip = dskip_row.unsqueeze(2).to_broadcast([P, C_H, HD])
            for m in range(MB):
                link(nc.gpsimd.tensor_tensor(c_y[:, m, :].rearrange("p (h d) -> p h d", d=HD),
                                             c_x[:, m, :].rearrange("p (h d) -> p h d", d=HD), skip, ALU.mult))
            started["y"] = misc["pool_self"].total
            pool.wait_ge(sem["ssd_dt"], 2)
            for g in range(C_G):
                def emit(k, last, g=g):
                    for a in range(2):
                        n = GH * g + a
                        if g or reached(k, a, 2):
                            pool.wait_ge(sem["ssd_seg"], n - 1 + 2 * k)
                        nc.gpsimd.tensor_tensor(
                            segD[a], tri_le[:, :].unsqueeze(1).to_broadcast([P, MB, P]),
                            dtA[:, :, ds(n + 2 * k, 1)].to_broadcast([P, MB, P]),
                            ALU.mult).then_inc(sem["ssd_seg_in"], 1)
                turns(pool, GH // 2, emit)

        def ssd_dve(dve, link):
            S = pC_x
            for b in range(2):
                link(nc.vector.memset(x_in[b][:, 0:TAPS - 1], 0.0))

            def emit(k, s):
                for g in range(S.groups):
                    n = s * S.groups + g
                    src, to, taps = x_in[n % 2], acc[n % 2], conv_taps(4 * k + n)
                    dve.wait_ge(*S.evac(n + 1 + 4 * k))
                    if reached(k, n, 2):
                        dve.wait_ge(sem["conv_out"], n - 1 + 4 * k)
                    nc.vector.tensor_scalar(to, src[:, 0:T], taps[0], conv_b[:, ds(4 * k + n, 1)],
                                            ALU.mult, ALU.add).then_inc(sem["conv_in"], 1)
                    for t in range(1, TAPS):
                        dve.wait_ge(sem["conv_in"], 3 * n + t + 12 * k)
                        ins = nc.vector.scalar_tensor_tensor(to, src[:, t:t + T], taps[t], to, ALU.mult, ALU.add)
                        ins.then_inc(sem["conv_in" if t < TAPS - 1 else "conv_acc"], 1)
            pairs(dve, S, emit)
            dve.wait_ge(*pC_dt.evac(MB))
            link(nc.vector.tensor_tensor(c_u, c_dt, dtb_row.unsqueeze(1).to_broadcast([P, MB, C_H]), ALU.add))
            nc.vector.scalar_tensor_tensor(acs, c_u, -1.0, c_u, ALU.mult, ALU.min).then_inc(sem["ssd_dt"], 1)
            dve.wait_ge(sem["ssd_ready"], 3)
            link(nc.vector.scalar_tensor_tensor(c_dt, c_u, 0.0, acs, ALU.max, ALU.add))
            nc.vector.scalar_tensor_tensor(dtA, c_dt, -1.0, a_neg[:, :].unsqueeze(1).to_broadcast([P, MB, C_H]),
                                           ALU.mult, ALU.mult).then_inc(sem["ssd_dt"], 1)
            for g in range(C_G):
                dve.wait_ge(sem["ssd_sc"], g + 1)
                nc.vector.tensor_tensor(c_sc[:, g],
                                        bank[g][:, :].rearrange("p (m l) -> p m l", m=MB),
                                        tri_le[:, :].unsqueeze(1).to_broadcast([P, MB, P]),
                                        ALU.mult).then_inc(sem["ssd_sc_out"], 1)
            dve.wait_ge(sem["xT_out"], 2 * MB)
            by_head = "p m (h d) -> p (m h) d"
            link(nc.vector.tensor_tensor(c_xdt.rearrange(by_head, d=HD), c_x.rearrange(by_head, d=HD),
                                         c_dt.rearrange("p m h -> p (m h)").unsqueeze(2).to_broadcast([P, MB * C_H, HD]),
                                         ALU.mult))
            dve.wait_ge(sem["ssd_ready"], 4)
            nb = MB - 1
            nc.vector.tensor_tensor(c_xd[:, 0:nb].rearrange(by_head, d=HD), c_xdt[:, 0:nb].rearrange(by_head, d=HD),
                                    eend[:, 0:nb].rearrange("p m h -> p (m h)").unsqueeze(2).to_broadcast([P, nb * C_H, HD]),
                                    ALU.mult).then_inc(sem["ssd_ready"], 1)
            dve.wait_ge(sem["pool_self"], started["y"])
            for g in range(C_G):
                def weigh(k, a, g=g):
                    n = GH * g + a
                    dve.wait_ge(sem["ssd_exp"], n + 1 + 2 * k)
                    nc.vector.tensor_tensor(att[a], att[a], c_sc[:, g],
                                            ALU.mult).then_inc(sem["ssd_att"], 1)

                def add(k, a, g=g):
                    n = GH * g + a
                    dve.wait_ge(sem["ssd_diag"], n + 1 + 2 * k)
                    y = c_y[:, :, ds((n + 2 * k) * HD, HD)]
                    nc.vector.tensor_tensor(y, y, bank[6 + a % 2][:, 0:MB * HD].rearrange("p (m d) -> p m d", m=MB),
                                            ALU.add).then_inc(sem["ssd_y"], 1)

                def emit_heads(k, last):
                    weigh(k, 0)
                    if reached(k, 0, 1):
                        add(k, -1)
                    weigh(k, 1)
                    add(k, 0)
                    if last:
                        add(k, 1)
                turns(dve, GH // 2, emit_heads)
            half = "p (h d) -> p h d"

            def per_head(t, m, g):
                return t[:, m, g * GH:(g + 1) * GH].unsqueeze(2).to_broadcast([P, GH, HD])
            for n in range(2 * (MB - 1)):
                m, g = n // 2, n % 2
                c0 = slice(g * 512, (g + 1) * 512)
                if m:
                    link(nc.vector.tensor_tensor(prev[:, m, c0].rearrange(half, d=HD),
                                                 prev[:, m - 1, c0].rearrange(half, d=HD), per_head(etot, m, g), ALU.mult))
                dve.wait_ge(sem["ssd_state"], n + 1)
                if m:
                    nc.vector.tensor_tensor(prev[:, m, c0], prev[:, m, c0], bank[n % 4][:, :],
                                            ALU.add).then_inc(sem["ssd_prev"], 1)
                    dve.wait_ge(sem["ssd_prev"], n + 1)
                else:
                    nc.vector.tensor_copy(prev[:, m, c0], bank[n % 4][:, :]).then_inc(sem["ssd_prev"], 1)
                    dve.wait_ge(sem["ssd_prev"], n + 1)
            for n in range(2 * (MB - 1)):
                m, g = n // 2 + 1, n % 2
                dve.wait_ge(sem["ssd_off"], n + 1)
                nc.vector.tensor_tensor(off.rearrange(half, d=HD), bank[n % 4][:, :].rearrange(half, d=HD),
                                        per_head(eacs, m, g), ALU.mult).then_inc(sem["ssd_off_out"], 1)
                dve.wait_ge(sem["ssd_off_out"], 2 * n + 1)
                y = c_y[:, m, g * 512:(g + 1) * 512]
                nc.vector.tensor_tensor(y, y, off, ALU.add).then_inc(sem["ssd_off_out"], 1)
                dve.wait_ge(sem["ssd_off_out"], 2 * n + 2)
            for m in range(MB):
                dve.wait_ge(*pC_z.evac(MB + m + 1))
                nc.vector.tensor_tensor(c_y[:, m, :], c_y[:, m, :], c_x[:, m, :], ALU.mult).then_inc(sem["ssd_gated"], 1)
            dve.wait_ge(sem["ssd_gated"], MB)
            norm_dve(dve, ssd_norm)

        SB = 2 * C_H
        st = Staging(staged=C["staged"].take(SB), headT=C["headT"].take(SB), headT_out=C["headT_out"].take(SB))
        sp_ = [[view(yT_t, 2048 * a + 512 * u, P * (u + 1)) for u in range(4)] for a in range(2)]
        w_at = [0, 128, 384, 768]
        w_ = [[cut(3584 + 1280 * a + w_at[u], P * (u + 1)) for u in range(4)] for a in range(2)]

        def stick_pool(pool):
            def stage(k, a):
                if reached(k, a, 2):
                    pool.wait_ge(*st.headT(2 * a - 2 + 4 * k))
                for buf, c0 in ((q_in, 0), (k_in, D)):
                    nc.gpsimd.tensor_copy(buf[a % 2][:, :, 0:HD],
                                          s_qkv[:, :, ds((2 * k + a) * HD + c0, HD)]).then_inc(st.staged.sem, 1)

            def emit(k, last):
                if isinstance(k, int) and k == 0:
                    stage(0, 0)
                for a in range(1, 2 if last else 3):
                    stage(k, a)
            pool.wait_ge(*pC_qkv.evac(6 * MB))
            turns(pool, C_H // 2, emit)

        def stick_pe(pe):
            def turn(k, a, which):
                pe.wait_ge(*st.staged(2 * a + which + 1 + 4 * k))
                for b in range(MB):
                    mm = nc.tensor.transpose(bank[which][0:QK_A, b * P:(b + 1) * P],
                                             (q_in, k_in)[which][a % 2][:, b, :], ident[:, :])
                mm.then_inc(st.headT.sem, 1)

            def score(k, j):
                a, u = j // 4, j % 4
                if u == 0:
                    pe.wait_ge(*st.headT_out(2 * a + 2 + 4 * k))
                if reached(k, j, 4):
                    pe.wait_ge(sem["w_exp"], j - 3 + 8 * k)
                kb = MB - 1 - u
                nc.tensor.matmul(bank[2 + u][:, 0:P * (u + 1)], kT[a][0:HD, kb * P:(kb + 1) * P],
                                 qT[a][0:HD, kb * P:T], start=True, stop=False, skip_group_check=True)
                nc.tensor.matmul(bank[2 + u][:, 0:P], ident_b[:, :], not_before[:, :], start=False,
                                 stop=False, skip_group_check=True).then_inc(sem["z"], 1)

            def remain(k, j):
                if not reached(k, j, 0):
                    return
                a, u = j // 4 % 2, j % 4
                pe.wait_ge(sem["sp"], j + 1 + 8 * k)
                for v in range(u, -1, -1):
                    w = P * (v + 1)
                    c0 = P * (u - v)
                    mm = nc.tensor.matmul(bank[2 + u][:, c0:c0 + w], (neg_ge if v == u else neg_ones)[:, :],
                                          sp_[a][v], start=False, stop=v == 0, skip_group_check=True)
                mm.then_inc(sem["remain"], 1)

            def values(k, a):
                if not reached(k, a, 0):
                    return
                pe.wait_ge(sem["w_exp"], 4 * a + 4 + 8 * k)
                if reached(k, a, 2):
                    pe.wait_ge(sem["s_y"], a - 1 + 2 * k)
                for b in range(MB):
                    for kb in range(b + 1):
                        u = MB - 1 - kb
                        mm = nc.tensor.matmul(
                            bank[6 + a % 2][:, b * HD:(b + 1) * HD], w_[a % 2][u][:, (b - kb) * P:(b - kb + 1) * P],
                            s_qkv[:, kb, ds((2 * k + a) * HD + 2 * D, HD)], start=kb == 0, stop=kb == b)
                mm.then_inc(sem["s_out"], 1)

            def emit(k, last):
                if isinstance(k, int) and k == 0:
                    turn(0, 0, 0)
                    turn(0, 0, 1)
                for j in range(8):
                    score(k, j)
                    if j % 4 in (2, 3) and not (last and j >= 4):
                        turn(k, j // 4 + 1, j % 4 - 2)
                    remain(k, j - 2)
                    if j % 4 == 3:
                        values(k, j // 4 - 1)
                if last:
                    remain(k, 6)
                    remain(k, 7)
                    values(k, 1)
            turns(pe, C_H // 2, emit)

        def stick_act(act):
            def weight_(k, j):
                if reached(k, j, 0):
                    u = j % 4
                    act.wait_ge(sem["remain"], j + 1 + 8 * k)
                    nc.scalar.activation(w_[j // 4 % 2][u], bank[2 + u][:, 0:P * (u + 1)],
                                         ACT.Exp).then_inc(sem["w_exp"], 1)

            nc.scalar.preload_act_table_set("natural_log_exp_and_others")

            def emit(k, last):
                for j in range(8):
                    t = sp_[j // 4][j % 4]
                    act.wait_ge(sem["z_min"], j + 1 + 8 * k)
                    nc.scalar.activation(t, t, ACT.Exp).then_inc(sem["soft"], 1)
                    act.wait_ge(sem["soft"], 2 * j + 1 + 16 * k)
                    nc.scalar.activation(t, t, ACT.Ln, bias=one_t[:, :]).then_inc(sem["soft"], 1)
                    weight_(k, j - 2)
                if last:
                    weight_(k, 6)
                    weight_(k, 7)
            turns(act, C_H // 2, emit)

        def stick_dve(dve):
            def collect(k, a, which):
                dve.wait_ge(*st.headT(2 * a + which + 1 + 4 * k))
                nc.vector.tensor_scalar((qT, kT)[which][a % 2][0:HD, :], bank[which][0:HD, :],
                                        (HD ** -0.5, 1.0)[which], None, ALU.mult).then_inc(st.headT_out.sem, 1)

            def softplus(k, j):
                if reached(k, j, 0):
                    t = sp_[j // 4 % 2][j % 4]
                    dve.wait_ge(sem["soft"], 2 * j + 2 + 16 * k)
                    nc.vector.tensor_tensor(t, bank[2 + j % 4][:, 0:P * (j % 4 + 1)], t,
                                            ALU.max).then_inc(sem["sp"], 1)

            def weigh(k, a):
                if reached(k, a, 0):
                    dve.wait_ge(sem["s_out"], a + 1 + 2 * k)
                    y = gate[:, :, ds((2 * k + a) * HD, HD)]
                    nc.vector.tensor_tensor(y, bank[6 + a % 2][:, 0:MB * HD].rearrange("p (m d) -> p m d", m=MB), y,
                                            ALU.mult).then_inc(sem["s_y"], 1)

            def emit(k, last):
                if isinstance(k, int) and k == 0:
                    collect(0, 0, 0)
                    collect(0, 0, 1)
                for j in range(8):
                    u = j % 4
                    dve.wait_ge(sem["z"], j + 1 + 8 * k)
                    nc.vector.tensor_scalar(sp_[j // 4][u], bank[2 + u][:, 0:P * (u + 1)], SOFT_MAX, None,
                                            ALU.min).then_inc(sem["z_min"], 1)
                    softplus(k, j - 1)
                    if u in (2, 3) and not (last and j >= 4):
                        collect(k, j // 4 + 1, u - 2)
                    if u == 3:
                        weigh(k, j // 4 - 1)
                if last:
                    softplus(k, 7)
                    weigh(k, 1)
            turns(dve, C_H // 2, emit)

        def gates_act(act):
            S = pC_gate

            def sigmoid(n):
                t = g_tmp[n % MB]
                act.wait_ge(sem["g_biased"], n + 1)
                nc.scalar.activation(t, t, ACT.Sigmoid).then_inc(sem["g_sig"], 1)
            for n in range(4 * MB):
                act.wait_ge(*S.done(n + 1))
                if n >= MB:
                    act.wait_ge(sem["g_done"], n - MB + 1)
                nc.scalar.activation(g_tmp[n % MB], S.banks(n)[:, :], ACT.Copy).then_inc(S.evac.sem, 1)
                if n:
                    sigmoid(n - 1)
            sigmoid(4 * MB - 1)

        def gates_dve(dve):
            S = pC_gate
            dve.wait_ge(row_in.sem, 64)

            def merge(n):
                c, m = n // MB, n % MB
                t = g_tmp[m]
                y = y_ssd[:, m, c % 2 * 512:c % 2 * 512 + 512]
                dve.wait_ge(sem["g_sig"], n + 1)
                if c < 2:
                    nc.vector.tensor_tensor(y, y, t, ALU.mult).then_inc(sem["g_done"], 1)
                else:
                    nc.vector.tensor_tensor(t, y_sb[:, m, c % 2 * 512:c % 2 * 512 + 512], t,
                                            ALU.mult).then_inc(sem["g_merge"], 1)
                    dve.wait_ge(sem["g_merge"], n - 2 * MB + 1)
                    nc.vector.tensor_tensor(y, y, t, ALU.add).then_inc(sem["g_done"], 1)
            dve.wait_ge(*pC_sb.evac(2 * MB))
            for n in range(4 * MB):
                c, m = n // MB, n % MB
                dve.wait_ge(*S.evac(n + 1))
                nc.vector.tensor_tensor(g_tmp[m], g_tmp[m], b_gate[:, c * 512:(c + 1) * 512],
                                        ALU.add).then_inc(sem["g_biased"], 1)
                if n:
                    merge(n - 1)
            merge(4 * MB - 1)
            dve.wait_ge(sem["g_done"], 4 * MB)

        block = ctx.enter_context(nc.Block())

        @block.sync
        def _(sp):
            for m in range(MB):
                sp.dma_start(h[:, m, :], i["x"][0, m * P:(m + 1) * P, :]).then_inc(loaded_x.sem, 16)
            sp.dma_start(mem_in, i["mem"][0].rearrange("(m p) d -> p m d", p=P)).then_inc(loaded_x.sem, 16)
            for S in (pA_lat, pA_qm, pA_gate, *p_mem, pA_q, pA_kv, pA_out, pB_qkv, pB_f, pB_qm, pB_gate,
                      pB_out, pC_x, pC_dt, pC_z, pC_ssd, pC_qkv, pC_zs, pC_sb, pC_gate, pC_out):
                project_sp(sp, S)
            for m in range(MB):
                sp.wait_ge(*post[2].add(m + 1))
                sp.dma_start(out[0, m * P:(m + 1) * P, :], h[:, m, :]).then_inc(stored.sem, 16)
            sp.wait_ge(stored.sem, 16 * MB)

        @block.gpsimd
        def _(pool):
            link = chain(pool, "pool_self")
            for t, v in ((ident, 0.0), (tri_le, 1.0), (tri_gt, 1.0), (neg_ge, -1.0), (ident_b, 0.0),
                         (later_keys, 0.0), (not_before, 0.0)):
                link(nc.gpsimd.memset(t[:, :], v))
            nc.gpsimd.memset(ones[:, :], 1.0)
            nc.gpsimd.memset(neg_ones[:, :], -1.0)
            nc.gpsimd.memset(eps_t[:, :], EPS)
            nc.gpsimd.memset(one_t[:, :], 1.0)
            for j in range(HALF):
                nc.gpsimd.memset(inv[:, j:j + 1], float(np.float32(ROPE_THETA ** (-j / HALF))))
            for t, cmp, fill, base, step, chan in (
                    (ident, ALU.not_equal, 1.0, 0, -1, 1), (tri_le, ALU.is_ge, 0.0, 0, 1, -1),
                    (tri_gt, ALU.is_ge, 0.0, -1, -1, 1), (neg_ge, ALU.is_ge, 0.0, 0, -1, 1),
                    (ident_b, ALU.not_equal, 1.0, 0, -1, 1),
                    (later_keys, ALU.is_ge, MASKED, 0, -1, 1), (not_before, ALU.is_ge, MASKED, -1, 1, -1)):
                ins = nc.gpsimd.affine_select(out=t[:, :], in_=t[:, :], pattern=[[step, P]], compare_op=cmp,
                                              fill=fill, base=base, channel_multiplier=chan)
            ins.then_inc(consts.sem, 1)

            def rotate(x1, x2, c, s, t):
                for n, (x, f) in enumerate(((x1, c), (x2, s), (x2, c), (x1, s))):
                    link(nc.gpsimd.tensor_tensor(t[n], x, f, ALU.mult))
                link(nc.gpsimd.tensor_tensor(x1, t[0], t[1], ALU.subtract))
                link(nc.gpsimd.tensor_tensor(x2, t[2], t[3], ALU.add))

            pool.wait_ge(sem["rope_trig"], 1)
            pool.wait_ge(*pA_lat.evac(2 * MB))
            kr = Q_LORA + KV_LORA
            rotate(lat[:, :, kr:kr + HALF], lat[:, :, kr + HALF:kr + ROPE], trig[:, 1], trig[:, 0],
                   rot_k)
            for a in range(2):
                link(nc.gpsimd.tensor_copy(k_in[a][:, :, NOPE:QK_A], lat[:, :, kr:kr + ROPE]))
            pool.wait_ge(*pA_q.evac(3 * MB))
            for m in range(MB):
                v = a_q[:, m, :].rearrange("p (h c) -> p h c", c=QK_A)
                b = [trig[:, n, m, :].unsqueeze(1).to_broadcast([P, A_H, HALF]) for n in (1, 0)]
                rotate(v[:, :, NOPE:NOPE + HALF], v[:, :, NOPE + HALF:QK_A], b[0], b[1],
                       [t[:, m * A_H:(m + 1) * A_H, :] for t in rot])
            pool.wait_ge(*pA_kv.evac(3 * MB))
            attend_pool(pool, attA)
            pool.wait_ge(*p_mem[1].evac(4))
            pool.wait_ge(*pA_qm.evac(MB))
            pool.wait_ge(*attA.headT(2 * A_H))
            attend_pool(pool, attAm)
            pool.dma_start(row[:, :], i["norm_post"][0:1, :].partition_broadcast(P)).then_inc(row_in.sem, 16)
            post_pool(pool, post[0])

            pool.wait_ge(*attAm.headT(2 * MEM_H))
            for a in range(2):
                nc.gpsimd.memset(q_in[a][:, :, HD:HD + 1], HD ** 0.5)
                link(nc.gpsimd.memset(k_in[a][:, :, HD + 1:HD + 2], 1.0))
            pool.wait_ge(*pB_qkv.evac(6 * MB))
            pool.wait_ge(sem["sums_out"], 2)
            attend_pool(pool, attB)
            pool.wait_ge(*pB_qm.evac(MB))
            pool.wait_ge(*attB.headT(2 * B_H))
            attend_pool(pool, attBm)
            pool.wait_ge(*post[0].out(3 * MB))
            pool.dma_start(row[:, :], i["norm_post"][1:2, :].partition_broadcast(P)).then_inc(row_in.sem, 16)
            post_pool(pool, post[1])

            ssd_pool(pool, link)
            stick_pool(pool)
            pool.wait_ge(sem["s_out"], C_H)
            pool.dma_start(b_gate, i["b_gate_2"].partition_broadcast(P)).then_inc(row_in.sem, 16)
            pool.dma_start(row[:, :], i["norm_post_2"].partition_broadcast(P)).then_inc(row_in.sem, 16)
            post_pool(pool, post[2])

        @block.scalar
        def _(act):
            def feature_major(name, n, at):
                act.dma_start(gains[:, at:at + n], name.rearrange("(c p) -> p c", p=P)).then_inc(params.sem, 16)

            with nc.allow_non_contiguous_dma("a few parameters, once"):
                act.dma_start(pos_i[:, :], i["positions"].rearrange("o (m p) -> p (o m)", p=P)).then_inc(params.sem, 16)
                feature_major(i["norm_pre"][0], KD, G_PRE[0])
                feature_major(i["mem_norm"], KD, G_MEM)
                feature_major(i["q_norm_a"][0], 3, G_Q)
                feature_major(i["kv_norm_a"][0], 2, G_KV)
                feature_major(i["norm_pre"][1], KD, G_PRE[1])
                feature_major(i["norm_pre_2"][0], KD, G_PRE[2])
                feature_major(i["ssd_norm_2"][0], KD, G_SSD)
                for t in range(TAPS):
                    act.dma_start(conv_k[:, t, :], i["conv_w_2"][0, t].rearrange("(c p) -> p c", p=P)).then_inc(params.sem, 16)
                act.dma_start(conv_b[:, :], i["conv_b_2"][0].rearrange("(c p) -> p c", p=P)).then_inc(params.sem, 16)
                for n, r in (("b_f", bf_row), ("dt_bias_2", dtb_row), ("a_log_2", alog_row), ("d_skip_2", dskip_row)):
                    act.dma_start(r, i[n].partition_broadcast(P)).then_inc(params.sem, 16)
            act.wait_ge(consts.sem, 1)
            act.wait_ge(params.sem, 16 * 17)
            norm_act(act, pre[0], lambda m: (loaded_x.sem, 16 * (MB + 1)))
            norm_act(act, pre_mem)
            act.wait_ge(sem["rope_ang"], 1)
            nc.scalar.activation(trig, turned, ACT.Sin).then_inc(sem["rope_trig"], 1)
            project_act(act, pA_lat)
            project_act(act, pA_qm)
            project_act(act, pA_gate)
            norm_act(act, latent)
            for S in (*p_mem, pA_q, pA_kv):
                project_act(act, S)
            attend_act(act, attA)
            attend_act(act, attAm)
            post_act(act, post[0], pA_out, latent.sq(2 * MB))
            norm_act(act, pre[1], lambda m: post[0].add(m + 1))
            project_act(act, pB_qkv)
            project_act(act, pB_f)
            act.wait_ge(sem["gates_in"], 1)
            nc.scalar.activation(b_t, b_t, ACT.Exp).then_inc(sem["gates_exp"], 1)
            act.wait_ge(sem["gates_exp"], 1)
            nc.scalar.activation(b_t, b_t, ACT.Ln, bias=one_t[:, :]).then_inc(sem["gates_log"], 1)
            project_act(act, pB_qm)
            project_act(act, pB_gate)
            attend_act(act, attB)
            attend_act(act, attBm)
            post_act(act, post[1], pB_out, pre[1].sq(MB))
            norm_act(act, pre[2], lambda m: post[1].add(m + 1))
            ssd_act(act)
            project_act(act, pC_qkv)
            project_act(act, pC_zs)
            stick_act(act)
            project_act(act, pC_sb)
            gates_act(act)
            post_act(act, post[2], pC_out, ssd_norm.sq(2 * MB))

        @block.vector
        def _(dve):
            link = chain(dve, "dve_self")
            dve.wait_ge(params.sem, 16 * 17)
            dve.wait_ge(consts.sem, 1)
            link(nc.vector.tensor_copy(pos_f[:, :], pos_i[:, :]))
            link(nc.vector.tensor_tensor(trig[:, 0], pos_f[:, :].unsqueeze(2).to_broadcast([P, MB, HALF]),
                                         inv[:, :].unsqueeze(1).to_broadcast([P, MB, HALF]), ALU.mult))
            rounder = 1.5 * 2.0 ** 23
            for n in range(2):
                link(nc.vector.tensor_scalar(turns_n[:, n], trig[:, 0], float(1 / (2 * np.pi)), 0.25 * n, ALU.mult, ALU.add))
                link(nc.vector.tensor_scalar(turns_n[:, n], turns_n[:, n], rounder, None, ALU.add))
                link(nc.vector.tensor_scalar(turns_n[:, n], turns_n[:, n], rounder, None, ALU.subtract))
                src = trig[:, 0]
                two_pi = 2 * np.pi
                c1 = 6.28125
                c2 = float(np.float32(np.round((two_pi - c1) * 2 ** 20) / 2 ** 20))
                c3 = float(two_pi - c1 - c2)
                for c in (c1, c2, c3):
                    link(nc.vector.scalar_tensor_tensor(turned[:, n], turns_n[:, n], -c, src, ALU.mult, ALU.add))
                    src = turned[:, n]
                if n:
                    link(nc.vector.tensor_scalar(turned[:, n], turned[:, n], float(np.pi / 2), None, ALU.add))
                pi_ = float(np.nextafter(np.float32(np.pi), np.float32(0)))
                link(nc.vector.tensor_scalar(turned[:, n], turned[:, n], pi_, -pi_, ALU.min, ALU.max))
            nc.vector.tensor_copy(done_t[:, :], pos_f[:, 0:1]).then_inc(sem["rope_ang"], 1)
            norm_dve(dve, pre[0])
            norm_dve(dve, pre_mem)
            norm_dve(dve, latent)
            attend_dve(dve, attA)
            attend_dve(dve, attAm)
            norm_dve(dve, ytA)
            post_dve(dve, post[0], (row_in.sem, 16))
            norm_dve(dve, pre[1])
            dve.wait_ge(*pB_f.evac(MB))
            link(nc.vector.tensor_tensor(b_f, b_f, bf_row.unsqueeze(1).to_broadcast([P, MB, B_H]), ALU.add))
            nc.vector.scalar_tensor_tensor(b_t, b_f, -1.0, b_f, ALU.mult, ALU.min).then_inc(sem["gates_in"], 1)
            dve.wait_ge(sem["gates_log"], 1)
            nc.vector.scalar_tensor_tensor(b_u, b_f, 0.0, b_t, ALU.min, ALU.subtract).then_inc(sem["gates_in"], 1)
            dve.wait_ge(sem["sums"], 1)
            f_sum = bank[7][:, 0:MB * B_H].rearrange("p (m h) -> p m h", m=MB)
            nc.vector.tensor_scalar(b_F, f_sum, -1.0, None, ALU.mult).then_inc(sem["sums_out"], 1)
            nc.vector.tensor_scalar(b_8F, f_sum, HD ** 0.5, None, ALU.mult).then_inc(sem["sums_out"], 1)
            attend_dve(dve, attB)
            attend_dve(dve, attBm)
            norm_dve(dve, ytB)
            post_dve(dve, post[1], (row_in.sem, 32))
            norm_dve(dve, pre[2])
            ssd_dve(dve, link)
            stick_dve(dve)
            norm_dve(dve, ytC)
            gates_dve(dve)
            norm_dve(dve, ytM)
            post_dve(dve, post[2], (row_in.sem, 64))

        @block.tensor
        def _(pe):
            pe.wait_ge(consts.sem, 1)
            norm_pe(pe, pre[0])
            pe.wait_ge(*pre[0].normed(2 * MB))
            norm_pe(pe, pre_mem)
            pe.wait_ge(*pre_mem.normed(2 * MEMB))
            project_pe(pe, pA_lat)
            pe.wait_ge(*pA_lat.evac(2 * MB))
            project_pe(pe, pA_qm)
            pe.wait_ge(*pA_qm.evac(MB))
            project_pe(pe, pA_gate)
            pe.wait_ge(*pA_gate.evac(2 * MB))
            norm_pe(pe, latent)
            pe.wait_ge(*latent.normed(2 * MB))
            for S in p_mem:
                project_pe(pe, S)
                pe.wait_ge(*S.evac(4))
            project_pe(pe, pA_q)
            pe.wait_ge(*pA_q.evac(3 * MB))
            project_pe(pe, pA_kv)
            pe.wait_ge(*pA_kv.evac(3 * MB))
            attend_pe(pe, attA)
            pe.wait_ge(*attA.weighed(4 * A_H))
            attend_pe(pe, attAm)
            pe.wait_ge(*attAm.weighed(4 * MEM_H))
            norm_pe(pe, ytA)
            pe.wait_ge(*ytA.normed(2 * MB))
            project_pe(pe, pA_out)
            norm_pe(pe, pre[1])
            pe.wait_ge(*pre[1].normed(2 * MB))
            project_pe(pe, pB_qkv)
            pe.wait_ge(*pB_qkv.evac(6 * MB))
            project_pe(pe, pB_f)
            pe.wait_ge(*pB_f.evac(MB))
            project_pe(pe, pB_qm)
            pe.wait_ge(*pB_qm.evac(MB))
            project_pe(pe, pB_gate)
            pe.wait_ge(sem["gates_in"], 2)
            for m in range(MB):
                to = bank[7][:, m * B_H:(m + 1) * B_H]
                for c in range(m + 1):
                    mm = nc.tensor.matmul(to, (tri_le if c == m else ones)[:, :], b_u[:, c, :],
                                          start=c == 0, stop=c == m)
            mm.then_inc(sem["sums"], 1)
            pe.wait_ge(*pB_gate.evac(2 * MB))
            pe.wait_ge(sem["sums_out"], 2)
            attend_pe(pe, attB)
            pe.wait_ge(*attB.weighed(4 * B_H))
            attend_pe(pe, attBm)
            pe.wait_ge(*attBm.weighed(4 * MEM_H))
            norm_pe(pe, ytB)
            pe.wait_ge(*ytB.normed(2 * MB))
            project_pe(pe, pB_out)
            norm_pe(pe, pre[2])
            pe.wait_ge(*pre[2].normed(2 * MB))
            ssd_pe(pe)
            project_pe(pe, pC_qkv)
            pe.wait_ge(*pC_qkv.evac(6 * MB))
            project_pe(pe, pC_zs)
            pe.wait_ge(*pC_zs.evac(2 * MB))
            stick_pe(pe)
            pe.wait_ge(sem["s_y"], C_H)
            norm_pe(pe, ytC)
            pe.wait_ge(*ytC.normed(2 * MB))
            project_pe(pe, pC_sb)
            pe.wait_ge(*pC_sb.evac(2 * MB))
            project_pe(pe, pC_gate)
            pe.wait_ge(sem["g_done"], 4 * MB)
            norm_pe(pe, ytM)
            pe.wait_ge(*ytM.normed(2 * MB))
            project_pe(pe, pC_out)


def kernel(**inputs):
    import concourse.bacc as bacc
    from concourse.bass_utils import run_bass_kernel_spmd

    nc = bacc.Bacc("TRN2", target_bir_lowering=False, num_devices=1)
    arrays, args = {}, {}
    for name, value in inputs.items():
        a = np.ascontiguousarray(value)
        arrays[f"in_{name}"] = a
        args[name] = nc.dram_tensor(f"in_{name}", a.shape, mybir.dt.from_np(a.dtype), kind="ExternalInput").ap()
    out = nc.dram_tensor("out_0", (1, T, D), F32, kind="ExternalOutput").ap()
    build(nc, args, out)
    r = run_bass_kernel_spmd(nc, [arrays], core_ids=[0])
    return r.results[0]["out_0"]
```

```python
from contextlib import ExitStack

import numpy as np
import concourse.bass as bass
from concourse import mybir

P = 128
F32 = mybir.dt.float32
I32 = mybir.dt.int32
BF16 = mybir.dt.bfloat16
F32R = mybir.dt.float32r
ALU = mybir.AluOpType
ACT = mybir.ActivationFunctionType
AX = mybir.AxisListType
ds = bass.ds

D = 1024
T = 512
MB = T // P
KD = D // P
N_MEM = 256
MEMB = N_MEM // P
MEM_W, MAIN_W = D // 4, D - D // 4
HD = 64
MEM_H, A_H, B_H = MEM_W // HD, MAIN_W // HD, MAIN_W // HD
NOPE, ROPE = 64, 32
QK_A = NOPE + ROPE
HALF = ROPE // 2
Q_LORA, KV_LORA = 384, 256
LAT = Q_LORA + KV_LORA + ROPE
EPS = 1e-6
MASKED = -1e30
C_H, C_G, C_N, TAPS = 16, 2, 128, 4
INNER = C_H * HD
CONV = INNER + 2 * C_G * C_N
CONVC = CONV // P
XC = INNER // P
GH = C_H // C_G
ROPE_THETA = 10000.0
ARENA = 27136
PIECE = 1024
RAW = 4
SOFT_MAX = 40.0


class Count:

    def __init__(self, sem):
        self.sem, self.total = sem, 0

    def take(self, n):
        mark = Mark(self.sem, self.total)
        self.total += n
        return mark


class Mark:

    def __init__(self, sem, base):
        self.sem, self.base = sem, base

    def __call__(self, n):
        return self.sem, n + self.base


class Projection:

    def __init__(self, n, groups, width, pieces, piece0, before, src, product, dst, func, loop, w, c0,
                 parity, banks_free, evac):
        self.n = n
        self.groups = groups
        self.width = width
        self.pieces = pieces
        self.piece0 = piece0
        self.before = before
        self.turn = (2 if loop else n) * len(pieces)
        self.src = src
        self.product = product
        self.dst = dst
        self.func = func
        self.loop = loop
        self.w = w
        self.c0 = c0
        self.parity = parity
        self.banks_free = banks_free
        self.evac = evac

    def done_after(self, k, q, g):
        return self.before + self.groups * q + g + 1 + self.groups * self.turn * k

    def done(self, k, s, g):
        return self.done_after(k, len(self.pieces) * (s + 1) - 1, g)


class Norm:

    def __init__(self, free, high, src, blocks, norms, parts, gain, stat, sq, root, rinv, scaled, turned, normed):
        self.free = free
        self.high = high
        self.src = src
        self.blocks = blocks
        self.norms = norms
        self.parts = parts
        self.gain = gain
        self.stat = stat
        self.sq = sq
        self.root = root
        self.rinv = rinv
        self.scaled = scaled
        self.turned = turned
        self.normed = normed


class PostNorm:

    def __init__(self, sq, sum, root, out, add):
        self.sq = sq
        self.sum = sum
        self.root = root
        self.out = out
        self.add = add


class Attend:

    def __init__(self, heads, width, keys, causal, scale, q, k, v, y0, extra_q, extra_k, staged, headT,
                 headT_out, scores, neg_max, exped, probT, probT_out, attended, weighed):
        self.heads = heads
        self.width = width
        self.keys = keys
        self.causal = causal
        self.scale = scale
        self.q = q
        self.k = k
        self.v = v
        self.y0 = y0
        self.extra_q = extra_q
        self.extra_k = extra_k
        self.staged = staged
        self.headT = headT
        self.headT_out = headT_out
        self.scores = scores
        self.neg_max = neg_max
        self.exped = exped
        self.probT = probT
        self.probT_out = probT_out
        self.attended = attended
        self.weighed = weighed


class Staging:

    def __init__(self, staged, headT, headT_out):
        self.staged = staged
        self.headT = headT
        self.headT_out = headT_out


def reached(k, n, least):
    return not isinstance(k, int) or k > 0 or n >= least


def turns(eng, n, emit):
    emit(0, False)
    if n > 2:
        with eng.Fori(1, n - 1) as k:
            emit(k, False)
    if n > 1:
        emit(n - 1, True)


def build(nc, i, out):
    ctx = ExitStack()
    with ctx:
        def sb(name, shape, dt=F32):
            return ctx.enter_context(nc.sbuf_tensor(name, shape, dt))

        def count(name):
            return Count(ctx.enter_context(nc.semaphore(name)))

        bank = [ctx.enter_context(nc.psum_tensor(f"bank{n}", [P, 512], F32)) for n in range(8)]

        h = sb("h", [P, MB, D])
        acts_hi, acts_lo = (sb(n, [P, KD, T], F32R) for n in ("acts_hi", "acts_lo"))
        w_hi = [sb(f"w_hi{n}", [P, PIECE], F32R) for n in range(2)]
        w_lo = [sb(f"w_lo{n}", [P, PIECE], F32R) for n in range(2)]
        w_raw = [sb(f"w_raw{n}", [P, PIECE]) for n in range(RAW)]
        hn = sb("hn", [P, 2, D])
        junk = sb("junk", [P, D])
        row = sb("row", [P, D])
        ident, tri_le, tri_gt, ones = (sb(n, [P, P]) for n in ("ident", "tri_le", "tri_gt", "ones"))
        neg_ge, neg_ones = (sb(n, [P, P]) for n in ("neg_ge", "neg_ones"))
        ident_b, later_keys, not_before = (sb(n, [P, P], BF16) for n in ("ident_b", "later_keys", "not_before"))
        gains = sb("gains", [P, 48])
        conv_k = sb("conv_k", [P, TAPS, CONVC])
        conv_b = sb("conv_b", [P, CONVC])
        small = sb("small", [P, 64])
        eps_t = sb("eps_t", [P, 1])
        one_t = sb("one_t", [P, 1])
        stat = sb("stat", [P, 40])
        norm_stat = sb("norm_stat", [P, 3, 24])
        inv = sb("inv", [P, HALF])
        pos_i = sb("pos_i", [P, MB], I32)
        pos_f = sb("pos_f", [P, MB])
        done_t = sb("done_t", [P, 1])
        arena = sb("arena", [P, ARENA])

        def view(flat, at, *shape):
            v = flat[:, at:at + int(np.prod(shape))]
            if len(shape) == 2:
                return v.rearrange("p (a b) -> p a b", a=shape[0])
            if len(shape) == 3:
                return v.rearrange("p (a b c) -> p a b c", a=shape[0], b=shape[1])
            return v

        def cut(at, *shape):
            assert at + int(np.prod(shape)) <= ARENA, (at, shape)
            return view(arena, at, *shape)

        q_in = [cut(a * 384, MB, QK_A) for a in range(2)]
        k_in = [cut(768 + a * 384, MB, QK_A) for a in range(2)]
        qT = [cut(1536 + a * 512, T) for a in range(2)]
        kT = [cut(2560 + a * 512, T) for a in range(2)]
        probs = [cut(3584 + a * 512, T) for a in range(4)]
        probsT = [cut(5632 + a * 512, T) for a in range(2)]
        W0 = 6656
        gate = cut(W0, MB, D)
        L0 = W0 + MB * D
        memkv = cut(ARENA - 2048, 2, MEMB, 2 * MEM_W)
        q_mem = cut(ARENA - 3072, MB, MEM_W)
        trig = cut(L0, 2, MB, HALF)
        turns_n = cut(L0 + 128, 2, MB, HALF)
        turned = cut(L0 + 256, 2, MB, HALF)
        k_rot = cut(L0 + 640, MB, ROPE)
        rot_k = [cut(L0 + 384 + n * 64, MB, HALF) for n in range(4)]
        a_q = cut(L0 + 2560, MB, A_H * QK_A)
        a_kv = cut(L0 + 2560 + 4608, MB, A_H * 2 * HD)
        rot = [cut(3584 + n * 768, MB * A_H, HALF) for n in range(4)]
        mem_in = cut(L0 + 2560, MEMB, D)
        lat = cut(L0 + 2560 + 4608, MB, LAT)
        b_qkv = cut(L0, MB, 3 * MAIN_W)
        b_f, b_F, b_8F, b_t, b_u = (cut(L0 + 9216 + n * 48, MB, B_H) for n in range(5))
        x_in = [cut(11264 + n * 516, 516) for n in range(2)]
        acc = [cut(11264 + 1032 + n * 512, T) for n in range(2)]
        xcT = cut(0, CONVC, T)
        c_xd = cut(0, MB, D)
        c_x = cut(6144, MB, D)
        c_xdt = cut(10240, MB, D)
        c_y = cut(14336, MB, D)
        c_B = cut(18432, C_G, MB, C_N)
        c_sc = cut(19456, C_G, MB, P)
        prev = cut(20480, MB - 1, D)
        c_dt, c_u, dtA, acs, tot, eacs, etot, eend = (cut(23552 + n * 64, MB, C_H) for n in range(8))
        segD = [cut(24064 + n * 512, MB, P) for n in range(2)]
        att = [cut(25088 + n * 512, MB, P) for n in range(2)]
        off = cut(26112, T)
        a_neg = sb("a_neg", [P, C_H])
        s_qkv = cut(L0, MB, 3 * D)
        y_ssd = cut(L0 + 3 * MB * D, MB, D)
        y_sb = gate
        b_gate = cut(L0, 2 * D)
        g_tmp = [cut(L0 + 2048 + n * 512, T) for n in range(4)]

        G_PRE = [0, 8, 16]
        G_MEM, G_SSD, G_Q, G_KV = 24, 32, 40, 43
        bf_row, dtb_row = small[:, 0:B_H], small[:, 12:28]
        alog_row, dskip_row = small[:, 28:44], small[:, 44:60]

        loaded_x = count("loaded_x")
        params = count("params")
        row_in = count("row_in")
        w_in = [count(f"w_in{n}") for n in range(RAW)]
        w_high, w_rest = count("w_high"), count("w_rest")
        consts = count("consts")
        stored = count("stored")
        C = {n: count(n) for n in (
            "product", "evac", "sq", "root", "rinv", "scaled", "turned", "high", "normed",
            "post_sq", "post_sum", "post_root", "post_out", "post_add",
            "staged", "headT", "headT_out", "scores", "neg_max", "exped", "probT",
            "probT_out", "attended", "weighed")}

        pieces = []
        products = [0]
        last_bank = [0, 0]

        def project(w, c0, width, n, groups, product, dst, func=ACT.Copy, loop=False, evac=True):
            rows = w.shape[0] // P
            kp = min(rows, PIECE // width)
            of_chunk = [(r, min(kp, rows - r)) for r in range(0, rows, kp)]
            piece0, before = len(pieces), products[0]
            for c in range(n):
                pieces.extend((width, r) for _, r in of_chunk)
            products[0] += n * groups * len(of_chunk)
            parity = 1 - last_bank[0] if evac else 0
            banks_free = C["evac"].total - last_bank[1] if evac else C["evac"].total
            last_bank[:] = [(parity + n - 1) % 2, groups if evac else 0]
            return Projection(n=n, groups=groups, width=width, pieces=of_chunk, piece0=piece0, before=before,
                              src=None, product=product, dst=dst, func=func, loop=loop, w=w, c0=c0, parity=parity,
                              banks_free=banks_free, evac=C["evac"].take(n * groups) if evac else None)

        def chunk_turns(eng, S, emit):
            def both(k, last):
                emit(k, 0)
                emit(k, 1)
            if S.loop:
                assert S.n % 2 == 0 and S.turn % RAW == 0
                turns(eng, S.n // 2, both)
            else:
                for c in range(S.n):
                    emit(0, c)

        def bank_of(S, s, g):
            return bank[4 * ((S.parity + s) % 2) + g]

        def tokens_by(k0=0):
            def product(x, w, kk, g):
                return x[:, k0 + kk, g * P:(g + 1) * P], w
            return product

        def by_tokens(x, w, kk, g):
            return w[:, g * P:(g + 1) * P], x[:, kk, :]

        def to_columns(dst, c0=0):
            def place(S, k, s, g):
                return dst[:, g, ds((2 * k + s) * S.width + c0, S.width)]
            return place

        def project_sp(sp, S):
            def emit(k, s):
                for j, (r0, r) in enumerate(S.pieces):
                    q = s * len(S.pieces) + j
                    p = S.piece0 + q
                    if p >= RAW or not isinstance(k, int) or k:
                        sp.wait_ge(w_rest.sem, p - RAW + 1 + S.turn * k)
                    src = S.w.rearrange("(k p) n -> p k n", p=P)[:, r0:r0 + r, ds(S.c0 + (2 * k + s) * S.width, S.width)]
                    sp.dma_start(w_raw[p % RAW][:, 0:r * S.width].rearrange("p (k n) -> p k n", k=r),
                                 src).then_inc(w_in[p % RAW].sem, 16)
            chunk_turns(sp, S, emit)

        def piece_size(S, k, q):
            if isinstance(k, int):
                p = S.piece0 + S.turn * k + q
                return pieces[p][0] * pieces[p][1] if p < len(pieces) else 0
            return S.width * S.pieces[q % len(S.pieces)][1]

        def high_part(act, p, size, more=0):
            act.wait_ge(w_in[p % RAW].sem, 16 * (p // RAW + 1) + more)
            nc.scalar.activation(w_hi[p % 2][:, 0:size], w_raw[p % RAW][:, 0:size], ACT.Copy).then_inc(w_high.sem, 1)

        def rest(p, size):
            nc.gpsimd.tensor_tensor(w_lo[p % 2][:, 0:size], w_raw[p % RAW][:, 0:size],
                                    w_hi[p % 2][:, 0:size].bitcast(F32), ALU.subtract).then_inc(w_rest.sem, 1)

        def split_ahead_act(act, S, k, q):
            size = piece_size(S, k, q + 2)
            if size:
                act.wait_ge(C["product"].sem, S.done_after(k, q, S.groups - 1))
                high_part(act, S.piece0 + q + 2, size, S.turn // RAW * 16 * k if S.loop else 0)

        def project_pool(pool, S):
            def emit(k, s):
                for j in range(len(S.pieces)):
                    q = s * len(S.pieces) + j
                    size = piece_size(S, k, q + 2)
                    if size:
                        pool.wait_ge(w_high.sem, S.piece0 + q + 3 + S.turn * k)
                        rest(S.piece0 + q + 2, size)
            chunk_turns(pool, S, emit)

        def project_pe(pe, S):
            if S.banks_free > 0:
                pe.wait_ge(C["evac"].sem, S.banks_free)

            def emit(k, s):
                if S.evac and (s or not isinstance(k, int) or k):
                    pe.wait_ge(*S.evac(S.groups * (s - 1 + 2 * k)))
                for j, (r0, r) in enumerate(S.pieces):
                    q = s * len(S.pieces) + j
                    p = S.piece0 + q
                    pe.wait_ge(w_rest.sem, p + 1 + S.turn * k)
                    wh, wl = (w[p % 2][:, 0:r * S.width].rearrange("p (k n) -> p k n", k=r) for w in (w_hi, w_lo))
                    for g in range(S.groups):
                        for kk in range(r):
                            for t, (x, w) in enumerate(((acts_hi, wh), (acts_hi, wl), (acts_lo, wh))):
                                lhs, rhs = S.product(x, w[:, kk, :], r0 + kk, g)
                                mm = nc.tensor.matmul(bank_of(S, s, g)[0:lhs.shape[1], 0:rhs.shape[1]], lhs, rhs,
                                                      start=r0 + kk + t == 0,
                                                      stop=j == len(S.pieces) - 1 and kk == r - 1 and t == 2)
                        mm.then_inc(C["product"].sem, 1)
            chunk_turns(pe, S, emit)

        def project_act(act, S, take=None):
            def emit(k, s):
                for j in range(len(S.pieces)):
                    split_ahead_act(act, S, k, s * len(S.pieces) + j)
                for g in range(S.groups if S.evac else 0):
                    act.wait_ge(C["product"].sem, S.done(k, s, g))
                    if take:
                        take(k, s, g)
                    else:
                        to = S.dst(S, k, s, g)
                        nc.scalar.activation(to, bank_of(S, s, g)[:, 0:to.shape[1]], S.func).then_inc(S.evac.sem, 1)
            chunk_turns(act, S, emit)

        norm_stages = []

        def norm_stage(src, blocks, norms, parts, gain, free=None):
            nn, np_ = len(norms), len(parts)
            norm_stages.append(1)
            return Norm(free=free, high=C["high"].take(blocks * np_), src=src, blocks=blocks, norms=norms, parts=parts, gain=gain,
                         stat=norm_stat[:, len(norm_stages) % 3],
                         sq=C["sq"].take(blocks * nn), root=C["root"].take(blocks * nn),
                         rinv=C["rinv"].take(blocks * nn), scaled=C["scaled"].take(blocks * nn),
                         turned=C["turned"].take(blocks * np_), normed=C["normed"].take(blocks * np_))

        def norm_act(act, N, ready=None):
            for m in range(N.blocks):
                if ready:
                    act.wait_ge(*ready(m))
                for a, (c0, width) in enumerate(N.norms):
                    n = m * len(N.norms) + a
                    if n:
                        act.wait_ge(*N.sq(n))
                    nc.scalar.activation(junk[:, 0:width], N.src[:, m, c0:c0 + width], ACT.Square,
                                         accum_out=N.stat[:, n:n + 1]).then_inc(N.sq.sem, 1)
                    act.wait_ge(*N.sq(n + 1))
                    nc.scalar.activation(N.stat[:, 8 + n:9 + n], N.stat[:, n:n + 1], ACT.Sqrt,
                                         bias=eps_t[:, :], scale=1.0 / width).then_inc(N.root.sem, 1)

        def norm_pe(pe, N, ready=None):
            for m in range(N.blocks):
                if ready:
                    pe.wait_ge(*ready(m))
                for p, (a, c0, n, _, b0) in enumerate(N.parts):
                    if N.norms:
                        pe.wait_ge(*N.scaled(m * len(N.norms) + a + 1))
                        rows = hn[:, m % 2, :]
                    else:
                        rows = N.src[:, m, :]
                    for c in range(n):
                        mm = nc.tensor.transpose(bank[b0 + m][:, c * P:(c + 1) * P],
                                                 rows[:, c0 + c * P:c0 + (c + 1) * P], ident[:, :])
                    mm.then_inc(N.turned.sem, 1)

        def norm_dve(dve, N):
            def scale(m):
                for a, (c0, width) in enumerate(N.norms):
                    n = m * len(N.norms) + a
                    dve.wait_ge(*N.root(n + 1))
                    nc.vector.reciprocal(N.stat[:, 16 + n:17 + n], N.stat[:, 8 + n:9 + n]).then_inc(N.rinv.sem, 1)
                if m >= 2:
                    dve.wait_ge(*N.turned((m - 1) * len(N.parts)))
                for a, (c0, width) in enumerate(N.norms):
                    n = m * len(N.norms) + a
                    dve.wait_ge(*N.rinv(n + 1))
                    nc.vector.tensor_scalar(hn[:, m % 2, c0:c0 + width], N.src[:, m, c0:c0 + width],
                                            N.stat[:, 16 + n:17 + n], None, ALU.mult).then_inc(N.scaled.sem, 1)

            def collect(m):
                for p, (a, c0, n, k0, b0) in enumerate(N.parts):
                    dve.wait_ge(*N.turned(m * len(N.parts) + p + 1))
                    hi, lo = (t[:, k0:k0 + n, m * P:(m + 1) * P] for t in (acts_hi, acts_lo))
                    of = bank[b0 + m][:, 0:n * P].rearrange("p (c t) -> p c t", c=n)
                    if N.gain is None:
                        nc.vector.tensor_copy(hi, of).then_inc(N.high.sem, 1)
                        dve.wait_ge(*N.high(m * len(N.parts) + p + 1))
                        nc.vector.tensor_tensor(lo, of, hi.bitcast(F32), ALU.subtract).then_inc(N.normed.sem, 1)
                    else:
                        g = gains[:, N.gain + k0:N.gain + k0 + n].unsqueeze(2).to_broadcast([P, n, P])
                        nc.vector.tensor_tensor(hi, of, g, ALU.mult).then_inc(N.high.sem, 1)
                        dve.wait_ge(*N.high(m * len(N.parts) + p + 1))
                        for c in range(n):
                            ins = nc.vector.scalar_tensor_tensor(
                                lo[:, c, :], of[:, c, :], gains[:, N.gain + k0 + c:N.gain + k0 + c + 1],
                                hi[:, c, :].bitcast(F32), ALU.mult, ALU.subtract)
                        ins.then_inc(N.normed.sem, 1)

            for m in range(N.blocks + 1):
                if m < N.blocks:
                    scale(m)
                if m == 1 and N.free:
                    dve.wait_ge(C["product"].sem, N.free.done_after(0, N.free.n * len(N.free.pieces) - 1,
                                                                    N.free.groups - 1))
                if m:
                    collect(m - 1)

        whole = [(0, D)]
        whole_parts = [(0, 0, 4, 0, 0), (0, 512, 4, 4, 4)]

        def post_stage():
            return PostNorm(sq=C["post_sq"].take(2 * MB), sum=C["post_sum"].take(MB),
                         root=C["post_root"].take(MB), out=C["post_out"].take(3 * MB),
                         add=C["post_add"].take(MB))

        def post_act(act, O, S, before):
            act.wait_ge(*before)
            for m in range(MB):
                act.wait_ge(C["product"].sem, S.done(0, 1, m))
                for half in range(2):
                    n = 2 * m + half
                    if n:
                        act.wait_ge(*O.sq(n))
                    nc.scalar.activation(junk[:, 0:512], bank[4 * half + m][:, :], ACT.Square,
                                         accum_out=stat[:, 24 + n:25 + n]).then_inc(O.sq.sem, 1)
                act.wait_ge(*O.sum(m + 1))
                nc.scalar.activation(stat[:, 32 + m:33 + m], stat[:, 32 + m:33 + m], ACT.Sqrt,
                                     bias=eps_t[:, :], scale=1.0 / D).then_inc(O.root.sem, 1)

        def post_dve(dve, O, row_ready):
            dve.wait_ge(*row_ready)
            for m in range(MB):
                dve.wait_ge(*O.sq(2 * m + 2))
                nc.vector.tensor_tensor(stat[:, 32 + m:33 + m], stat[:, 24 + 2 * m:25 + 2 * m],
                                        stat[:, 25 + 2 * m:26 + 2 * m], ALU.add).then_inc(O.sum.sem, 1)
                dve.wait_ge(*O.root(m + 1))
                nc.vector.reciprocal(stat[:, 36 + m:37 + m], stat[:, 32 + m:33 + m]).then_inc(O.out.sem, 1)
                dve.wait_ge(*O.out(3 * m + 1))
                for half in range(2):
                    c0 = 512 * half
                    nc.vector.scalar_tensor_tensor(
                        gate[:, m, c0:c0 + 512], bank[4 * half + m][:, :], stat[:, 36 + m:37 + m],
                        row[:, c0:c0 + 512], ALU.mult, ALU.mult).then_inc(O.out.sem, 1)

        def post_pool(pool, O):
            for m in range(MB):
                pool.wait_ge(*O.out(3 * m + 3))
                nc.gpsimd.tensor_tensor(h[:, m, :], h[:, m, :], gate[:, m, :], ALU.add).then_inc(O.add.sem, 1)

        def attend_stage(heads, width, keys, causal_, scale, q, k, v, extra_q, extra_k, y0):
            s = 4 * heads
            return Attend(heads=heads, width=width, keys=keys, causal=causal_, scale=scale, q=q, k=k,
                         v=v, y0=y0, extra_q=extra_q, extra_k=extra_k,
                         staged=C["staged"].take(2 * heads), headT=C["headT"].take(2 * heads),
                         headT_out=C["headT_out"].take(2 * heads), scores=C["scores"].take(s),
                         neg_max=C["neg_max"].take(s),
                         exped=C["exped"].take(s), probT=C["probT"].take(s),
                         probT_out=C["probT_out"].take(s), attended=C["attended"].take(s),
                         weighed=C["weighed"].take(s))

        def n_keys(A, b):
            return b + 1 if A.causal else A.keys

        def attend_pool(pool, A):
            def emit(k, last):
                for a in range(2):
                    if reached(k, a, 2):
                        pool.wait_ge(*A.headT(2 * a - 2 + 4 * k))
                    parts_q = [A.q(k, a)] + A.extra_q(k, a)
                    parts_k = [A.k(k, a)] + A.extra_k(k, a)
                    for parts, buf, n in ((parts_q, q_in[a], MB), (parts_k, k_in[a], A.keys)):
                        for c0, src in parts:
                            ins = nc.gpsimd.tensor_copy(buf[:, 0:n, c0:c0 + src.shape[2]], src)
                        ins.then_inc(A.staged.sem, 1)
            turns(pool, A.heads // 2, emit)

        def attend_pe(pe, A):
            def turn(k, a, which):
                pe.wait_ge(*A.staged(2 * a + which + 1 + 4 * k))
                buf, n = ((q_in, MB), (k_in, A.keys))[which]
                for b in range(n):
                    mm = nc.tensor.transpose(bank[which][0:A.width, b * P:(b + 1) * P],
                                             buf[a % 2][:, b, 0:A.width], ident[:, :])
                mm.then_inc(A.headT.sem, 1)

            def score(k, j):
                a, b = j // 4 % 2, j % 4
                if b == 0:
                    pe.wait_ge(*A.headT_out(2 * (j // 4) + 2 + 4 * k))
                if reached(k, j, 4):
                    pe.wait_ge(*A.exped(j - 3 + 8 * k))
                n = n_keys(A, b) * P
                mm = nc.tensor.matmul(bank[2 + b][:, 0:n], qT[a][0:A.width, b * P:(b + 1) * P],
                                 kT[a][0:A.width, 0:n], start=True, stop=not A.causal)
                if A.causal:
                    mm = nc.tensor.matmul(bank[2 + b][:, n - P:n], ident_b[:, :], later_keys[:, :],
                                          start=False, stop=True)
                mm.then_inc(A.scores.sem, 1)

            def turn_probs(k, j):
                if not reached(k, j, 0):
                    return
                b = j % 4
                pe.wait_ge(*A.exped(j + 1 + 8 * k))
                if reached(k, j, 1):
                    pe.wait_ge(*A.probT_out(j + 8 * k))
                for c in range(n_keys(A, b)):
                    mm = nc.tensor.transpose(bank[6][:, c * P:(c + 1) * P],
                                             probs[b][:, c * P:(c + 1) * P], ident[:, :])
                mm.then_inc(A.probT.sem, 1)

            def values(k, j):
                if not reached(k, j, 0):
                    return
                b = j % 4
                pe.wait_ge(*A.probT_out(j + 1 + 8 * k))
                if reached(k, j, 1):
                    pe.wait_ge(*A.weighed(j + 8 * k))
                n = n_keys(A, b)
                for c in range(n):
                    mm = nc.tensor.matmul(bank[7][:, 0:HD], probsT[j % 2][:, c * P:(c + 1) * P],
                                          A.v(k, j // 4, c), start=c == 0, stop=c == n - 1)
                mm.then_inc(A.attended.sem, 1)

            def emit(k, last):
                if isinstance(k, int) and k == 0:
                    turn(0, 0, 0)
                    turn(0, 0, 1)
                for j in range(8):
                    score(k, j)
                    if j % 4 in (0, 2) and not (last and j >= 4):
                        turn(k, j // 4 + 1, j % 4 // 2)
                    turn_probs(k, j - 2)
                    values(k, j - 3)
                if last:
                    turn_probs(k, 6)
                    turn_probs(k, 7)
                    for j in (5, 6, 7):
                        values(k, j)
            turns(pe, A.heads // 2, emit)

        def attend_act(act, A):
            def collect(k, a, which):
                n = (MB, A.keys)[which] * P
                act.wait_ge(*A.headT(2 * a + which + 1 + 4 * k))
                nc.scalar.activation((qT, kT)[which][a % 2][0:A.width, 0:n], bank[which][0:A.width, 0:n],
                                     ACT.Copy, scale=(A.scale, 1.0)[which]).then_inc(A.headT_out.sem, 1)

            def emit(k, last):
                if isinstance(k, int) and k == 0:
                    collect(0, 0, 0)
                    collect(0, 0, 1)
                for j in range(8):
                    b = j % 4
                    n = n_keys(A, b) * P
                    act.wait_ge(*A.neg_max(j + 1 + 8 * k))
                    if reached(k, j, 4):
                        act.wait_ge(*A.probT(j - 3 + 8 * k))
                    nc.scalar.activation(probs[b][:, 0:n], bank[2 + b][:, 0:n], ACT.Exp,
                                         bias=stat[:, j:j + 1], accum_out=stat[:, 8 + j:9 + j]
                                         ).then_inc(A.exped.sem, 1)
                    if b in (0, 2) and not (last and j >= 4):
                        collect(k, j // 4 + 1, b // 2)
            turns(act, A.heads // 2, emit)

        def attend_dve(dve, A):
            def maximum(k, j):
                b = j % 4
                n = n_keys(A, b) * P
                dve.wait_ge(*A.scores(j + 1 + 8 * k))
                nc.vector.tensor_reduce(stat[:, j:j + 1], bank[2 + b][:, 0:n], AX.X, ALU.max,
                                        negate=True).then_inc(A.neg_max.sem, 1)

            def collect(k, j):
                if not reached(k, j, 0):
                    return
                b = j % 4
                n = n_keys(A, b) * P
                dve.wait_ge(*A.probT(j + 1 + 8 * k))
                nc.vector.reciprocal(stat[:, 16 + j % 8:17 + j % 8], stat[:, 8 + j % 8:9 + j % 8])
                if reached(k, j, 2):
                    dve.wait_ge(*A.attended(j - 1 + 8 * k))
                nc.vector.tensor_copy(probsT[j % 2][:, 0:n], bank[6][:, 0:n]).then_inc(A.probT_out.sem, 1)

            def weigh(k, j):
                if not reached(k, j, 0):
                    return
                dve.wait_ge(*A.attended(j + 1 + 8 * k))
                y = gate[:, j % 4, ds((2 * k + j // 4) * HD + A.y0, HD)]
                nc.vector.scalar_tensor_tensor(y, bank[7][:, 0:HD], stat[:, 16 + j % 8:17 + j % 8], y,
                                               ALU.mult, ALU.mult).then_inc(A.weighed.sem, 1)

            def emit(k, last):
                for j in range(8):
                    maximum(k, j)
                    collect(k, j - 2)
                    weigh(k, j - 3)
                if last:
                    collect(k, 6)
                    weigh(k, 5)
                    collect(k, 7)
                    weigh(k, 6)
                    weigh(k, 7)
            turns(dve, A.heads // 2, emit)

        def head_of(src, stride, c0=0, width=HD, at=0):
            def pick(k, a):
                return at, src[:, :, ds((2 * k + a) * stride + c0, width)]
            return pick

        def rows_of(src, stride, c0=0):
            def pick(k, a, c):
                return src[:, c, ds((2 * k + a) * stride + c0, HD)]
            return pick

        def none(k, a):
            return []

        pre = [norm_stage(h, MB, whole, whole_parts, G_PRE[0])]
        tb = tokens_by()
        pA_lat = project(i["w_in_a"][0], 0, LAT // 2, 2, MB, tb, to_columns(lat))
        pA_qm = project(i["w_in_a"][0], LAT, MEM_W, 1, MB, tb, to_columns(q_mem))
        pA_gate = project(i["w_in_a"][0], LAT + MEM_W, 512, 2, MB, tb, to_columns(gate), ACT.Silu)
        pre_mem = norm_stage(mem_in, MEMB, whole, whole_parts, G_MEM, pA_gate)

        def mem_place(layer):
            def place(S, k, s, g):
                return memkv[:, layer, g, :]
            return place

        p_mem = [project(i["w_mem_kv"][n], 0, 2 * MEM_W, 1, MEMB, tb, mem_place(n)) for n in range(2)]
        latent = norm_stage(lat, MB, [(0, Q_LORA), (Q_LORA, KV_LORA)],
                            [(0, 0, 3, 0, 0), (1, Q_LORA, 2, 3, 4)], G_Q, p_mem[1])

        pA_q = project(i["w_q_up_a"][0], 0, 384, 3, MB, tb, to_columns(a_q))
        pA_kv = project(i["w_kv_up_a"][0], 0, 512, 3, MB, tokens_by(Q_LORA // P), to_columns(a_kv))
        attA = attend_stage(A_H, QK_A, MB, True, QK_A ** -0.5, head_of(a_q, QK_A, 0, QK_A),
                            head_of(a_kv, 2 * HD), rows_of(a_kv, 2 * HD, HD), none, none, 0)

        def mem_attend(layer):
            return attend_stage(MEM_H, HD, MEMB, False, HD ** -0.5, head_of(q_mem, HD),
                                head_of(memkv[:, layer], HD), rows_of(memkv[:, layer], HD, MEM_W),
                                none, none, MAIN_W)

        attAm = mem_attend(0)
        no_norm = [(0, 0, 4, 0, 0), (0, 512, 4, 4, 4)]
        ytA = norm_stage(gate, MB, [], no_norm, None, pA_kv)
        pA_out = project(i["w_out"][0], 0, 512, 2, MB, tb, None, evac=False)
        post = [post_stage()]

        pre.append(norm_stage(h, MB, whole, whole_parts, G_PRE[1], pA_out))
        wb = i["w_in_b"][0]
        pB_qkv = project(wb, 0, 384, 6, MB, tb, to_columns(b_qkv), loop=True)
        pB_f = project(wb, 3 * MAIN_W, B_H, 1, MB, tb, to_columns(b_f))
        pB_qm = project(wb, 3 * MAIN_W + B_H, MEM_W, 1, MB, tb, to_columns(q_mem))
        pB_gate = project(wb, 3 * MAIN_W + B_H + MEM_W, 512, 2, MB, tb, to_columns(gate), ACT.Silu)
        attB = attend_stage(
            B_H, HD + 2, MB, True, HD ** -0.5, head_of(b_qkv, HD), head_of(b_qkv, HD, MAIN_W),
            rows_of(b_qkv, HD, 2 * MAIN_W),
            lambda k, a: [(HD + 1, b_8F[:, :, ds(2 * k + a, 1)])],
            lambda k, a: [(HD, b_F[:, :, ds(2 * k + a, 1)])], 0)
        attBm = mem_attend(1)
        ytB = norm_stage(gate, MB, [], no_norm, None, pB_gate)
        pB_out = project(i["w_out"][1], 0, 512, 2, MB, tb, None, evac=False)
        post.append(post_stage())

        pre.append(norm_stage(h, MB, whole, whole_parts, G_PRE[2], pB_out))
        wc = i["w_in_2"][0]
        Z0, X0, DT0, Q0 = 0, INNER, INNER + CONV, INNER + CONV + C_H
        ZS0, G0 = Q0 + 3 * D, Q0 + 4 * D
        pC_x = project(wc, X0, 256, 6, 2, by_tokens, None, loop=True)
        pC_dt = project(wc, DT0, C_H, 1, MB, tb, to_columns(c_dt))
        pC_z = project(wc, Z0, 512, 2, MB, tb, to_columns(c_x), ACT.Silu)
        ssd_norm = norm_stage(c_y, MB, [(0, 512), (512, 512)], [(0, 0, 4, 0, 0), (1, 512, 4, 4, 4)], G_SSD, pC_z)
        pC_ssd = project(i["w_ssd_proj_2"][0], 0, 512, 2, MB, tb, to_columns(y_ssd))
        pre_qkv = norm_stage(h, MB, whole, whole_parts, G_PRE[2], pC_ssd)
        pC_qkv = project(wc, Q0, 512, 6, MB, tb, to_columns(s_qkv), loop=True)
        pC_zs = project(wc, ZS0, 512, 2, MB, tb, to_columns(gate), ACT.Silu)
        ytC = norm_stage(gate, MB, [], no_norm, None, pC_zs)
        pC_sb = project(i["w_sb_proj_2"][0], 0, 512, 2, MB, tb, to_columns(y_sb))

        pre_gate = norm_stage(h, MB, whole, whole_parts, G_PRE[2], pC_sb)
        pC_gate = project(wc, G0, 512, 4, MB, tb, None)
        ytM = norm_stage(y_ssd, MB, [], no_norm, None, pC_gate)
        pC_out = project(i["w_out_2"][0], 0, 512, 2, MB, tb, None, evac=False)
        post.append(post_stage())

        misc = {n: count(n) for n in (
            "pool_self", "dve_self", "act_self", "rope_ang", "rope_trig", "rope_done", "kr_done",
            "gates_in", "gates_exp", "gates_log", "sums", "sums_out",
            "conv_in", "conv_acc", "conv_out", "xT_turned", "xT_out", "ssd_dt", "ssd_sc", "ssd_sc_out",
            "ssd_seg", "ssd_seg_in", "ssd_exp", "ssd_att", "ssd_diag", "ssd_y", "ssd_state",
            "ssd_prev", "ssd_off", "ssd_off_out", "ssd_ready", "ssd_gated",
            "z", "z_min", "soft", "sp", "remain", "w_exp", "s_out", "s_y",
            "g_biased", "g_sig", "g_merge", "g_done")}
        started = {}
        sem = {n: c.sem for n, c in misc.items()}

        def chain(eng, name):
            def link(ins):
                misc[name].total += 1
                ins.then_inc(sem[name], 1)
                eng.wait_ge(sem[name], misc[name].total)
            return link

        XT = 2 * MB + C_G

        def conv_taps(c):
            return [conv_k[:, t, ds(c, 1)] for t in range(TAPS)]

        def ssd_act(act):
            S = pC_x

            def silu(k, n):
                act.wait_ge(sem["conv_acc"], n + 1 + 4 * k)
                nc.scalar.activation(xcT[:, ds(4 * k + n, 1), :].rearrange("p o t -> p (o t)"),
                                     acc[n % 2], ACT.Silu).then_inc(sem["conv_out"], 1)

            def take(k, s, g):
                n = s * S.groups + g
                if reached(k, n, 2):
                    act.wait_ge(sem["conv_acc"], n - 1 + 4 * k)
                nc.scalar.activation(x_in[n % 2][:, TAPS - 1:TAPS - 1 + T], bank_of(S, s, g)[:, :],
                                     ACT.Copy).then_inc(S.evac.sem, 1)
                if reached(k, n, 1):
                    silu(k, n - 1)
            act.wait_ge(*pre[2].normed(1))
            project_act(act, S, take)
            silu(S.n // 2 - 1, 3)
            project_act(act, pC_dt)
            for f in range(XT):
                act.wait_ge(sem["xT_turned"], f + 1)
                to = c_x[:, f // 2, f % 2 * 512:f % 2 * 512 + 512] if f < 2 * MB else \
                    c_B[:, f - 2 * MB].rearrange("p m n -> p (m n)")
                nc.scalar.activation(to, bank[4 + f % 4][:, :], ACT.Copy).then_inc(sem["xT_out"], 1)
            act.wait_ge(sem["ssd_dt"], 1)
            nc.scalar.activation(acs, acs, ACT.Exp).then_inc(sem["ssd_ready"], 1)
            act.wait_ge(sem["ssd_ready"], 1)
            nc.scalar.activation(acs, acs, ACT.Ln, bias=one_t[:, :]).then_inc(sem["ssd_ready"], 1)
            nc.scalar.activation(a_neg[:, :], alog_row, ACT.Exp).then_inc(sem["ssd_ready"], 1)
            act.wait_ge(sem["sums"], 2)
            nc.scalar.activation(cut(23552 + 5 * 64, 3 * MB * C_H), bank[2][:, 0:3 * MB * C_H],
                                 ACT.Exp).then_inc(sem["ssd_ready"], 1)
            for g in range(C_G):
                def emit_heads(k, last, g=g):
                    for a in range(2):
                        n = GH * g + a
                        act.wait_ge(sem["ssd_seg"], n + 1 + 2 * k)
                        if g or reached(k, a, 2):
                            act.wait_ge(sem["ssd_diag"], n - 1 + 2 * k)
                        nc.scalar.activation(att[a].rearrange("p m l -> p (m l)"), bank[4 + a][:, :],
                                             ACT.Exp).then_inc(sem["ssd_exp"], 1)
                turns(act, GH // 2, emit_heads)
            act.wait_ge(sem["ssd_y"], C_H)
            project_act(act, pC_z)
            norm_act(act, ssd_norm, lambda m: (sem["ssd_gated"], m + 1))
            norm_act(act, pre_qkv)
            project_act(act, pC_ssd)

        def ssd_pe(pe):
            project_pe(pe, pC_x)
            project_pe(pe, pC_dt)
            pe.wait_ge(sem["conv_out"], CONVC)
            for f in range(XT):
                if f >= 4:
                    pe.wait_ge(sem["xT_out"], f - 3)
                for c in range(4):
                    src = xcT[:, 4 * (f % 2) + c, f // 2 * P:(f // 2 + 1) * P] if f < 2 * MB else \
                        xcT[:, XC + f - 2 * MB, c * P:(c + 1) * P]
                    mm = nc.tensor.transpose(bank[4 + f % 4][:, c * P:(c + 1) * P], src, ident[:, :])
                mm.then_inc(sem["xT_turned"], 1)
            pe.wait_ge(*pC_dt.evac(MB))
            for g in range(C_G):
                for m in range(MB):
                    mm = nc.tensor.matmul(bank[g][:, m * P:(m + 1) * P], xcT[:, XC + g, m * P:(m + 1) * P],
                                          xcT[:, XC + C_G + g, m * P:(m + 1) * P], start=True, stop=True)
                mm.then_inc(sem["ssd_sc"], 1)
            pe.wait_ge(sem["ssd_dt"], 2)
            for n, w in enumerate((tri_le, ones, tri_gt)):
                mm = nc.tensor.matmul(bank[2][:, n * 64:(n + 1) * 64], w[:, :],
                                      dtA.rearrange("p m h -> p (m h)"), start=True, stop=True)
            mm.then_inc(sem["sums"], 1)
            pe.wait_ge(sem["xT_out"], XT)
            for g in range(C_G):
                def seg(k, a, g=g):
                    n = GH * g + a
                    pe.wait_ge(sem["ssd_seg_in"], n + 1 + 2 * k)
                    if g or reached(k, a, 2):
                        pe.wait_ge(sem["ssd_exp"], n - 1 + 2 * k)
                    nc.tensor.matmul(bank[4 + a][:, :], tri_gt[:, :], segD[a].rearrange("p m l -> p (m l)"),
                                     start=True, stop=True).then_inc(sem["ssd_seg"], 1)

                def diag(k, a, g=g):
                    n = GH * g + a
                    b = a % 2
                    pe.wait_ge(sem["ssd_att"], n + 1 + 2 * k)
                    if g or reached(k, a, 2):
                        pe.wait_ge(sem["ssd_y"], n - 1 + 2 * k)
                    for m in range(MB):
                        mm = nc.tensor.matmul(bank[6 + b][:, m * HD:(m + 1) * HD], att[b][:, m, :],
                                              c_xdt[:, m, ds((n + 2 * k) * HD, HD)], start=True, stop=True)
                    mm.then_inc(sem["ssd_diag"], 1)

                def emit(k, last):
                    seg(k, 0)
                    if reached(k, 0, 1):
                        diag(k, -1)
                    seg(k, 1)
                    diag(k, 0)
                    if last:
                        diag(k, 1)
                turns(pe, GH // 2, emit)
            pe.wait_ge(sem["ssd_sc_out"], C_G)
            pe.wait_ge(sem["ssd_ready"], 5)
            for n in range(2 * (MB - 1)):
                m, g = n // 2, n % 2
                if n >= 4:
                    pe.wait_ge(sem["ssd_prev"], n - 3)
                nc.tensor.matmul(bank[n % 4][:, :], c_B[:, g, m, :], c_xd[:, m, g * 512:(g + 1) * 512],
                                 start=True, stop=True).then_inc(sem["ssd_state"], 1)
            for n in range(2 * (MB - 1)):
                m, g = n // 2 + 1, n % 2
                pe.wait_ge(sem["ssd_prev"], max(n + 1, 2 * (MB - 1)) if n < 4 else 2 * (MB - 1))
                if n >= 4:
                    pe.wait_ge(sem["ssd_off_out"], 2 * (n - 3))
                nc.tensor.matmul(bank[n % 4][:, :], xcT[:, XC + C_G + g, m * P:(m + 1) * P],
                                 prev[:, m - 1, g * 512:(g + 1) * 512],
                                 start=True, stop=True).then_inc(sem["ssd_off"], 1)
            pe.wait_ge(sem["ssd_off_out"], 4 * (MB - 1))
            project_pe(pe, pC_z)
            pe.wait_ge(*pC_z.evac(2 * MB))
            norm_pe(pe, ssd_norm)
            pe.wait_ge(*ssd_norm.normed(2 * MB))
            project_pe(pe, pC_ssd)
            pe.wait_ge(*pC_ssd.evac(2 * MB))
            norm_pe(pe, pre_qkv)
            pe.wait_ge(*pre_qkv.normed(2 * MB))

        def ssd_pool(pool, link):
            pool.wait_ge(sem["xT_out"], 2 * MB)
            skip = dskip_row.unsqueeze(2).to_broadcast([P, C_H, HD])
            for m in range(MB):
                link(nc.gpsimd.tensor_tensor(c_y[:, m, :].rearrange("p (h d) -> p h d", d=HD),
                                             c_x[:, m, :].rearrange("p (h d) -> p h d", d=HD), skip, ALU.mult))
            started["y"] = misc["pool_self"].total
            pool.wait_ge(sem["ssd_dt"], 2)
            for g in range(C_G):
                def emit(k, last, g=g):
                    for a in range(2):
                        n = GH * g + a
                        if g or reached(k, a, 2):
                            pool.wait_ge(sem["ssd_seg"], n - 1 + 2 * k)
                        nc.gpsimd.tensor_tensor(
                            segD[a], tri_le[:, :].unsqueeze(1).to_broadcast([P, MB, P]),
                            dtA[:, :, ds(n + 2 * k, 1)].to_broadcast([P, MB, P]),
                            ALU.mult).then_inc(sem["ssd_seg_in"], 1)
                turns(pool, GH // 2, emit)

        def ssd_dve(dve, link):
            S = pC_x
            for b in range(2):
                link(nc.vector.memset(x_in[b][:, 0:TAPS - 1], 0.0))

            def emit(k, s):
                for g in range(S.groups):
                    n = s * S.groups + g
                    src, to, taps = x_in[n % 2], acc[n % 2], conv_taps(4 * k + n)
                    dve.wait_ge(*S.evac(n + 1 + 4 * k))
                    if reached(k, n, 2):
                        dve.wait_ge(sem["conv_out"], n - 1 + 4 * k)
                    nc.vector.tensor_scalar(to, src[:, 0:T], taps[0], conv_b[:, ds(4 * k + n, 1)],
                                            ALU.mult, ALU.add).then_inc(sem["conv_in"], 1)
                    for t in range(1, TAPS):
                        dve.wait_ge(sem["conv_in"], 3 * n + t + 12 * k)
                        ins = nc.vector.scalar_tensor_tensor(to, src[:, t:t + T], taps[t], to, ALU.mult, ALU.add)
                        ins.then_inc(sem["conv_in" if t < TAPS - 1 else "conv_acc"], 1)
            chunk_turns(dve, S, emit)
            dve.wait_ge(*pC_dt.evac(MB))
            link(nc.vector.tensor_tensor(c_u, c_dt, dtb_row.unsqueeze(1).to_broadcast([P, MB, C_H]), ALU.add))
            nc.vector.scalar_tensor_tensor(acs, c_u, -1.0, c_u, ALU.mult, ALU.min).then_inc(sem["ssd_dt"], 1)
            dve.wait_ge(sem["ssd_ready"], 3)
            link(nc.vector.scalar_tensor_tensor(c_dt, c_u, 0.0, acs, ALU.max, ALU.add))
            nc.vector.scalar_tensor_tensor(dtA, c_dt, -1.0, a_neg[:, :].unsqueeze(1).to_broadcast([P, MB, C_H]),
                                           ALU.mult, ALU.mult).then_inc(sem["ssd_dt"], 1)
            for g in range(C_G):
                dve.wait_ge(sem["ssd_sc"], g + 1)
                nc.vector.tensor_tensor(c_sc[:, g],
                                        bank[g][:, :].rearrange("p (m l) -> p m l", m=MB),
                                        tri_le[:, :].unsqueeze(1).to_broadcast([P, MB, P]),
                                        ALU.mult).then_inc(sem["ssd_sc_out"], 1)
            dve.wait_ge(sem["xT_out"], 2 * MB)
            by_head = "p m (h d) -> p (m h) d"
            link(nc.vector.tensor_tensor(c_xdt.rearrange(by_head, d=HD), c_x.rearrange(by_head, d=HD),
                                         c_dt.rearrange("p m h -> p (m h)").unsqueeze(2).to_broadcast([P, MB * C_H, HD]),
                                         ALU.mult))
            dve.wait_ge(sem["ssd_ready"], 4)
            nb = MB - 1
            nc.vector.tensor_tensor(c_xd[:, 0:nb].rearrange(by_head, d=HD), c_xdt[:, 0:nb].rearrange(by_head, d=HD),
                                    eend[:, 0:nb].rearrange("p m h -> p (m h)").unsqueeze(2).to_broadcast([P, nb * C_H, HD]),
                                    ALU.mult).then_inc(sem["ssd_ready"], 1)
            dve.wait_ge(sem["pool_self"], started["y"])
            for g in range(C_G):
                def weigh(k, a, g=g):
                    n = GH * g + a
                    dve.wait_ge(sem["ssd_exp"], n + 1 + 2 * k)
                    nc.vector.tensor_tensor(att[a], att[a], c_sc[:, g],
                                            ALU.mult).then_inc(sem["ssd_att"], 1)

                def add(k, a, g=g):
                    n = GH * g + a
                    dve.wait_ge(sem["ssd_diag"], n + 1 + 2 * k)
                    y = c_y[:, :, ds((n + 2 * k) * HD, HD)]
                    nc.vector.tensor_tensor(y, y, bank[6 + a % 2][:, 0:MB * HD].rearrange("p (m d) -> p m d", m=MB),
                                            ALU.add).then_inc(sem["ssd_y"], 1)

                def emit_heads(k, last):
                    weigh(k, 0)
                    if reached(k, 0, 1):
                        add(k, -1)
                    weigh(k, 1)
                    add(k, 0)
                    if last:
                        add(k, 1)
                turns(dve, GH // 2, emit_heads)
            half = "p (h d) -> p h d"

            def per_head(t, m, g):
                return t[:, m, g * GH:(g + 1) * GH].unsqueeze(2).to_broadcast([P, GH, HD])
            for n in range(2 * (MB - 1)):
                m, g = n // 2, n % 2
                c0 = slice(g * 512, (g + 1) * 512)
                if m:
                    link(nc.vector.tensor_tensor(prev[:, m, c0].rearrange(half, d=HD),
                                                 prev[:, m - 1, c0].rearrange(half, d=HD), per_head(etot, m, g), ALU.mult))
                dve.wait_ge(sem["ssd_state"], n + 1)
                if m:
                    nc.vector.tensor_tensor(prev[:, m, c0], prev[:, m, c0], bank[n % 4][:, :],
                                            ALU.add).then_inc(sem["ssd_prev"], 1)
                    dve.wait_ge(sem["ssd_prev"], n + 1)
                else:
                    nc.vector.tensor_copy(prev[:, m, c0], bank[n % 4][:, :]).then_inc(sem["ssd_prev"], 1)
                    dve.wait_ge(sem["ssd_prev"], n + 1)
            for n in range(2 * (MB - 1)):
                m, g = n // 2 + 1, n % 2
                dve.wait_ge(sem["ssd_off"], n + 1)
                nc.vector.tensor_tensor(off.rearrange(half, d=HD), bank[n % 4][:, :].rearrange(half, d=HD),
                                        per_head(eacs, m, g), ALU.mult).then_inc(sem["ssd_off_out"], 1)
                dve.wait_ge(sem["ssd_off_out"], 2 * n + 1)
                y = c_y[:, m, g * 512:(g + 1) * 512]
                nc.vector.tensor_tensor(y, y, off, ALU.add).then_inc(sem["ssd_off_out"], 1)
                dve.wait_ge(sem["ssd_off_out"], 2 * n + 2)
            for m in range(MB):
                dve.wait_ge(*pC_z.evac(MB + m + 1))
                nc.vector.tensor_tensor(c_y[:, m, :], c_y[:, m, :], c_x[:, m, :], ALU.mult).then_inc(sem["ssd_gated"], 1)
            dve.wait_ge(sem["ssd_gated"], MB)
            norm_dve(dve, ssd_norm)
            norm_dve(dve, pre_qkv)

        SB = 2 * C_H
        st = Staging(staged=C["staged"].take(SB), headT=C["headT"].take(SB), headT_out=C["headT_out"].take(SB))
        w_at = [0, 128, 384, 768]
        hn_ = hn[:, :, :].rearrange("p m d -> p (m d)")
        sp_ = [[view(hn_, 1280 * a + w_at[u], P * (u + 1)) for u in range(4 - a)] for a in range(2)]
        sp_[1].append(junk[:, 0:T])
        w_ = [[cut(3584 + 1280 * a + w_at[u], P * (u + 1)) for u in range(4)] for a in range(2)]

        def stick_pool(pool):
            def stage(k, a):
                if reached(k, a, 2):
                    pool.wait_ge(*st.headT(2 * a - 2 + 4 * k))
                for buf, c0 in ((q_in, 0), (k_in, D)):
                    nc.gpsimd.tensor_copy(buf[a % 2][:, :, 0:HD],
                                          s_qkv[:, :, ds((2 * k + a) * HD + c0, HD)]).then_inc(st.staged.sem, 1)

            def emit(k, last):
                if isinstance(k, int) and k == 0:
                    stage(0, 0)
                for a in range(1, 2 if last else 3):
                    stage(k, a)
            pool.wait_ge(*pC_qkv.evac(6 * MB))
            turns(pool, C_H // 2, emit)

        def stick_pe(pe):
            def turn(k, a, which):
                pe.wait_ge(*st.staged(2 * a + which + 1 + 4 * k))
                for b in range(MB):
                    mm = nc.tensor.transpose(bank[which][0:QK_A, b * P:(b + 1) * P],
                                             (q_in, k_in)[which][a % 2][:, b, :], ident[:, :])
                mm.then_inc(st.headT.sem, 1)

            def score(k, j):
                a, u = j // 4, j % 4
                if u == 0:
                    pe.wait_ge(*st.headT_out(2 * a + 2 + 4 * k))
                if reached(k, j, 4):
                    pe.wait_ge(sem["w_exp"], j - 3 + 8 * k)
                kb = MB - 1 - u
                nc.tensor.matmul(bank[2 + u][:, 0:P * (u + 1)], kT[a][0:HD, kb * P:(kb + 1) * P],
                                 qT[a][0:HD, kb * P:T], start=True, stop=False, skip_group_check=True)
                nc.tensor.matmul(bank[2 + u][:, 0:P], ident_b[:, :], not_before[:, :], start=False,
                                 stop=False, skip_group_check=True).then_inc(sem["z"], 1)

            def remain(k, j):
                if not reached(k, j, 0):
                    return
                a, u = j // 4 % 2, j % 4
                pe.wait_ge(sem["sp"], j + 1 + 8 * k)
                for v in range(u, -1, -1):
                    w = P * (v + 1)
                    c0 = P * (u - v)
                    mm = nc.tensor.matmul(bank[2 + u][:, c0:c0 + w], (neg_ge if v == u else neg_ones)[:, :],
                                          sp_[a][v], start=False, stop=v == 0, skip_group_check=True)
                mm.then_inc(sem["remain"], 1)

            def values(k, a):
                if not reached(k, a, 0):
                    return
                pe.wait_ge(sem["w_exp"], 4 * a + 4 + 8 * k)
                if reached(k, a, 2):
                    pe.wait_ge(sem["s_y"], a - 1 + 2 * k)
                for b in range(MB):
                    for kb in range(b + 1):
                        u = MB - 1 - kb
                        mm = nc.tensor.matmul(
                            bank[6 + a % 2][:, b * HD:(b + 1) * HD], w_[a % 2][u][:, (b - kb) * P:(b - kb + 1) * P],
                            s_qkv[:, kb, ds((2 * k + a) * HD + 2 * D, HD)], start=kb == 0, stop=kb == b)
                mm.then_inc(sem["s_out"], 1)

            def emit(k, last):
                if isinstance(k, int) and k == 0:
                    turn(0, 0, 0)
                    turn(0, 0, 1)
                for j in range(8):
                    score(k, j)
                    if j % 4 in (2, 3) and not (last and j >= 4):
                        turn(k, j // 4 + 1, j % 4 - 2)
                    remain(k, j - 2)
                    if j % 4 == 3:
                        values(k, j // 4 - 1)
                if last:
                    remain(k, 6)
                    remain(k, 7)
                    values(k, 1)
            turns(pe, C_H // 2, emit)

        def stick_act(act):
            def weight_(k, j):
                if reached(k, j, 0):
                    u = j % 4
                    act.wait_ge(sem["remain"], j + 1 + 8 * k)
                    nc.scalar.activation(w_[j // 4 % 2][u], bank[2 + u][:, 0:P * (u + 1)],
                                         ACT.Exp).then_inc(sem["w_exp"], 1)

            nc.scalar.preload_act_table_set("natural_log_exp_and_others")

            def emit(k, last):
                for j in range(8):
                    t = sp_[j // 4][j % 4]
                    act.wait_ge(sem["z_min"], j + 1 + 8 * k)
                    nc.scalar.activation(t, t, ACT.Exp).then_inc(sem["soft"], 1)
                    act.wait_ge(sem["soft"], 2 * j + 1 + 16 * k)
                    nc.scalar.activation(t, t, ACT.Ln, bias=one_t[:, :]).then_inc(sem["soft"], 1)
                    weight_(k, j - 2)
                if last:
                    weight_(k, 6)
                    weight_(k, 7)
            turns(act, C_H // 2, emit)

        def stick_dve(dve):
            def collect(k, a, which):
                dve.wait_ge(*st.headT(2 * a + which + 1 + 4 * k))
                nc.vector.tensor_scalar((qT, kT)[which][a % 2][0:HD, :], bank[which][0:HD, :],
                                        (HD ** -0.5, 1.0)[which], None, ALU.mult).then_inc(st.headT_out.sem, 1)

            def softplus(k, j):
                if reached(k, j, 0):
                    t = sp_[j // 4 % 2][j % 4]
                    dve.wait_ge(sem["soft"], 2 * j + 2 + 16 * k)
                    nc.vector.tensor_tensor(t, bank[2 + j % 4][:, 0:P * (j % 4 + 1)], t,
                                            ALU.max).then_inc(sem["sp"], 1)

            def weigh(k, a):
                if reached(k, a, 0):
                    dve.wait_ge(sem["s_out"], a + 1 + 2 * k)
                    y = gate[:, :, ds((2 * k + a) * HD, HD)]
                    nc.vector.tensor_tensor(y, bank[6 + a % 2][:, 0:MB * HD].rearrange("p (m d) -> p m d", m=MB), y,
                                            ALU.mult).then_inc(sem["s_y"], 1)

            def emit(k, last):
                if isinstance(k, int) and k == 0:
                    collect(0, 0, 0)
                    collect(0, 0, 1)
                for j in range(8):
                    u = j % 4
                    dve.wait_ge(sem["z"], j + 1 + 8 * k)
                    nc.vector.tensor_scalar(sp_[j // 4][u], bank[2 + u][:, 0:P * (u + 1)], SOFT_MAX, None,
                                            ALU.min).then_inc(sem["z_min"], 1)
                    softplus(k, j - 1)
                    if u in (2, 3) and not (last and j >= 4):
                        collect(k, j // 4 + 1, u - 2)
                    if u == 3:
                        weigh(k, j // 4 - 1)
                if last:
                    softplus(k, 7)
                    weigh(k, 1)
            turns(dve, C_H // 2, emit)

        def gates_act(act):
            S = pC_gate

            def sigmoid(n):
                t = g_tmp[n % MB]
                act.wait_ge(sem["g_biased"], n + 1)
                nc.scalar.activation(t, t, ACT.Sigmoid).then_inc(sem["g_sig"], 1)

            def take(k, s, g):
                n = s * MB + g
                if n >= MB:
                    act.wait_ge(sem["g_done"], n - MB + 1)
                nc.scalar.activation(g_tmp[g], bank_of(S, s, g)[:, :], ACT.Copy).then_inc(S.evac.sem, 1)
                if n:
                    sigmoid(n - 1)
            project_act(act, S, take)
            sigmoid(4 * MB - 1)

        def gates_dve(dve):
            S = pC_gate
            dve.wait_ge(row_in.sem, 64)

            def merge(n):
                c, m = n // MB, n % MB
                t = g_tmp[m]
                y = y_ssd[:, m, c % 2 * 512:c % 2 * 512 + 512]
                dve.wait_ge(sem["g_sig"], n + 1)
                if c < 2:
                    nc.vector.tensor_tensor(y, y, t, ALU.mult).then_inc(sem["g_done"], 1)
                else:
                    nc.vector.tensor_tensor(t, y_sb[:, m, c % 2 * 512:c % 2 * 512 + 512], t,
                                            ALU.mult).then_inc(sem["g_merge"], 1)
                    dve.wait_ge(sem["g_merge"], n - 2 * MB + 1)
                    nc.vector.tensor_tensor(y, y, t, ALU.add).then_inc(sem["g_done"], 1)
            dve.wait_ge(*pC_sb.evac(2 * MB))
            for n in range(4 * MB):
                c, m = n // MB, n % MB
                dve.wait_ge(*S.evac(n + 1))
                nc.vector.tensor_tensor(g_tmp[m], g_tmp[m], b_gate[:, c * 512:(c + 1) * 512],
                                        ALU.add).then_inc(sem["g_biased"], 1)
                if n:
                    merge(n - 1)
            merge(4 * MB - 1)
            dve.wait_ge(sem["g_done"], 4 * MB)

        block = ctx.enter_context(nc.Block())

        @block.sync
        def _(sp):
            for m in range(MB):
                sp.dma_start(h[:, m, :], i["x"][0, m * P:(m + 1) * P, :]).then_inc(loaded_x.sem, 16)
            sp.dma_start(mem_in, i["mem"][0].rearrange("(m p) d -> p m d", p=P)).then_inc(loaded_x.sem, 16)
            for S in (pA_lat, pA_qm, pA_gate, *p_mem, pA_q, pA_kv, pA_out, pB_qkv, pB_f, pB_qm, pB_gate,
                      pB_out, pC_x, pC_dt, pC_z, pC_ssd, pC_qkv, pC_zs, pC_sb, pC_gate, pC_out):
                project_sp(sp, S)
            for m in range(MB):
                sp.wait_ge(*post[2].add(m + 1))
                sp.dma_start(out[0, m * P:(m + 1) * P, :], h[:, m, :]).then_inc(stored.sem, 16)
            sp.wait_ge(stored.sem, 16 * MB)

        @block.gpsimd
        def _(pool):
            link = chain(pool, "pool_self")
            for t, v in ((ident, 0.0), (tri_le, 1.0), (tri_gt, 1.0), (neg_ge, -1.0), (ident_b, 0.0),
                         (later_keys, 0.0), (not_before, 0.0)):
                link(nc.gpsimd.memset(t[:, :], v))
            nc.gpsimd.memset(ones[:, :], 1.0)
            nc.gpsimd.memset(neg_ones[:, :], -1.0)
            nc.gpsimd.memset(eps_t[:, :], EPS)
            nc.gpsimd.memset(one_t[:, :], 1.0)
            for j in range(HALF):
                nc.gpsimd.memset(inv[:, j:j + 1], float(np.float32(ROPE_THETA ** (-j / HALF))))
            for t, cmp, fill, base, step, chan in (
                    (ident, ALU.not_equal, 1.0, 0, -1, 1), (tri_le, ALU.is_ge, 0.0, 0, 1, -1),
                    (tri_gt, ALU.is_ge, 0.0, -1, -1, 1), (neg_ge, ALU.is_ge, 0.0, 0, -1, 1),
                    (ident_b, ALU.not_equal, 1.0, 0, -1, 1),
                    (later_keys, ALU.is_ge, MASKED, 0, -1, 1), (not_before, ALU.is_ge, MASKED, -1, 1, -1)):
                ins = nc.gpsimd.affine_select(out=t[:, :], in_=t[:, :], pattern=[[step, P]], compare_op=cmp,
                                              fill=fill, base=base, channel_multiplier=chan)
            ins.then_inc(consts.sem, 1)

            for p in range(2):
                pool.wait_ge(w_high.sem, p + 1)
                rest(p, pieces[p][0] * pieces[p][1])
            for S in (pA_lat, pA_qm, pA_gate, *p_mem, pA_q, pA_kv):
                project_pool(pool, S)
            pool.wait_ge(*pA_kv.evac(3 * MB))
            pool.wait_ge(sem["kr_done"], 1)
            for a in range(2):
                link(nc.gpsimd.tensor_copy(k_in[a][:, :, NOPE:QK_A], k_rot))
            pool.wait_ge(sem["rope_done"], 1)
            attend_pool(pool, attA)
            pool.wait_ge(*p_mem[1].evac(MEMB))
            pool.wait_ge(*pA_qm.evac(MB))
            pool.wait_ge(*attA.headT(2 * A_H))
            attend_pool(pool, attAm)
            pool.dma_start(row[:, :], i["norm_post"][0:1, :].partition_broadcast(P)).then_inc(row_in.sem, 16)
            project_pool(pool, pA_out)
            post_pool(pool, post[0])
            for S in (pB_qkv, pB_f, pB_qm, pB_gate):
                project_pool(pool, S)

            pool.wait_ge(*attAm.headT(2 * MEM_H))
            for a in range(2):
                nc.gpsimd.memset(q_in[a][:, :, HD:HD + 1], HD ** 0.5)
                link(nc.gpsimd.memset(k_in[a][:, :, HD + 1:HD + 2], 1.0))
            pool.wait_ge(*pB_qkv.evac(6 * MB))
            pool.wait_ge(sem["sums_out"], 2)
            attend_pool(pool, attB)
            pool.wait_ge(*pB_qm.evac(MB))
            pool.wait_ge(*attB.headT(2 * B_H))
            attend_pool(pool, attBm)
            project_pool(pool, pB_out)
            pool.wait_ge(*post[0].out(3 * MB))
            pool.dma_start(row[:, :], i["norm_post"][1:2, :].partition_broadcast(P)).then_inc(row_in.sem, 16)
            post_pool(pool, post[1])

            project_pool(pool, pC_x)
            project_pool(pool, pC_dt)
            ssd_pool(pool, link)
            for S in (pC_z, pC_ssd, pC_qkv, pC_zs):
                project_pool(pool, S)
            stick_pool(pool)
            pool.wait_ge(sem["s_out"], C_H)
            pool.dma_start(b_gate, i["b_gate_2"].partition_broadcast(P)).then_inc(row_in.sem, 16)
            pool.dma_start(row[:, :], i["norm_post_2"].partition_broadcast(P)).then_inc(row_in.sem, 16)
            for S in (pC_sb, pC_gate, pC_out):
                project_pool(pool, S)
            post_pool(pool, post[2])

        @block.scalar
        def _(act):
            def feature_major(name, n, at):
                act.dma_start(gains[:, at:at + n], name.rearrange("(c p) -> p c", p=P)).then_inc(params.sem, 16)

            with nc.allow_non_contiguous_dma("a few parameters, once"):
                act.dma_start(pos_i[:, :], i["positions"].rearrange("o (m p) -> p (o m)", p=P)).then_inc(params.sem, 16)
                feature_major(i["norm_pre"][0], KD, G_PRE[0])
                feature_major(i["mem_norm"], KD, G_MEM)
                feature_major(i["q_norm_a"][0], 3, G_Q)
                feature_major(i["kv_norm_a"][0], 2, G_KV)
                feature_major(i["norm_pre"][1], KD, G_PRE[1])
                feature_major(i["norm_pre_2"][0], KD, G_PRE[2])
                feature_major(i["ssd_norm_2"][0], KD, G_SSD)
                for t in range(TAPS):
                    act.dma_start(conv_k[:, t, :], i["conv_w_2"][0, t].rearrange("(c p) -> p c", p=P)).then_inc(params.sem, 16)
                act.dma_start(conv_b[:, :], i["conv_b_2"][0].rearrange("(c p) -> p c", p=P)).then_inc(params.sem, 16)
                for n, r in (("b_f", bf_row), ("dt_bias_2", dtb_row), ("a_log_2", alog_row), ("d_skip_2", dskip_row)):
                    act.dma_start(r, i[n].partition_broadcast(P)).then_inc(params.sem, 16)
            act.wait_ge(consts.sem, 1)
            act.wait_ge(params.sem, 16 * 17)
            for p in range(2):
                high_part(act, p, pieces[p][0] * pieces[p][1])
            norm_act(act, pre[0], lambda m: (loaded_x.sem, 16 * (MB + 1)))
            norm_act(act, pre_mem)
            act.wait_ge(sem["rope_ang"], 1)
            nc.scalar.activation(trig, turned, ACT.Sin).then_inc(sem["rope_trig"], 1)
            project_act(act, pA_lat)
            project_act(act, pA_qm)
            project_act(act, pA_gate)
            norm_act(act, latent)
            for S in (*p_mem, pA_q, pA_kv):
                project_act(act, S)
            attend_act(act, attA)
            attend_act(act, attAm)
            project_act(act, pA_out)
            post_act(act, post[0], pA_out, latent.sq(2 * MB))
            norm_act(act, pre[1], lambda m: post[0].add(m + 1))
            project_act(act, pB_qkv)
            project_act(act, pB_f)
            act.wait_ge(sem["gates_in"], 1)
            nc.scalar.activation(b_t, b_t, ACT.Exp).then_inc(sem["gates_exp"], 1)
            act.wait_ge(sem["gates_exp"], 1)
            nc.scalar.activation(b_t, b_t, ACT.Ln, bias=one_t[:, :]).then_inc(sem["gates_log"], 1)
            project_act(act, pB_qm)
            project_act(act, pB_gate)
            attend_act(act, attB)
            attend_act(act, attBm)
            project_act(act, pB_out)
            post_act(act, post[1], pB_out, pre[1].sq(MB))
            norm_act(act, pre[2], lambda m: post[1].add(m + 1))
            ssd_act(act)
            project_act(act, pC_qkv)
            project_act(act, pC_zs)
            stick_act(act)
            norm_act(act, pre_gate)
            project_act(act, pC_sb)
            gates_act(act)
            project_act(act, pC_out)
            post_act(act, post[2], pC_out, pre_gate.sq(MB))

        @block.vector
        def _(dve):
            link = chain(dve, "dve_self")
            dve.wait_ge(params.sem, 16 * 17)
            dve.wait_ge(consts.sem, 1)
            link(nc.vector.tensor_copy(pos_f[:, :], pos_i[:, :]))
            link(nc.vector.tensor_tensor(trig[:, 0], pos_f[:, :].unsqueeze(2).to_broadcast([P, MB, HALF]),
                                         inv[:, :].unsqueeze(1).to_broadcast([P, MB, HALF]), ALU.mult))
            rounder = 1.5 * 2.0 ** 23
            for n in range(2):
                link(nc.vector.tensor_scalar(turns_n[:, n], trig[:, 0], float(1 / (2 * np.pi)), 0.25 * n, ALU.mult, ALU.add))
                link(nc.vector.tensor_scalar(turns_n[:, n], turns_n[:, n], rounder, None, ALU.add))
                link(nc.vector.tensor_scalar(turns_n[:, n], turns_n[:, n], rounder, None, ALU.subtract))
                src = trig[:, 0]
                two_pi = 2 * np.pi
                c1 = 6.28125
                c2 = float(np.float32(np.round((two_pi - c1) * 2 ** 20) / 2 ** 20))
                c3 = float(two_pi - c1 - c2)
                for c in (c1, c2, c3):
                    link(nc.vector.scalar_tensor_tensor(turned[:, n], turns_n[:, n], -c, src, ALU.mult, ALU.add))
                    src = turned[:, n]
                if n:
                    link(nc.vector.tensor_scalar(turned[:, n], turned[:, n], float(np.pi / 2), None, ALU.add))
                pi_ = float(np.nextafter(np.float32(np.pi), np.float32(0)))
                link(nc.vector.tensor_scalar(turned[:, n], turned[:, n], pi_, -pi_, ALU.min, ALU.max))
            nc.vector.tensor_copy(done_t[:, :], pos_f[:, 0:1]).then_inc(sem["rope_ang"], 1)
            norm_dve(dve, pre[0])
            norm_dve(dve, pre_mem)

            def rotate(x1, x2, y1, y2, c, s, t):
                for n, (x, f) in enumerate(((x1, c), (x2, s), (x2, c), (x1, s))):
                    ins = nc.vector.tensor_tensor(t[n], x, f, ALU.mult)
                link(ins)
                nc.vector.tensor_tensor(y1, t[0], t[1], ALU.subtract)
                return nc.vector.tensor_tensor(y2, t[2], t[3], ALU.add)

            dve.wait_ge(sem["rope_trig"], 1)
            dve.wait_ge(*pA_lat.evac(2 * MB))
            kr = Q_LORA + KV_LORA
            rotate(lat[:, :, kr:kr + HALF], lat[:, :, kr + HALF:kr + ROPE], k_rot[:, :, 0:HALF],
                   k_rot[:, :, HALF:ROPE], trig[:, 1], trig[:, 0], rot_k).then_inc(sem["kr_done"], 1)
            norm_dve(dve, latent)
            dve.wait_ge(*pA_q.evac(3 * MB))
            for m in range(MB):
                v = a_q[:, m, :].rearrange("p (h c) -> p h c", c=QK_A)
                x1, x2 = v[:, :, NOPE:NOPE + HALF], v[:, :, NOPE + HALF:QK_A]
                b = [trig[:, n, m, :].unsqueeze(1).to_broadcast([P, A_H, HALF]) for n in (1, 0)]
                ins = rotate(x1, x2, x1, x2, b[0], b[1], [t[:, m * A_H:(m + 1) * A_H, :] for t in rot])
            ins.then_inc(sem["rope_done"], 1)
            attend_dve(dve, attA)
            attend_dve(dve, attAm)
            norm_dve(dve, ytA)
            post_dve(dve, post[0], (row_in.sem, 16))
            norm_dve(dve, pre[1])
            dve.wait_ge(*pB_f.evac(MB))
            link(nc.vector.tensor_tensor(b_f, b_f, bf_row.unsqueeze(1).to_broadcast([P, MB, B_H]), ALU.add))
            nc.vector.scalar_tensor_tensor(b_t, b_f, -1.0, b_f, ALU.mult, ALU.min).then_inc(sem["gates_in"], 1)
            dve.wait_ge(sem["gates_log"], 1)
            nc.vector.scalar_tensor_tensor(b_u, b_f, 0.0, b_t, ALU.min, ALU.subtract).then_inc(sem["gates_in"], 1)
            dve.wait_ge(sem["sums"], 1)
            f_sum = bank[7][:, 0:MB * B_H].rearrange("p (m h) -> p m h", m=MB)
            nc.vector.tensor_scalar(b_F, f_sum, -1.0, None, ALU.mult).then_inc(sem["sums_out"], 1)
            nc.vector.tensor_scalar(b_8F, f_sum, HD ** 0.5, None, ALU.mult).then_inc(sem["sums_out"], 1)
            attend_dve(dve, attB)
            attend_dve(dve, attBm)
            norm_dve(dve, ytB)
            post_dve(dve, post[1], (row_in.sem, 32))
            norm_dve(dve, pre[2])
            ssd_dve(dve, link)
            stick_dve(dve)
            norm_dve(dve, ytC)
            norm_dve(dve, pre_gate)
            gates_dve(dve)
            norm_dve(dve, ytM)
            post_dve(dve, post[2], (row_in.sem, 64))

        @block.tensor
        def _(pe):
            pe.wait_ge(consts.sem, 1)
            norm_pe(pe, pre[0])
            pe.wait_ge(*pre[0].normed(2 * MB))
            project_pe(pe, pA_lat)
            project_pe(pe, pA_qm)
            project_pe(pe, pA_gate)
            pe.wait_ge(*pA_gate.evac(2 * MB))
            norm_pe(pe, pre_mem)
            pe.wait_ge(*pre_mem.normed(2 * MEMB))
            for S in p_mem:
                project_pe(pe, S)
            pe.wait_ge(*p_mem[1].evac(MEMB))
            norm_pe(pe, latent)
            pe.wait_ge(*latent.normed(2 * MB))
            project_pe(pe, pA_q)
            project_pe(pe, pA_kv)
            pe.wait_ge(*pA_kv.evac(3 * MB))
            attend_pe(pe, attA)
            pe.wait_ge(*attA.weighed(4 * A_H))
            attend_pe(pe, attAm)
            pe.wait_ge(*attAm.weighed(4 * MEM_H))
            norm_pe(pe, ytA)
            pe.wait_ge(*ytA.normed(2 * MB))
            project_pe(pe, pA_out)
            norm_pe(pe, pre[1])
            pe.wait_ge(*pre[1].normed(2 * MB))
            project_pe(pe, pB_qkv)
            project_pe(pe, pB_f)
            project_pe(pe, pB_qm)
            project_pe(pe, pB_gate)
            pe.wait_ge(*pB_gate.evac(2 * MB))
            pe.wait_ge(sem["gates_in"], 2)
            for m in range(MB):
                to = bank[7][:, m * B_H:(m + 1) * B_H]
                for c in range(m + 1):
                    mm = nc.tensor.matmul(to, (tri_le if c == m else ones)[:, :], b_u[:, c, :],
                                          start=c == 0, stop=c == m)
            mm.then_inc(sem["sums"], 1)
            pe.wait_ge(sem["sums_out"], 2)
            attend_pe(pe, attB)
            pe.wait_ge(*attB.weighed(4 * B_H))
            attend_pe(pe, attBm)
            pe.wait_ge(*attBm.weighed(4 * MEM_H))
            norm_pe(pe, ytB)
            pe.wait_ge(*ytB.normed(2 * MB))
            project_pe(pe, pB_out)
            norm_pe(pe, pre[2])
            pe.wait_ge(*pre[2].normed(2 * MB))
            ssd_pe(pe)
            project_pe(pe, pC_qkv)
            project_pe(pe, pC_zs)
            pe.wait_ge(*pC_zs.evac(2 * MB))
            stick_pe(pe)
            pe.wait_ge(sem["s_y"], C_H)
            norm_pe(pe, ytC)
            pe.wait_ge(*ytC.normed(2 * MB))
            project_pe(pe, pC_sb)
            pe.wait_ge(*pC_sb.evac(2 * MB))
            norm_pe(pe, pre_gate)
            pe.wait_ge(*pre_gate.normed(2 * MB))
            project_pe(pe, pC_gate)
            pe.wait_ge(sem["g_done"], 4 * MB)
            norm_pe(pe, ytM)
            pe.wait_ge(*ytM.normed(2 * MB))
            project_pe(pe, pC_out)


def kernel(**inputs):
    import concourse.bacc as bacc
    from concourse.bass_utils import run_bass_kernel_spmd

    nc = bacc.Bacc("TRN2", target_bir_lowering=False, num_devices=1)
    arrays, args = {}, {}
    for name, value in inputs.items():
        a = np.ascontiguousarray(value)
        arrays[f"in_{name}"] = a
        args[name] = nc.dram_tensor(f"in_{name}", a.shape, mybir.dt.from_np(a.dtype), kind="ExternalInput").ap()
    out = nc.dram_tensor("out_0", (1, T, D), F32, kind="ExternalOutput").ap()
    build(nc, args, out)
    r = run_bass_kernel_spmd(nc, [arrays], core_ids=[0])
    return r.results[0]["out_0"]
```

```python
from contextlib import ExitStack

import numpy as np
import concourse.bass as bass
from concourse import mybir

P = 128
F32 = mybir.dt.float32
I32 = mybir.dt.int32
BF16 = mybir.dt.bfloat16
F32R = mybir.dt.float32r
ALU = mybir.AluOpType
ACT = mybir.ActivationFunctionType
AX = mybir.AxisListType
ds = bass.ds

D = 1024
T = 512
MB = T // P
KD = D // P
N_MEM = 256
MEMB = N_MEM // P
MEM_W, MAIN_W = D // 4, D - D // 4
HD = 64
MEM_H, A_H, B_H = MEM_W // HD, MAIN_W // HD, MAIN_W // HD
NOPE, ROPE = 64, 32
QK_A = NOPE + ROPE
HALF = ROPE // 2
Q_LORA, KV_LORA = 384, 256
LAT = Q_LORA + KV_LORA + ROPE
EPS = 1e-6
MASKED = -1e30
C_H, C_G, C_N, TAPS = 16, 2, 128, 4
INNER = C_H * HD
CONV = INNER + 2 * C_G * C_N
CONVC = CONV // P
XC = INNER // P
GH = C_H // C_G
ROPE_THETA = 10000.0
ARENA = 27136
PIECE = 1024
RAW = 4
SOFT_MAX = 40.0


class Count:

    def __init__(self, sem):
        self.sem, self.total = sem, 0

    def take(self, n):
        mark = Mark(self.sem, self.total)
        self.total += n
        return mark


class Mark:

    def __init__(self, sem, base):
        self.sem, self.base = sem, base

    def __call__(self, n):
        return self.sem, n + self.base


class Projection:

    def __init__(self, n, groups, width, pieces, piece0, before, src, product, dst, func, loop, w, c0,
                 parity, banks_free, evac):
        self.n = n
        self.groups = groups
        self.width = width
        self.pieces = pieces
        self.piece0 = piece0
        self.before = before
        self.turn = (2 if loop else n) * len(pieces)
        self.src = src
        self.product = product
        self.dst = dst
        self.func = func
        self.loop = loop
        self.w = w
        self.c0 = c0
        self.parity = parity
        self.banks_free = banks_free
        self.evac = evac

    def done_after(self, k, q, g):
        return self.before + self.groups * q + g + 1 + self.groups * self.turn * k

    def done(self, k, s, g):
        return self.done_after(k, len(self.pieces) * (s + 1) - 1, g)


class Norm:

    def __init__(self, free, gain_in, high_act, src, blocks, norms, parts, gain, stat, sq, root, rinv, scaled, turned, normed):
        self.free = free
        self.gain_in = gain_in
        self.high_act = high_act
        self.src = src
        self.blocks = blocks
        self.norms = norms
        self.parts = parts
        self.gain = gain
        self.stat = stat
        self.sq = sq
        self.root = root
        self.rinv = rinv
        self.scaled = scaled
        self.turned = turned
        self.normed = normed


class PostNorm:

    def __init__(self, sq, sum, root, out, add):
        self.sq = sq
        self.sum = sum
        self.root = root
        self.out = out
        self.add = add


class Attend:

    def __init__(self, heads, width, keys, causal, scale, q, k, v, y0, extra_q, extra_k, staged, headT,
                 headT_out, scores, neg_max, exped, probT, probT_out, attended, weighed):
        self.heads = heads
        self.width = width
        self.keys = keys
        self.causal = causal
        self.scale = scale
        self.q = q
        self.k = k
        self.v = v
        self.y0 = y0
        self.extra_q = extra_q
        self.extra_k = extra_k
        self.staged = staged
        self.headT = headT
        self.headT_out = headT_out
        self.scores = scores
        self.neg_max = neg_max
        self.exped = exped
        self.probT = probT
        self.probT_out = probT_out
        self.attended = attended
        self.weighed = weighed


class Staging:

    def __init__(self, staged, headT, headT_out):
        self.staged = staged
        self.headT = headT
        self.headT_out = headT_out


def reached(k, n, least):
    return not isinstance(k, int) or k > 0 or n >= least


def turns(eng, n, emit):
    emit(0, False)
    if n > 2:
        with eng.Fori(1, n - 1) as k:
            emit(k, False)
    if n > 1:
        emit(n - 1, True)


def build(nc, i, out):
    ctx = ExitStack()
    with ctx:
        def sb(name, shape, dt=F32):
            return ctx.enter_context(nc.sbuf_tensor(name, shape, dt))

        def count(name):
            return Count(ctx.enter_context(nc.semaphore(name)))

        bank = [ctx.enter_context(nc.psum_tensor(f"bank{n}", [P, 512], F32)) for n in range(8)]

        h = sb("h", [P, MB, D])
        acts_hi, acts_lo = (sb(n, [P, KD, T], F32R) for n in ("acts_hi", "acts_lo"))
        w_hi = [sb(f"w_hi{n}", [P, PIECE], F32R) for n in range(2)]
        w_lo = [sb(f"w_lo{n}", [P, PIECE], F32R) for n in range(2)]
        w_raw = [sb(f"w_raw{n}", [P, PIECE]) for n in range(RAW)]
        hn = sb("hn", [P, 2, D])
        junk = sb("junk", [P, D])
        row = sb("row", [P, D])
        ident, tri_le, tri_gt, ones = (sb(n, [P, P]) for n in ("ident", "tri_le", "tri_gt", "ones"))
        neg_ge, neg_ones = (sb(n, [P, P]) for n in ("neg_ge", "neg_ones"))
        ident_b, later_keys, not_before = (sb(n, [P, P], BF16) for n in ("ident_b", "later_keys", "not_before"))
        conv_k = sb("conv_k", [P, TAPS, CONVC])
        conv_b = sb("conv_b", [P, CONVC])
        small = sb("small", [P, 64])
        eps_t = sb("eps_t", [P, 1])
        one_t = sb("one_t", [P, 1])
        stat = sb("stat", [P, 40])
        norm_stat = sb("norm_stat", [P, 3, 24])
        inv = sb("inv", [P, HALF])
        pos_i = sb("pos_i", [P, MB], I32)
        pos_f = sb("pos_f", [P, MB])
        done_t = sb("done_t", [P, 1])
        arena = sb("arena", [P, ARENA])

        def view(flat, at, *shape):
            v = flat[:, at:at + int(np.prod(shape))]
            if len(shape) == 2:
                return v.rearrange("p (a b) -> p a b", a=shape[0])
            if len(shape) == 3:
                return v.rearrange("p (a b c) -> p a b c", a=shape[0], b=shape[1])
            return v

        def cut(at, *shape):
            assert at + int(np.prod(shape)) <= ARENA, (at, shape)
            return view(arena, at, *shape)

        q_in = [cut(a * 384, MB, QK_A) for a in range(2)]
        k_in = [cut(768 + a * 384, MB, QK_A) for a in range(2)]
        qT = [cut(1536 + a * 512, T) for a in range(2)]
        kT = [cut(2560 + a * 512, T) for a in range(2)]
        probs = [cut(3584 + a * 512, T) for a in range(4)]
        probsT = [cut(5632 + a * 512, T) for a in range(2)]
        W0 = 6656
        gate = cut(W0, MB, D)
        L0 = W0 + MB * D
        memkv = cut(ARENA - 2048, 2, MEMB, 2 * MEM_W)
        q_mem = cut(ARENA - 3072, MB, MEM_W)
        trig = cut(L0, 2, MB, HALF)
        turns_n = cut(L0 + 128, 2, MB, HALF)
        turned = cut(L0 + 256, 2, MB, HALF)
        k_rot = cut(L0 + 640, MB, ROPE)
        rot_k = [cut(L0 + 384 + n * 64, MB, HALF) for n in range(4)]
        a_q = cut(L0 + 2560, MB, A_H * QK_A)
        a_kv = cut(L0 + 2560 + 4608, MB, A_H * 2 * HD)
        rot = [cut(3584 + n * 768, MB * A_H, HALF) for n in range(4)]
        mem_in = cut(L0 + 2560, MEMB, D)
        lat = cut(L0 + 2560 + 4608, MB, LAT)
        b_qkv = cut(L0, MB, 3 * MAIN_W)
        b_f, b_F, b_8F, b_t, b_u = (cut(L0 + 9216 + n * 48, MB, B_H) for n in range(5))
        x_in = [cut(11264 + n * 516, 516) for n in range(2)]
        acc = [cut(11264 + 1032 + n * 512, T) for n in range(2)]
        xcT = cut(0, CONVC, T)
        c_xd = cut(0, MB, D)
        c_x = cut(6144, MB, D)
        c_xdt = cut(10240, MB, D)
        c_y = cut(14336, MB, D)
        c_B = cut(18432, C_G, MB, C_N)
        c_sc = cut(19456, C_G, MB, P)
        prev = cut(20480, MB - 1, D)
        c_dt, c_u, dtA, acs, tot, eacs, etot, eend = (cut(23552 + n * 64, MB, C_H) for n in range(8))
        segD = [cut(24064 + n * 512, MB, P) for n in range(2)]
        att = [cut(25088 + n * 512, MB, P) for n in range(2)]
        off = cut(26112, T)
        a_neg = sb("a_neg", [P, C_H])
        s_qkv = cut(L0, MB, 3 * D)
        y_ssd = cut(L0 + 3 * MB * D, MB, D)
        y_sb = gate
        b_gate = cut(L0, 2 * D)
        g_tmp = [cut(L0 + 2048 + n * 512, T) for n in range(4)]

        G_PRE = [cut(at, D) for at in (0, 14336, 14336)]
        G_MEM, G_LAT, G_SSD = cut(1024, D), cut(2048, Q_LORA + KV_LORA), cut(24064, D)
        G_QKV, G_GATE = cut(11264, D), cut(L0 + 4096, D)
        bf_row, dtb_row = small[:, 0:B_H], small[:, 12:28]
        alog_row, dskip_row = small[:, 28:44], small[:, 44:60]

        loaded_x = [count(f"loaded_x{m}") for m in range(MB)]
        loaded_mem = count("loaded_mem")
        params_first = count("params_first")
        params = count("params")
        row_in = count("row_in")
        gain_in = count("gain_in")
        gain_first = count("gain_first")
        w_in = [count(f"w_in{n}") for n in range(RAW)]
        w_high, w_rest = count("w_high"), count("w_rest")
        consts = count("consts")
        stored = count("stored")
        C = {n: count(n) for n in (
            "product", "evac", "sq", "root", "rinv", "scaled", "turned", "high_act", "normed",
            "post_sq", "post_sum", "post_root", "post_out", "post_add",
            "staged", "headT", "headT_out", "scores", "neg_max", "exped", "probT",
            "probT_out", "attended", "weighed")}

        pieces = []
        products = [0]
        last_bank = [0, 0]

        def project(w, c0, width, n, groups, product, dst, func=ACT.Copy, loop=False, evac=True):
            rows = w.shape[0] // P
            kp = min(rows, PIECE // width)
            of_chunk = [(r, min(kp, rows - r)) for r in range(0, rows, kp)]
            piece0, before = len(pieces), products[0]
            for c in range(n):
                pieces.extend((width, r) for _, r in of_chunk)
            products[0] += n * groups * len(of_chunk)
            parity = 1 - last_bank[0] if evac else 0
            banks_free = C["evac"].total - last_bank[1] if evac else C["evac"].total
            last_bank[:] = [(parity + n - 1) % 2, groups if evac else 0]
            return Projection(n=n, groups=groups, width=width, pieces=of_chunk, piece0=piece0, before=before,
                              src=None, product=product, dst=dst, func=func, loop=loop, w=w, c0=c0, parity=parity,
                              banks_free=banks_free, evac=C["evac"].take(n * groups) if evac else None)

        def chunk_turns(eng, S, emit):
            def both(k, last):
                emit(k, 0)
                emit(k, 1)
            if S.loop:
                assert S.n % 2 == 0 and S.turn % RAW == 0
                turns(eng, S.n // 2, both)
            else:
                for c in range(S.n):
                    emit(0, c)

        def bank_of(S, s, g):
            return bank[4 * ((S.parity + s) % 2) + g]

        def tokens_by(k0=0):
            def product(x, w, kk, g):
                return x[:, k0 + kk, g * P:(g + 1) * P], w
            return product

        def by_tokens(x, w, kk, g):
            return w[:, g * P:(g + 1) * P], x[:, kk, :]

        def to_columns(dst, c0=0):
            def place(S, k, s, g):
                return dst[:, g, ds((2 * k + s) * S.width + c0, S.width)]
            return place

        def project_sp(sp, S):
            def emit(k, s):
                for j, (r0, r) in enumerate(S.pieces):
                    q = s * len(S.pieces) + j
                    p = S.piece0 + q
                    if p >= RAW or not isinstance(k, int) or k:
                        sp.wait_ge(w_rest.sem, p - RAW + 1 + S.turn * k)
                    src = S.w.rearrange("(k p) n -> p k n", p=P)[:, r0:r0 + r, ds(S.c0 + (2 * k + s) * S.width, S.width)]
                    sp.dma_start(w_raw[p % RAW][:, 0:r * S.width].rearrange("p (k n) -> p k n", k=r),
                                 src).then_inc(w_in[p % RAW].sem, 16)
            chunk_turns(sp, S, emit)

        def piece_size(S, k, q):
            if isinstance(k, int):
                p = S.piece0 + S.turn * k + q
                return pieces[p][0] * pieces[p][1] if p < len(pieces) else 0
            return S.width * S.pieces[q % len(S.pieces)][1]

        def high_part(act, p, size, more=0):
            act.wait_ge(w_in[p % RAW].sem, 16 * (p // RAW + 1) + more)
            nc.scalar.activation(w_hi[p % 2][:, 0:size], w_raw[p % RAW][:, 0:size], ACT.Copy).then_inc(w_high.sem, 1)

        def rest(p, size):
            nc.gpsimd.tensor_tensor(w_lo[p % 2][:, 0:size], w_raw[p % RAW][:, 0:size],
                                    w_hi[p % 2][:, 0:size].bitcast(F32), ALU.subtract).then_inc(w_rest.sem, 1)

        def split_ahead_act(act, S, k, q):
            size = piece_size(S, k, q + 2)
            if size:
                act.wait_ge(C["product"].sem, S.done_after(k, q, S.groups - 1))
                high_part(act, S.piece0 + q + 2, size, S.turn // RAW * 16 * k if S.loop else 0)

        def project_pool(pool, S, early=None):
            def emit(k, s):
                for j in range(len(S.pieces)):
                    q = s * len(S.pieces) + j
                    if early and q >= S.turn - 2:
                        early(q - S.turn + 2)
                    size = piece_size(S, k, q + 2)
                    if size:
                        pool.wait_ge(w_high.sem, S.piece0 + q + 3 + S.turn * k)
                        rest(S.piece0 + q + 2, size)
            chunk_turns(pool, S, emit)

        def project_pe(pe, S, acts=None):
            if S.banks_free > 0:
                pe.wait_ge(C["evac"].sem, S.banks_free)

            def emit(k, s):
                if S.evac and (s or not isinstance(k, int) or k):
                    pe.wait_ge(*S.evac(S.groups * (s - 1 + 2 * k)))
                for j, (r0, r) in enumerate(S.pieces):
                    q = s * len(S.pieces) + j
                    p = S.piece0 + q
                    pe.wait_ge(w_rest.sem, p + 1 + S.turn * k)
                    wh, wl = (w[p % 2][:, 0:r * S.width].rearrange("p (k n) -> p k n", k=r) for w in (w_hi, w_lo))
                    for g in range(S.groups):
                        if acts and isinstance(k, int) and k == 0 and q == 0:
                            pe.wait_ge(*acts.normed((g + 1) * len(acts.parts)))
                        for kk in range(r):
                            for t, (x, w) in enumerate(((acts_hi, wh), (acts_hi, wl), (acts_lo, wh))):
                                lhs, rhs = S.product(x, w[:, kk, :], r0 + kk, g)
                                mm = nc.tensor.matmul(bank_of(S, s, g)[0:lhs.shape[1], 0:rhs.shape[1]], lhs, rhs,
                                                      start=r0 + kk + t == 0,
                                                      stop=j == len(S.pieces) - 1 and kk == r - 1 and t == 2)
                        mm.then_inc(C["product"].sem, 1)
            chunk_turns(pe, S, emit)

        def project_act(act, S, take=None, early=None):
            def emit(k, s):
                last = len(S.pieces) - 1
                for j in range(last):
                    split_ahead_act(act, S, k, s * len(S.pieces) + j)
                for g in range(S.groups if S.evac else 0):
                    act.wait_ge(C["product"].sem, S.done(k, s, g))
                    if take:
                        take(k, s, g)
                    else:
                        to = S.dst(S, k, s, g)
                        nc.scalar.activation(to, bank_of(S, s, g)[:, 0:to.shape[1]], S.func).then_inc(S.evac.sem, 1)
                if early and s == S.n - 1:
                    early()
                split_ahead_act(act, S, k, s * len(S.pieces) + last)
            chunk_turns(act, S, emit)

        norm_stages = []

        def norm_stage(src, blocks, norms, parts, gain, free=None, gain_in=None):
            nn, np_ = len(norms), len(parts)
            norm_stages.append(1)
            return Norm(free=free, gain_in=gain_in, high_act=C["high_act"].take(blocks * 2), src=src, blocks=blocks, norms=norms, parts=parts, gain=gain,
                         stat=norm_stat[:, len(norm_stages) % 3],
                         sq=C["sq"].take(blocks * nn), root=C["root"].take(blocks * nn),
                         rinv=C["rinv"].take(blocks * nn), scaled=C["scaled"].take(blocks * nn),
                         turned=C["turned"].take(blocks * np_), normed=C["normed"].take(blocks * np_))

        def wait_free(eng, N):
            if N.free:
                eng.wait_ge(C["product"].sem, N.free.done_after(0, N.free.n * len(N.free.pieces) - 1,
                                                                N.free.groups - 1))

        def round_act(act, N, m):
            if m == 0:
                wait_free(act, N)
            for p, (a, c0, n, k0, b0) in enumerate(N.parts):
                act.wait_ge(*N.turned(m * len(N.parts) + p + 1))
                nc.scalar.activation(acts_hi[:, k0:k0 + n, m * P:(m + 1) * P],
                                     bank[b0 + m][:, 0:n * P].rearrange("p (c t) -> p c t", c=n),
                                     ACT.Copy).then_inc(N.high_act.sem, 1)

        def round_all_act(act, N):
            for m in range(N.blocks):
                round_act(act, N, m)

        def norm_act(act, N, ready=None, rounds=True):
            for m in range(N.blocks + rounds):
                norm_act_step(act, N, m, ready, rounds)

        def norm_act_step(act, N, m, ready=None, rounds=True):
            if m < N.blocks:
                if ready:
                    act.wait_ge(*ready(m))
                for a, (c0, width) in enumerate(N.norms):
                    n = m * len(N.norms) + a
                    if n:
                        act.wait_ge(*N.sq(n))
                    nc.scalar.activation(junk[:, 0:width], N.src[:, m, c0:c0 + width], ACT.Square,
                                         accum_out=N.stat[:, n:n + 1]).then_inc(N.sq.sem, 1)
                    act.wait_ge(*N.sq(n + 1))
                    nc.scalar.activation(N.stat[:, 8 + n:9 + n], N.stat[:, n:n + 1], ACT.Sqrt,
                                         bias=eps_t[:, :], scale=1.0 / width).then_inc(N.root.sem, 1)
            if rounds and m:
                round_act(act, N, m - 1)

        def norm_pe(pe, N, ready=None):
            for m in range(N.blocks):
                if ready:
                    pe.wait_ge(*ready(m))
                for p, (a, c0, n, _, b0) in enumerate(N.parts):
                    if N.norms:
                        pe.wait_ge(*N.scaled(m * len(N.norms) + a + 1))
                        rows = hn[:, m % 2, :]
                    else:
                        rows = N.src[:, m, :]
                    for c in range(n):
                        mm = nc.tensor.transpose(bank[b0 + m][:, c * P:(c + 1) * P],
                                                 rows[:, c0 + c * P:c0 + (c + 1) * P], ident[:, :])
                    mm.then_inc(N.turned.sem, 1)

        def norm_dve(dve, N):
            for m in range(N.blocks + 1):
                norm_dve_step(dve, N, m)

        def norm_dve_step(dve, N, m):
            def scale(m):
                for a, (c0, width) in enumerate(N.norms):
                    n = m * len(N.norms) + a
                    dve.wait_ge(*N.root(n + 1))
                    nc.vector.reciprocal(N.stat[:, 16 + n:17 + n], N.stat[:, 8 + n:9 + n]).then_inc(N.rinv.sem, 1)
                if m >= 2:
                    dve.wait_ge(*N.turned((m - 1) * len(N.parts)))
                for a, (c0, width) in enumerate(N.norms):
                    n = m * len(N.norms) + a
                    dve.wait_ge(*N.rinv(n + 1))
                    nc.vector.scalar_tensor_tensor(hn[:, m % 2, c0:c0 + width], N.src[:, m, c0:c0 + width],
                                                   N.stat[:, 16 + n:17 + n], N.gain[:, c0:c0 + width],
                                                   ALU.mult, ALU.mult).then_inc(N.scaled.sem, 1)

            def collect(m):
                for p, (a, c0, n, k0, b0) in enumerate(N.parts):
                    dve.wait_ge(*N.turned(m * len(N.parts) + p + 1))
                    hi, lo = (t[:, k0:k0 + n, m * P:(m + 1) * P] for t in (acts_hi, acts_lo))
                    of = bank[b0 + m][:, 0:n * P].rearrange("p (c t) -> p c t", c=n)
                    dve.wait_ge(*N.high_act(m * 2 + p + 1))
                    nc.vector.tensor_tensor(lo, of, hi.bitcast(F32), ALU.subtract).then_inc(N.normed.sem, 1)

            if N.norms and m == 0:
                dve.wait_ge(*N.gain_in)
            if m < N.blocks:
                scale(m)
            if m == 1:
                wait_free(dve, N)
            if m:
                collect(m - 1)

        whole = [(0, D)]
        whole_parts = [(0, 0, 4, 0, 0), (0, 512, 4, 4, 4)]

        def post_stage():
            return PostNorm(sq=C["post_sq"].take(2 * MB), sum=C["post_sum"].take(MB),
                         root=C["post_root"].take(MB), out=C["post_out"].take(3 * MB),
                         add=C["post_add"].take(2 * MB))

        AHEAD = 1

        def post_act(act, O, S, before, N=None):
            act.wait_ge(*before)
            for m in range(MB):
                act.wait_ge(C["product"].sem, S.done(0, 1, m))
                for half in range(2):
                    n = 2 * m + half
                    if n >= 2:
                        act.wait_ge(*O.sq(n - 1))
                    nc.scalar.activation(junk[:, 512 * half:512 * half + 512], bank[4 * half + m][:, :], ACT.Square,
                                         accum_out=stat[:, 24 + n:25 + n]).then_inc(O.sq.sem, 1)
                act.wait_ge(*O.sum(m + 1))
                nc.scalar.activation(stat[:, 32 + m:33 + m], stat[:, 32 + m:33 + m], ACT.Sqrt,
                                     bias=eps_t[:, :], scale=1.0 / D).then_inc(O.root.sem, 1)
                if N and m >= AHEAD:
                    norm_act_step(act, N, m - AHEAD, lambda m: O.add(2 * m + 2))
            for m in range(MB - AHEAD, MB + 1) if N else ():
                norm_act_step(act, N, m, lambda m: O.add(2 * m + 2))

        def post_dve(dve, O, row_ready, N=None):
            dve.wait_ge(*row_ready)
            for m in range(MB):
                dve.wait_ge(*O.sq(2 * m + 2))
                nc.vector.tensor_tensor(stat[:, 32 + m:33 + m], stat[:, 24 + 2 * m:25 + 2 * m],
                                        stat[:, 25 + 2 * m:26 + 2 * m], ALU.add).then_inc(O.sum.sem, 1)
                dve.wait_ge(*O.root(m + 1))
                nc.vector.reciprocal(stat[:, 36 + m:37 + m], stat[:, 32 + m:33 + m]).then_inc(O.out.sem, 1)
                dve.wait_ge(*O.out(3 * m + 1))
                for half in range(2):
                    c0 = 512 * half
                    nc.vector.scalar_tensor_tensor(
                        gate[:, m, c0:c0 + 512], bank[4 * half + m][:, :], stat[:, 36 + m:37 + m],
                        row[:, c0:c0 + 512], ALU.mult, ALU.mult).then_inc(O.out.sem, 1)
                if N and m >= AHEAD:
                    norm_dve_step(dve, N, m - AHEAD)
            for m in range(MB - AHEAD, MB + 1) if N else ():
                norm_dve_step(dve, N, m)

        def post_pool(pool, O):
            for m in range(MB):
                for half in range(2):
                    pool.wait_ge(*O.out(3 * m + 2 + half))
                    c0 = slice(512 * half, 512 * half + 512)
                    nc.gpsimd.tensor_tensor(h[:, m, c0], h[:, m, c0], gate[:, m, c0], ALU.add).then_inc(O.add.sem, 1)

        LAG = 2

        def attend_stage(heads, width, keys, causal_, scale, q, k, v, extra_q, extra_k, y0):
            s = 4 * heads
            return Attend(heads=heads, width=width, keys=keys, causal=causal_, scale=scale, q=q, k=k,
                         v=v, y0=y0, extra_q=extra_q, extra_k=extra_k,
                         staged=C["staged"].take(2 * heads), headT=C["headT"].take(2 * heads),
                         headT_out=C["headT_out"].take(2 * heads), scores=C["scores"].take(s),
                         neg_max=C["neg_max"].take(s),
                         exped=C["exped"].take(s), probT=C["probT"].take(s),
                         probT_out=C["probT_out"].take(s), attended=C["attended"].take(s),
                         weighed=C["weighed"].take(s))

        def n_keys(A, b):
            return b + 1 if A.causal else A.keys

        def stage_head(pool, A, k, a):
            if reached(k, a, 2):
                pool.wait_ge(*A.headT(2 * a - 2 + 4 * k))
            parts_q = [A.q(k, a)] + A.extra_q(k, a)
            parts_k = [A.k(k, a)] + A.extra_k(k, a)
            for parts, buf, n in ((parts_q, q_in[a], MB), (parts_k, k_in[a], A.keys)):
                for c0, src in parts:
                    ins = nc.gpsimd.tensor_copy(buf[:, 0:n, c0:c0 + src.shape[2]], src)
                ins.then_inc(A.staged.sem, 1)

        def attend_pool(pool, A, all_there=None, staged=True):
            if all_there:
                pool.wait_ge(*all_there)

            def emit(k, last):
                for a in range(2):
                    if not (staged and isinstance(k, int) and k == 0):
                        stage_head(pool, A, k, a)
            turns(pool, A.heads // 2, emit)

        def turn_head(pe, A, k, a, which):
            pe.wait_ge(*A.staged(2 * a + which + 1 + 4 * k))
            buf, n = ((q_in, MB), (k_in, A.keys))[which]
            for b in range(n):
                mm = nc.tensor.transpose(bank[which][0:A.width, b * P:(b + 1) * P],
                                         buf[a % 2][:, b, 0:A.width], ident[:, :])
            mm.then_inc(A.headT.sem, 1)

        def enter_pe(pe, S, A):
            banks_0_to_3 = (S.parity + S.n - 1) % 2 == 0
            pe.wait_ge(*S.evac((S.n - (not banks_0_to_3)) * S.groups))
            turn_head(pe, A, 0, 0, 0)
            turn_head(pe, A, 0, 0, 1)
            pe.wait_ge(*S.evac(S.n * S.groups))

        def attend_pe(pe, A, then=None):
            def turn(k, a, which):
                turn_head(pe, A, k, a, which)

            def score(k, j):
                a, b = j // 4 % 2, j % 4
                if b == 0:
                    pe.wait_ge(*A.headT_out(2 * (j // 4) + 2 + 4 * k))
                if reached(k, j, 4):
                    pe.wait_ge(*A.exped(j - 3 + 8 * k))
                n = n_keys(A, b) * P
                mm = nc.tensor.matmul(bank[2 + b][:, 0:n], qT[a][0:A.width, b * P:(b + 1) * P],
                                 kT[a][0:A.width, 0:n], start=True, stop=not A.causal)
                if A.causal:
                    mm = nc.tensor.matmul(bank[2 + b][:, n - P:n], ident_b[:, :], later_keys[:, :],
                                          start=False, stop=True)
                mm.then_inc(A.scores.sem, 1)

            def turn_probs(k, j):
                if not reached(k, j, 0):
                    return
                b = j % 4
                pe.wait_ge(*A.exped(j + 1 + 8 * k))
                if reached(k, j, 1):
                    pe.wait_ge(*A.probT_out(j + 8 * k))
                for c in range(n_keys(A, b)):
                    mm = nc.tensor.transpose(bank[6][:, c * P:(c + 1) * P],
                                             probs[b][:, c * P:(c + 1) * P], ident[:, :])
                mm.then_inc(A.probT.sem, 1)

            def values(k, j):
                if not reached(k, j, 0):
                    return
                b = j % 4
                pe.wait_ge(*A.probT_out(j + 1 + 8 * k))
                if reached(k, j, 1):
                    pe.wait_ge(*A.weighed(j + 8 * k))
                n = n_keys(A, b)
                for c in range(n):
                    mm = nc.tensor.matmul(bank[7][:, 0:HD], probsT[j % 2][:, c * P:(c + 1) * P],
                                          A.v(k, j // 4, c), start=c == 0, stop=c == n - 1)
                mm.then_inc(A.attended.sem, 1)

            def emit(k, last):
                for j in range(8):
                    score(k, j)
                    if last and then and j >= 6:
                        turn_head(pe, then, 0, 0, j - 6)
                    if j % 4 in (0, 2) and not (last and j >= 4):
                        turn(k, j // 4 + 1, j % 4 // 2)
                    turn_probs(k, j - LAG)
                    values(k, j - LAG - 1)
                if last:
                    for j in range(8, 9 + LAG):
                        if j < 8 + LAG:
                            turn_probs(k, j - LAG)
                        values(k, j - LAG - 1)
            turns(pe, A.heads // 2, emit)

        def collect_head(act, A, k, a, which):
            n = (MB, A.keys)[which] * P
            act.wait_ge(*A.headT(2 * a + which + 1 + 4 * k))
            nc.scalar.activation((qT, kT)[which][a % 2][0:A.width, 0:n], bank[which][0:A.width, 0:n],
                                 ACT.Copy, scale=(A.scale, 1.0)[which]).then_inc(A.headT_out.sem, 1)

        def enter_act(act, A):
            collect_head(act, A, 0, 0, 0)
            collect_head(act, A, 0, 0, 1)

        def attend_act(act, A, then=None):
            def collect(k, a, which):
                collect_head(act, A, k, a, which)

            def emit(k, last):
                for j in range(8):
                    b = j % 4
                    n = n_keys(A, b) * P
                    act.wait_ge(*A.neg_max(j + 1 + 8 * k))
                    if reached(k, j, 4):
                        act.wait_ge(*A.probT(j - 3 + 8 * k))
                    nc.scalar.activation(probs[b][:, 0:n], bank[2 + b][:, 0:n], ACT.Exp,
                                         bias=stat[:, j:j + 1], accum_out=stat[:, 8 + j:9 + j]
                                         ).then_inc(A.exped.sem, 1)
                    if b in (0, 2) and not (last and j >= 4):
                        collect(k, j // 4 + 1, b // 2)
                    if last and then and j >= 6:
                        collect_head(act, then, 0, 0, j - 6)
            turns(act, A.heads // 2, emit)

        def attend_dve(dve, A):
            def maximum(k, j):
                b = j % 4
                n = n_keys(A, b) * P
                dve.wait_ge(*A.scores(j + 1 + 8 * k))
                nc.vector.tensor_reduce(stat[:, j:j + 1], bank[2 + b][:, 0:n], AX.X, ALU.max,
                                        negate=True).then_inc(A.neg_max.sem, 1)

            def collect(k, j):
                if not reached(k, j, 0):
                    return
                b = j % 4
                n = n_keys(A, b) * P
                dve.wait_ge(*A.probT(j + 1 + 8 * k))
                nc.vector.reciprocal(stat[:, 16 + j % 8:17 + j % 8], stat[:, 8 + j % 8:9 + j % 8])
                if reached(k, j, 2):
                    dve.wait_ge(*A.attended(j - 1 + 8 * k))
                nc.vector.tensor_copy(probsT[j % 2][:, 0:n], bank[6][:, 0:n]).then_inc(A.probT_out.sem, 1)

            def weigh(k, j):
                if not reached(k, j, 0):
                    return
                dve.wait_ge(*A.attended(j + 1 + 8 * k))
                y = gate[:, j % 4, ds((2 * k + j // 4) * HD + A.y0, HD)]
                nc.vector.scalar_tensor_tensor(y, bank[7][:, 0:HD], stat[:, 16 + j % 8:17 + j % 8], y,
                                               ALU.mult, ALU.mult).then_inc(A.weighed.sem, 1)

            def emit(k, last):
                for j in range(8):
                    maximum(k, j)
                    collect(k, j - LAG)
                    weigh(k, j - LAG - 1)
                if last:
                    for j in range(8, 9 + LAG):
                        if j < 8 + LAG:
                            collect(k, j - LAG)
                        weigh(k, j - LAG - 1)
            turns(dve, A.heads // 2, emit)

        def head_of(src, stride, c0=0, width=HD, at=0):
            def pick(k, a):
                return at, src[:, :, ds((2 * k + a) * stride + c0, width)]
            return pick

        def rows_of(src, stride, c0=0):
            def pick(k, a, c):
                return src[:, c, ds((2 * k + a) * stride + c0, HD)]
            return pick

        def none(k, a):
            return []

        pre = [norm_stage(h, MB, whole, whole_parts, G_PRE[0], gain_in=(params_first.sem, 16))]
        tb = tokens_by()
        pA_lat = project(i["w_in_a"][0], 0, LAT // 2, 2, MB, tb, to_columns(lat))
        pA_qm = project(i["w_in_a"][0], LAT, MEM_W, 1, MB, tb, to_columns(q_mem))
        pA_gate = project(i["w_in_a"][0], LAT + MEM_W, 512, 2, MB, tb, to_columns(gate), ACT.Silu)
        pre_mem = norm_stage(mem_in, MEMB, whole, whole_parts, G_MEM, pA_gate, (gain_first.sem, 48))

        def mem_place(layer):
            def place(S, k, s, g):
                return memkv[:, layer, g, :]
            return place

        p_mem = [project(i["w_mem_kv"][n], 0, 2 * MEM_W, 1, MEMB, tb, mem_place(n)) for n in range(2)]
        latent = norm_stage(lat, MB, [(0, Q_LORA), (Q_LORA, KV_LORA)],
                            [(0, 0, 3, 0, 0), (1, Q_LORA, 2, 3, 4)], G_LAT, p_mem[1], (gain_first.sem, 48))

        pA_q = project(i["w_q_up_a"][0], 0, 384, 3, MB, tb, to_columns(a_q))
        pA_kv = project(i["w_kv_up_a"][0], 0, 512, 3, MB, tokens_by(Q_LORA // P), to_columns(a_kv))
        attA = attend_stage(A_H, QK_A, MB, True, QK_A ** -0.5, head_of(a_q, QK_A, 0, QK_A),
                            head_of(a_kv, 2 * HD), rows_of(a_kv, 2 * HD, HD), none, none, 0)

        def mem_attend(layer):
            return attend_stage(MEM_H, HD, MEMB, False, HD ** -0.5, head_of(q_mem, HD),
                                head_of(memkv[:, layer], HD), rows_of(memkv[:, layer], HD, MEM_W),
                                none, none, MAIN_W)

        attAm = mem_attend(0)
        no_norm = [(0, 0, 4, 0, 0), (0, 512, 4, 4, 4)]
        ytA = norm_stage(gate, MB, [], no_norm, None, pA_kv)
        pA_out = project(i["w_out"][0], 0, 512, 2, MB, tb, None, evac=False)
        post = [post_stage()]

        pre.append(norm_stage(h, MB, whole, whole_parts, G_PRE[1], pA_out, (gain_in.sem, 16)))
        wb = i["w_in_b"][0]
        pB_qkv = project(wb, 0, 384, 6, MB, tb, to_columns(b_qkv), loop=True)
        pB_f = project(wb, 3 * MAIN_W, B_H, 1, MB, tb, to_columns(b_f))
        pB_qm = project(wb, 3 * MAIN_W + B_H, MEM_W, 1, MB, tb, to_columns(q_mem))
        pB_gate = project(wb, 3 * MAIN_W + B_H + MEM_W, 512, 2, MB, tb, to_columns(gate), ACT.Silu)
        sum_bank = bank_of(pB_gate, 0, MB - 1)
        attB = attend_stage(
            B_H, HD + 2, MB, True, HD ** -0.5, head_of(b_qkv, HD), head_of(b_qkv, HD, MAIN_W),
            rows_of(b_qkv, HD, 2 * MAIN_W),
            lambda k, a: [(HD + 1, b_8F[:, :, ds(2 * k + a, 1)])],
            lambda k, a: [(HD, b_F[:, :, ds(2 * k + a, 1)])], 0)
        attBm = mem_attend(1)
        ytB = norm_stage(gate, MB, [], no_norm, None, pB_gate)
        pB_out = project(i["w_out"][1], 0, 512, 2, MB, tb, None, evac=False)
        post.append(post_stage())

        pre.append(norm_stage(h, MB, whole, whole_parts, G_PRE[2], pB_out, (gain_in.sem, 32)))
        wc = i["w_in_2"][0]
        Z0, X0, DT0, Q0 = 0, INNER, INNER + CONV, INNER + CONV + C_H
        ZS0, G0 = Q0 + 3 * D, Q0 + 4 * D
        pC_x = project(wc, X0, 256, 6, 2, by_tokens, None, loop=True)
        pC_dt = project(wc, DT0, C_H, 1, MB, tb, to_columns(c_dt))
        pC_z = project(wc, Z0, 512, 2, MB, tb, to_columns(c_x), ACT.Silu)
        ssd_norm = norm_stage(c_y, MB, [(0, 512), (512, 512)], [(0, 0, 4, 0, 0), (1, 512, 4, 4, 4)], G_SSD, pC_z, (gain_in.sem, 64))
        pC_ssd = project(i["w_ssd_proj_2"][0], 0, 512, 2, MB, tb, to_columns(y_ssd))
        pre_qkv = norm_stage(h, MB, whole, whole_parts, G_QKV, pC_ssd, (gain_in.sem, 64))
        pC_qkv = project(wc, Q0, 512, 6, MB, tb, to_columns(s_qkv), loop=True)
        pC_zs = project(wc, ZS0, 512, 2, MB, tb, to_columns(gate), ACT.Silu)
        ytC = norm_stage(gate, MB, [], no_norm, None, pC_zs)
        pC_sb = project(i["w_sb_proj_2"][0], 0, 512, 2, MB, tb, to_columns(y_sb))

        pre_gate = norm_stage(h, MB, whole, whole_parts, G_GATE, pC_sb, (gain_in.sem, 80))
        pC_gate = project(wc, G0, 512, 4, MB, tb, None)
        ytM = norm_stage(y_ssd, MB, [], no_norm, None, pC_gate)
        pC_out = project(i["w_out_2"][0], 0, 512, 2, MB, tb, None, evac=False)
        post.append(post_stage())

        misc = {n: count(n) for n in (
            "pool_self", "dve_self", "act_self", "rope_ang", "rope_trig", "rope_done", "kr_done",
            "gates_in", "gates_exp", "gates_log", "sums", "sums_out",
            "conv_in", "conv_acc", "conv_out", "xT_turned", "xT_out", "ssd_dt", "ssd_sc", "ssd_sc_out",
            "ssd_seg", "ssd_seg_in", "ssd_exp", "ssd_att", "ssd_diag", "ssd_y", "ssd_state",
            "ssd_prev", "ssd_off", "ssd_off_out", "ssd_ready", "ssd_gated",
            "z", "z_min", "soft", "sp", "remain", "w_exp", "s_out", "s_y",
            "g_sig", "g_merge", "g_done")}
        started = {}
        sem = {n: c.sem for n, c in misc.items()}

        def chain(eng, name):
            def link(ins):
                misc[name].total += 1
                ins.then_inc(sem[name], 1)
                eng.wait_ge(sem[name], misc[name].total)
            return link

        XT = 2 * MB + C_G

        def conv_taps(c):
            return [conv_k[:, t, ds(c, 1)] for t in range(TAPS)]

        def ssd_act(act):
            S = pC_x

            def silu(k, n):
                act.wait_ge(sem["conv_acc"], n + 1 + 4 * k)
                nc.scalar.activation(xcT[:, ds(4 * k + n, 1), :].rearrange("p o t -> p (o t)"),
                                     acc[n % 2], ACT.Silu).then_inc(sem["conv_out"], 1)

            def take(k, s, g):
                n = s * S.groups + g
                if reached(k, n, 2):
                    act.wait_ge(sem["conv_acc"], n - 1 + 4 * k)
                nc.scalar.activation(x_in[n % 2][:, TAPS - 1:TAPS - 1 + T], bank_of(S, s, g)[:, :],
                                     ACT.Copy).then_inc(S.evac.sem, 1)
                if reached(k, n, 1):
                    silu(k, n - 1)
            act.wait_ge(*pre[2].normed(1))
            project_act(act, S, take)
            silu(S.n // 2 - 1, 3)
            project_act(act, pC_dt)
            for f in range(XT):
                act.wait_ge(sem["xT_turned"], f + 1)
                to = c_x[:, f // 2, f % 2 * 512:f % 2 * 512 + 512] if f < 2 * MB else \
                    c_B[:, f - 2 * MB].rearrange("p m n -> p (m n)")
                nc.scalar.activation(to, bank[4 + f % 4][:, :], ACT.Copy).then_inc(sem["xT_out"], 1)
            act.wait_ge(sem["ssd_dt"], 1)
            nc.scalar.activation(acs, acs, ACT.Exp).then_inc(sem["ssd_ready"], 1)
            act.wait_ge(sem["ssd_ready"], 1)
            nc.scalar.activation(acs, acs, ACT.Ln, bias=one_t[:, :]).then_inc(sem["ssd_ready"], 1)
            nc.scalar.activation(a_neg[:, :], alog_row, ACT.Exp).then_inc(sem["ssd_ready"], 1)
            act.wait_ge(sem["sums"], 2)
            nc.scalar.activation(cut(23552 + 5 * 64, 3 * MB * C_H), bank[2][:, 0:3 * MB * C_H],
                                 ACT.Exp).then_inc(sem["ssd_ready"], 1)
            for g in range(C_G):
                def emit_heads(k, last, g=g):
                    for a in range(2):
                        n = GH * g + a
                        act.wait_ge(sem["ssd_seg"], n + 1 + 2 * k)
                        if g or reached(k, a, 2):
                            act.wait_ge(sem["ssd_diag"], n - 1 + 2 * k)
                        nc.scalar.activation(att[a].rearrange("p m l -> p (m l)"), bank[4 + a][:, :],
                                             ACT.Exp).then_inc(sem["ssd_exp"], 1)
                turns(act, GH // 2, emit_heads)
            act.wait_ge(sem["ssd_y"], C_H)
            project_act(act, pC_z)
            norm_act(act, ssd_norm, lambda m: (sem["ssd_gated"], m + 1))
            norm_act(act, pre_qkv, rounds=False)
            project_act(act, pC_ssd)
            round_all_act(act, pre_qkv)

        def ssd_pe(pe):
            project_pe(pe, pC_x)
            project_pe(pe, pC_dt)
            pe.wait_ge(sem["conv_out"], CONVC)
            for f in range(XT):
                if f >= 4:
                    pe.wait_ge(sem["xT_out"], f - 3)
                for c in range(4):
                    src = xcT[:, 4 * (f % 2) + c, f // 2 * P:(f // 2 + 1) * P] if f < 2 * MB else \
                        xcT[:, XC + f - 2 * MB, c * P:(c + 1) * P]
                    mm = nc.tensor.transpose(bank[4 + f % 4][:, c * P:(c + 1) * P], src, ident[:, :])
                mm.then_inc(sem["xT_turned"], 1)
            pe.wait_ge(*pC_dt.evac(MB))
            for g in range(C_G):
                for m in range(MB):
                    mm = nc.tensor.matmul(bank[g][:, m * P:(m + 1) * P], xcT[:, XC + g, m * P:(m + 1) * P],
                                          xcT[:, XC + C_G + g, m * P:(m + 1) * P], start=True, stop=True)
                mm.then_inc(sem["ssd_sc"], 1)
            pe.wait_ge(sem["ssd_dt"], 2)
            for n, w in enumerate((tri_le, ones, tri_gt)):
                mm = nc.tensor.matmul(bank[2][:, n * 64:(n + 1) * 64], w[:, :],
                                      dtA.rearrange("p m h -> p (m h)"), start=True, stop=True)
            mm.then_inc(sem["sums"], 1)
            pe.wait_ge(sem["xT_out"], XT)
            for g in range(C_G):
                def seg(k, a, g=g):
                    n = GH * g + a
                    pe.wait_ge(sem["ssd_seg_in"], n + 1 + 2 * k)
                    if g or reached(k, a, 2):
                        pe.wait_ge(sem["ssd_exp"], n - 1 + 2 * k)
                    nc.tensor.matmul(bank[4 + a][:, :], tri_gt[:, :], segD[a].rearrange("p m l -> p (m l)"),
                                     start=True, stop=True).then_inc(sem["ssd_seg"], 1)

                def diag(k, a, g=g):
                    n = GH * g + a
                    b = a % 2
                    pe.wait_ge(sem["ssd_att"], n + 1 + 2 * k)
                    if g or reached(k, a, 2):
                        pe.wait_ge(sem["ssd_y"], n - 1 + 2 * k)
                    for m in range(MB):
                        mm = nc.tensor.matmul(bank[6 + b][:, m * HD:(m + 1) * HD], att[b][:, m, :],
                                              c_xdt[:, m, ds((n + 2 * k) * HD, HD)], start=True, stop=True)
                    mm.then_inc(sem["ssd_diag"], 1)

                def emit(k, last):
                    seg(k, 0)
                    if reached(k, 0, 1):
                        diag(k, -1)
                    seg(k, 1)
                    diag(k, 0)
                    if last:
                        diag(k, 1)
                turns(pe, GH // 2, emit)
            pe.wait_ge(sem["ssd_sc_out"], C_G)
            pe.wait_ge(sem["ssd_ready"], 5)
            for n in range(2 * (MB - 1)):
                m, g = n // 2, n % 2
                if n >= 4:
                    pe.wait_ge(sem["ssd_prev"], n - 3)
                nc.tensor.matmul(bank[n % 4][:, :], c_B[:, g, m, :], c_xd[:, m, g * 512:(g + 1) * 512],
                                 start=True, stop=True).then_inc(sem["ssd_state"], 1)
            for n in range(2 * (MB - 1)):
                m, g = n // 2 + 1, n % 2
                pe.wait_ge(sem["ssd_prev"], max(n + 1, 2 * (MB - 1)) if n < 4 else 2 * (MB - 1))
                if n >= 4:
                    pe.wait_ge(sem["ssd_off_out"], 2 * (n - 3))
                nc.tensor.matmul(bank[n % 4][:, :], xcT[:, XC + C_G + g, m * P:(m + 1) * P],
                                 prev[:, m - 1, g * 512:(g + 1) * 512],
                                 start=True, stop=True).then_inc(sem["ssd_off"], 1)
            pe.wait_ge(sem["ssd_off_out"], 4 * (MB - 1))
            project_pe(pe, pC_z)
            pe.wait_ge(*pC_z.evac(2 * MB))
            norm_pe(pe, ssd_norm)
            project_pe(pe, pC_ssd, ssd_norm)
            pe.wait_ge(*pC_ssd.evac(2 * MB))
            norm_pe(pe, pre_qkv)

        def ssd_pool(pool, link):
            pool.wait_ge(sem["xT_out"], 2 * MB)
            skip = dskip_row.unsqueeze(2).to_broadcast([P, C_H, HD])
            for m in range(MB):
                link(nc.gpsimd.tensor_tensor(c_y[:, m, :].rearrange("p (h d) -> p h d", d=HD),
                                             c_x[:, m, :].rearrange("p (h d) -> p h d", d=HD), skip, ALU.mult))
            started["y"] = misc["pool_self"].total
            pool.wait_ge(sem["ssd_dt"], 2)
            for g in range(C_G):
                def emit(k, last, g=g):
                    for a in range(2):
                        n = GH * g + a
                        if g or reached(k, a, 2):
                            pool.wait_ge(sem["ssd_seg"], n - 1 + 2 * k)
                        nc.gpsimd.tensor_tensor(
                            segD[a], tri_le[:, :].unsqueeze(1).to_broadcast([P, MB, P]),
                            dtA[:, :, ds(n + 2 * k, 1)].to_broadcast([P, MB, P]),
                            ALU.mult).then_inc(sem["ssd_seg_in"], 1)
                turns(pool, GH // 2, emit)

        def ssd_dve(dve, link):
            S = pC_x
            for b in range(2):
                link(nc.vector.memset(x_in[b][:, 0:TAPS - 1], 0.0))

            def emit(k, s):
                for g in range(S.groups):
                    n = s * S.groups + g
                    src, to, taps = x_in[n % 2], acc[n % 2], conv_taps(4 * k + n)
                    dve.wait_ge(*S.evac(n + 1 + 4 * k))
                    if reached(k, n, 2):
                        dve.wait_ge(sem["conv_out"], n - 1 + 4 * k)
                    nc.vector.tensor_scalar(to, src[:, 0:T], taps[0], conv_b[:, ds(4 * k + n, 1)],
                                            ALU.mult, ALU.add).then_inc(sem["conv_in"], 1)
                    for t in range(1, TAPS):
                        dve.wait_ge(sem["conv_in"], 3 * n + t + 12 * k)
                        ins = nc.vector.scalar_tensor_tensor(to, src[:, t:t + T], taps[t], to, ALU.mult, ALU.add)
                        ins.then_inc(sem["conv_in" if t < TAPS - 1 else "conv_acc"], 1)
            chunk_turns(dve, S, emit)
            dve.wait_ge(*pC_dt.evac(MB))
            link(nc.vector.tensor_tensor(c_u, c_dt, dtb_row.unsqueeze(1).to_broadcast([P, MB, C_H]), ALU.add))
            nc.vector.scalar_tensor_tensor(acs, c_u, -1.0, c_u, ALU.mult, ALU.min).then_inc(sem["ssd_dt"], 1)
            dve.wait_ge(sem["ssd_ready"], 3)
            link(nc.vector.scalar_tensor_tensor(c_dt, c_u, 0.0, acs, ALU.max, ALU.add))
            nc.vector.scalar_tensor_tensor(dtA, c_dt, -1.0, a_neg[:, :].unsqueeze(1).to_broadcast([P, MB, C_H]),
                                           ALU.mult, ALU.mult).then_inc(sem["ssd_dt"], 1)
            for g in range(C_G):
                dve.wait_ge(sem["ssd_sc"], g + 1)
                nc.vector.tensor_tensor(c_sc[:, g],
                                        bank[g][:, :].rearrange("p (m l) -> p m l", m=MB),
                                        tri_le[:, :].unsqueeze(1).to_broadcast([P, MB, P]),
                                        ALU.mult).then_inc(sem["ssd_sc_out"], 1)
            dve.wait_ge(sem["xT_out"], 2 * MB)
            by_head = "p m (h d) -> p (m h) d"
            link(nc.vector.tensor_tensor(c_xdt.rearrange(by_head, d=HD), c_x.rearrange(by_head, d=HD),
                                         c_dt.rearrange("p m h -> p (m h)").unsqueeze(2).to_broadcast([P, MB * C_H, HD]),
                                         ALU.mult))
            dve.wait_ge(sem["ssd_ready"], 4)
            nb = MB - 1
            nc.vector.tensor_tensor(c_xd[:, 0:nb].rearrange(by_head, d=HD), c_xdt[:, 0:nb].rearrange(by_head, d=HD),
                                    eend[:, 0:nb].rearrange("p m h -> p (m h)").unsqueeze(2).to_broadcast([P, nb * C_H, HD]),
                                    ALU.mult).then_inc(sem["ssd_ready"], 1)
            dve.wait_ge(sem["pool_self"], started["y"])
            for g in range(C_G):
                def weigh(k, a, g=g):
                    n = GH * g + a
                    dve.wait_ge(sem["ssd_exp"], n + 1 + 2 * k)
                    nc.vector.tensor_tensor(att[a], att[a], c_sc[:, g],
                                            ALU.mult).then_inc(sem["ssd_att"], 1)

                def add(k, a, g=g):
                    n = GH * g + a
                    dve.wait_ge(sem["ssd_diag"], n + 1 + 2 * k)
                    y = c_y[:, :, ds((n + 2 * k) * HD, HD)]
                    nc.vector.tensor_tensor(y, y, bank[6 + a % 2][:, 0:MB * HD].rearrange("p (m d) -> p m d", m=MB),
                                            ALU.add).then_inc(sem["ssd_y"], 1)

                def emit_heads(k, last):
                    weigh(k, 0)
                    if reached(k, 0, 1):
                        add(k, -1)
                    weigh(k, 1)
                    add(k, 0)
                    if last:
                        add(k, 1)
                turns(dve, GH // 2, emit_heads)
            half = "p (h d) -> p h d"

            def per_head(t, m, g):
                return t[:, m, g * GH:(g + 1) * GH].unsqueeze(2).to_broadcast([P, GH, HD])
            for n in range(2 * (MB - 1)):
                m, g = n // 2, n % 2
                c0 = slice(g * 512, (g + 1) * 512)
                if m:
                    link(nc.vector.tensor_tensor(prev[:, m, c0].rearrange(half, d=HD),
                                                 prev[:, m - 1, c0].rearrange(half, d=HD), per_head(etot, m, g), ALU.mult))
                dve.wait_ge(sem["ssd_state"], n + 1)
                if m:
                    nc.vector.tensor_tensor(prev[:, m, c0], prev[:, m, c0], bank[n % 4][:, :],
                                            ALU.add).then_inc(sem["ssd_prev"], 1)
                    dve.wait_ge(sem["ssd_prev"], n + 1)
                else:
                    nc.vector.tensor_copy(prev[:, m, c0], bank[n % 4][:, :]).then_inc(sem["ssd_prev"], 1)
                    dve.wait_ge(sem["ssd_prev"], n + 1)
            for n in range(2 * (MB - 1)):
                m, g = n // 2 + 1, n % 2
                dve.wait_ge(sem["ssd_off"], n + 1)
                nc.vector.tensor_tensor(off.rearrange(half, d=HD), bank[n % 4][:, :].rearrange(half, d=HD),
                                        per_head(eacs, m, g), ALU.mult).then_inc(sem["ssd_off_out"], 1)
                dve.wait_ge(sem["ssd_off_out"], 2 * n + 1)
                y = c_y[:, m, g * 512:(g + 1) * 512]
                nc.vector.tensor_tensor(y, y, off, ALU.add).then_inc(sem["ssd_off_out"], 1)
                dve.wait_ge(sem["ssd_off_out"], 2 * n + 2)
            for m in range(MB):
                dve.wait_ge(*pC_z.evac(MB + m + 1))
                nc.vector.tensor_tensor(c_y[:, m, :], c_y[:, m, :], c_x[:, m, :], ALU.mult).then_inc(sem["ssd_gated"], 1)
            dve.wait_ge(sem["ssd_gated"], MB)
            norm_dve(dve, ssd_norm)
            norm_dve(dve, pre_qkv)

        SB = 2 * C_H
        st = Staging(staged=C["staged"].take(SB), headT=C["headT"].take(SB), headT_out=C["headT_out"].take(SB))
        w_at = [0, 128, 384, 768]
        hn_ = hn[:, :, :].rearrange("p m d -> p (m d)")
        sp_ = [[view(hn_, 1280 * a + w_at[u], P * (u + 1)) for u in range(4 - a)] for a in range(2)]
        sp_[1].append(junk[:, 0:T])
        w_ = [[cut(3584 + 1280 * a + w_at[u], P * (u + 1)) for u in range(4)] for a in range(2)]

        def stick_pool(pool):
            def stage(k, a):
                if reached(k, a, 2):
                    pool.wait_ge(*st.headT(2 * a - 2 + 4 * k))
                for buf, c0 in ((q_in, 0), (k_in, D)):
                    nc.gpsimd.tensor_copy(buf[a % 2][:, :, 0:HD],
                                          s_qkv[:, :, ds((2 * k + a) * HD + c0, HD)]).then_inc(st.staged.sem, 1)

            def emit(k, last):
                if isinstance(k, int) and k == 0:
                    stage(0, 0)
                for a in range(1, 2 if last else 3):
                    stage(k, a)
            pool.wait_ge(*pC_qkv.evac(6 * MB))
            turns(pool, C_H // 2, emit)

        def stick_pe(pe):
            def turn(k, a, which):
                pe.wait_ge(*st.staged(2 * a + which + 1 + 4 * k))
                for b in range(MB):
                    mm = nc.tensor.transpose(bank[which][0:QK_A, b * P:(b + 1) * P],
                                             (q_in, k_in)[which][a % 2][:, b, :], ident[:, :])
                mm.then_inc(st.headT.sem, 1)

            def score(k, j):
                a, u = j // 4, j % 4
                if u == 0:
                    pe.wait_ge(*st.headT_out(2 * a + 2 + 4 * k))
                if reached(k, j, 4):
                    pe.wait_ge(sem["w_exp"], j - 3 + 8 * k)
                kb = MB - 1 - u
                nc.tensor.matmul(bank[2 + u][:, 0:P * (u + 1)], kT[a][0:HD, kb * P:(kb + 1) * P],
                                 qT[a][0:HD, kb * P:T], start=True, stop=False, skip_group_check=True)
                nc.tensor.matmul(bank[2 + u][:, 0:P], ident_b[:, :], not_before[:, :], start=False,
                                 stop=False, skip_group_check=True).then_inc(sem["z"], 1)

            def remain(k, j):
                if not reached(k, j, 0):
                    return
                a, u = j // 4 % 2, j % 4
                pe.wait_ge(sem["sp"], j + 1 + 8 * k)
                for v in range(u, -1, -1):
                    w = P * (v + 1)
                    c0 = P * (u - v)
                    mm = nc.tensor.matmul(bank[2 + u][:, c0:c0 + w], (neg_ge if v == u else neg_ones)[:, :],
                                          sp_[a][v], start=False, stop=v == 0, skip_group_check=True)
                mm.then_inc(sem["remain"], 1)

            def values(k, a):
                if not reached(k, a, 0):
                    return
                pe.wait_ge(sem["w_exp"], 4 * a + 4 + 8 * k)
                if reached(k, a, 2):
                    pe.wait_ge(sem["s_y"], a - 1 + 2 * k)
                for b in range(MB):
                    for kb in range(b + 1):
                        u = MB - 1 - kb
                        mm = nc.tensor.matmul(
                            bank[6 + a % 2][:, b * HD:(b + 1) * HD], w_[a % 2][u][:, (b - kb) * P:(b - kb + 1) * P],
                            s_qkv[:, kb, ds((2 * k + a) * HD + 2 * D, HD)], start=kb == 0, stop=kb == b)
                mm.then_inc(sem["s_out"], 1)

            def emit(k, last):
                if isinstance(k, int) and k == 0:
                    turn(0, 0, 0)
                    turn(0, 0, 1)
                for j in range(8):
                    score(k, j)
                    if j % 4 in (2, 3) and not (last and j >= 4):
                        turn(k, j // 4 + 1, j % 4 - 2)
                    remain(k, j - 2)
                    if j % 4 == 3:
                        values(k, j // 4 - 1)
                if last:
                    remain(k, 6)
                    remain(k, 7)
                    values(k, 1)
            turns(pe, C_H // 2, emit)

        def stick_act(act):
            def weight_(k, j):
                if reached(k, j, 0):
                    u = j % 4
                    act.wait_ge(sem["remain"], j + 1 + 8 * k)
                    nc.scalar.activation(w_[j // 4 % 2][u], bank[2 + u][:, 0:P * (u + 1)],
                                         ACT.Exp).then_inc(sem["w_exp"], 1)

            nc.scalar.preload_act_table_set("natural_log_exp_and_others")

            def emit(k, last):
                for j in range(8):
                    t = sp_[j // 4][j % 4]
                    act.wait_ge(sem["z_min"], j + 1 + 8 * k)
                    nc.scalar.activation(t, t, ACT.Exp).then_inc(sem["soft"], 1)
                    act.wait_ge(sem["soft"], 2 * j + 1 + 16 * k)
                    nc.scalar.activation(t, t, ACT.Ln, bias=one_t[:, :]).then_inc(sem["soft"], 1)
                    weight_(k, j - 2)
                if last:
                    weight_(k, 6)
                    weight_(k, 7)
            turns(act, C_H // 2, emit)

        def stick_dve(dve):
            def collect(k, a, which):
                dve.wait_ge(*st.headT(2 * a + which + 1 + 4 * k))
                nc.vector.tensor_scalar((qT, kT)[which][a % 2][0:HD, :], bank[which][0:HD, :],
                                        (HD ** -0.5, 1.0)[which], None, ALU.mult).then_inc(st.headT_out.sem, 1)

            def softplus(k, j):
                if reached(k, j, 0):
                    t = sp_[j // 4 % 2][j % 4]
                    dve.wait_ge(sem["soft"], 2 * j + 2 + 16 * k)
                    nc.vector.tensor_tensor(t, bank[2 + j % 4][:, 0:P * (j % 4 + 1)], t,
                                            ALU.max).then_inc(sem["sp"], 1)

            def weigh(k, a):
                if reached(k, a, 0):
                    dve.wait_ge(sem["s_out"], a + 1 + 2 * k)
                    y = gate[:, :, ds((2 * k + a) * HD, HD)]
                    nc.vector.tensor_tensor(y, bank[6 + a % 2][:, 0:MB * HD].rearrange("p (m d) -> p m d", m=MB), y,
                                            ALU.mult).then_inc(sem["s_y"], 1)

            def emit(k, last):
                if isinstance(k, int) and k == 0:
                    collect(0, 0, 0)
                    collect(0, 0, 1)
                for j in range(8):
                    u = j % 4
                    dve.wait_ge(sem["z"], j + 1 + 8 * k)
                    nc.vector.tensor_scalar(sp_[j // 4][u], bank[2 + u][:, 0:P * (u + 1)], SOFT_MAX, None,
                                            ALU.min).then_inc(sem["z_min"], 1)
                    softplus(k, j - 1)
                    if u in (2, 3) and not (last and j >= 4):
                        collect(k, j // 4 + 1, u - 2)
                    if u == 3:
                        weigh(k, j // 4 - 1)
                if last:
                    softplus(k, 7)
                    weigh(k, 1)
            turns(dve, C_H // 2, emit)

        def gates_act(act):
            S = pC_gate

            def sigmoid(n):
                t = g_tmp[n % MB]
                act.wait_ge(*S.evac(n + 1))
                nc.scalar.activation(t, t, ACT.Sigmoid).then_inc(sem["g_sig"], 1)

            def take(k, s, g):
                n = s * MB + g
                if n:
                    sigmoid(n - 1)
            project_act(act, S, take)
            sigmoid(4 * MB - 1)

        def gates_dve(dve):
            S = pC_gate
            dve.wait_ge(row_in.sem, 64)

            def merge(n):
                c, m = n // MB, n % MB
                t = g_tmp[m]
                y = y_ssd[:, m, c % 2 * 512:c % 2 * 512 + 512]
                dve.wait_ge(sem["g_sig"], n + 1)
                if c < 2:
                    nc.vector.tensor_tensor(y, y, t, ALU.mult).then_inc(sem["g_done"], 1)
                else:
                    nc.vector.tensor_tensor(t, y_sb[:, m, c % 2 * 512:c % 2 * 512 + 512], t,
                                            ALU.mult).then_inc(sem["g_merge"], 1)
                    dve.wait_ge(sem["g_merge"], n - 2 * MB + 1)
                    nc.vector.tensor_tensor(y, y, t, ALU.add).then_inc(sem["g_done"], 1)
            dve.wait_ge(*pC_sb.evac(2 * MB))
            for n in range(4 * MB):
                c, m = n // MB, n % MB
                dve.wait_ge(C["product"].sem, S.done(0, c, m))
                if n >= MB:
                    dve.wait_ge(sem["g_done"], n - MB + 1)
                nc.vector.tensor_tensor(g_tmp[m], bank_of(S, c, m)[:, :], b_gate[:, c * 512:(c + 1) * 512],
                                        ALU.add).then_inc(S.evac.sem, 1)
                if n:
                    merge(n - 1)
            merge(4 * MB - 1)
            dve.wait_ge(sem["g_done"], 4 * MB)

        block = ctx.enter_context(nc.Block())

        @block.sync
        def _(sp):
            for m in range(MB):
                sp.dma_start(h[:, m, :], i["x"][0, m * P:(m + 1) * P, :]).then_inc(loaded_x[m].sem, 16)
            project_sp(sp, pA_lat)
            sp.dma_start(mem_in, i["mem"][0].rearrange("(m p) d -> p m d", p=P)).then_inc(loaded_mem.sem, 16)
            for S in (pA_qm, pA_gate, *p_mem, pA_q, pA_kv, pA_out, pB_qkv, pB_f, pB_qm, pB_gate,
                      pB_out, pC_x, pC_dt, pC_z, pC_ssd, pC_qkv, pC_zs, pC_sb, pC_gate, pC_out):
                project_sp(sp, S)
            for m in range(MB):
                sp.wait_ge(*post[2].add(2 * m + 2))
                sp.dma_start(out[0, m * P:(m + 1) * P, :], h[:, m, :]).then_inc(stored.sem, 16)
            sp.wait_ge(stored.sem, 16 * MB)

        @block.gpsimd
        def _(pool):
            link = chain(pool, "pool_self")
            for t, v in ((ident, 0.0), (tri_le, 1.0), (tri_gt, 1.0), (neg_ge, -1.0), (ident_b, 0.0),
                         (later_keys, 0.0), (not_before, 0.0)):
                link(nc.gpsimd.memset(t[:, :], v))
            nc.gpsimd.memset(ones[:, :], 1.0)
            nc.gpsimd.memset(neg_ones[:, :], -1.0)
            nc.gpsimd.memset(eps_t[:, :], EPS)
            nc.gpsimd.memset(one_t[:, :], 1.0)
            for j in range(HALF):
                nc.gpsimd.memset(inv[:, j:j + 1], float(np.float32(ROPE_THETA ** (-j / HALF))))
            for t, cmp, fill, base, step, chan in (
                    (ident, ALU.not_equal, 1.0, 0, -1, 1), (tri_le, ALU.is_ge, 0.0, 0, 1, -1),
                    (tri_gt, ALU.is_ge, 0.0, -1, -1, 1), (neg_ge, ALU.is_ge, 0.0, 0, -1, 1),
                    (ident_b, ALU.not_equal, 1.0, 0, -1, 1),
                    (later_keys, ALU.is_ge, MASKED, 0, -1, 1), (not_before, ALU.is_ge, MASKED, -1, 1, -1)):
                ins = nc.gpsimd.affine_select(out=t[:, :], in_=t[:, :], pattern=[[step, P]], compare_op=cmp,
                                              fill=fill, base=base, channel_multiplier=chan)
            ins.then_inc(consts.sem, 1)

            for p in range(2):
                pool.wait_ge(w_high.sem, p + 1)
                rest(p, pieces[p][0] * pieces[p][1])
            for S in (pA_lat, pA_qm, pA_gate, *p_mem, pA_q):
                project_pool(pool, S)

            def early_A(a):
                if a == 0:
                    pool.wait_ge(*pre_mem.scaled(MEMB))
                    pool.wait_ge(sem["kr_done"], 1)
                    for b in range(2):
                        link(nc.gpsimd.tensor_copy(k_in[b][:, :, NOPE:QK_A], k_rot))
                    pool.wait_ge(sem["rope_done"], 1)
                    pool.wait_ge(*pA_kv.evac(MB))
                stage_head(pool, attA, 0, a)
            project_pool(pool, pA_kv, early_A)
            attend_pool(pool, attA, pA_kv.evac(3 * MB))
            pool.wait_ge(*p_mem[1].evac(MEMB))
            pool.wait_ge(*pA_qm.evac(MB))
            pool.wait_ge(*attA.headT(2 * A_H))
            attend_pool(pool, attAm, staged=False)
            pool.dma_start(row[:, :], i["norm_post"][0:1, :].partition_broadcast(P)).then_inc(row_in.sem, 16)
            pool.wait_ge(*attAm.headT(2 * MEM_H))
            pool.dma_start(G_PRE[1], i["norm_pre"][1:2, :].partition_broadcast(P)).then_inc(gain_in.sem, 16)
            project_pool(pool, pA_out)
            post_pool(pool, post[0])
            for S in (pB_qkv, pB_f, pB_qm):
                project_pool(pool, S)

            pool.wait_ge(*attAm.headT(2 * MEM_H))
            for a in range(2):
                nc.gpsimd.memset(q_in[a][:, :, HD:HD + 1], HD ** 0.5)
                link(nc.gpsimd.memset(k_in[a][:, :, HD + 1:HD + 2], 1.0))

            def early_B(a):
                if a == 0:
                    pool.wait_ge(*pB_qkv.evac(6 * MB))
                    pool.wait_ge(sem["sums_out"], 2)
                stage_head(pool, attB, 0, a)
            project_pool(pool, pB_gate, early_B)
            attend_pool(pool, attB)
            pool.wait_ge(*pB_qm.evac(MB))
            pool.wait_ge(*attB.headT(2 * B_H))
            attend_pool(pool, attBm, staged=False)
            project_pool(pool, pB_out)
            pool.wait_ge(*post[0].out(3 * MB))
            pool.dma_start(row[:, :], i["norm_post"][1:2, :].partition_broadcast(P)).then_inc(row_in.sem, 16)
            pool.wait_ge(*attBm.attended(4 * MEM_H))
            pool.dma_start(G_PRE[2], i["norm_pre_2"].partition_broadcast(P)).then_inc(gain_in.sem, 16)
            post_pool(pool, post[1])

            project_pool(pool, pC_x)
            project_pool(pool, pC_dt)
            ssd_pool(pool, link)
            pool.wait_ge(sem["ssd_seg"], C_H)
            pool.dma_start(G_SSD, i["ssd_norm_2"].partition_broadcast(P)).then_inc(gain_in.sem, 16)
            pool.wait_ge(sem["ssd_y"], C_H)
            pool.wait_ge(sem["ssd_ready"], 5)
            pool.dma_start(G_QKV, i["norm_pre_2"].partition_broadcast(P)).then_inc(gain_in.sem, 16)
            for S in (pC_z, pC_ssd, pC_qkv, pC_zs):
                project_pool(pool, S)
            stick_pool(pool)
            pool.wait_ge(sem["s_out"], C_H)
            pool.dma_start(G_GATE, i["norm_pre_2"].partition_broadcast(P)).then_inc(gain_in.sem, 16)
            pool.dma_start(b_gate, i["b_gate_2"].partition_broadcast(P)).then_inc(row_in.sem, 16)
            pool.dma_start(row[:, :], i["norm_post_2"].partition_broadcast(P)).then_inc(row_in.sem, 16)
            for S in (pC_sb, pC_gate, pC_out):
                project_pool(pool, S)
            post_pool(pool, post[2])

        @block.scalar
        def _(act):
            act.dma_start(G_PRE[0], i["norm_pre"][0:1, :].partition_broadcast(P)).then_inc(params_first.sem, 16)
            act.wait_ge(consts.sem, 1)
            norm_act(act, pre[0], lambda m: (loaded_x[m].sem, 16))
            for p in range(2):
                high_part(act, p, pieces[p][0] * pieces[p][1])
            with nc.allow_non_contiguous_dma("a few parameters, once"):
                act.dma_start(pos_i[:, :], i["positions"].rearrange("o (m p) -> p (o m)", p=P)).then_inc(params.sem, 16)
                act.dma_start(G_MEM, i["mem_norm"].partition_broadcast(P)).then_inc(gain_first.sem, 16)
                act.dma_start(G_LAT[:, 0:Q_LORA], i["q_norm_a"].partition_broadcast(P)).then_inc(gain_first.sem, 16)
                act.dma_start(G_LAT[:, Q_LORA:], i["kv_norm_a"].partition_broadcast(P)).then_inc(gain_first.sem, 16)
                for t in range(TAPS):
                    act.dma_start(conv_k[:, t, :], i["conv_w_2"][0, t].rearrange("(c p) -> p c", p=P)).then_inc(params.sem, 16)
                act.dma_start(conv_b[:, :], i["conv_b_2"][0].rearrange("(c p) -> p c", p=P)).then_inc(params.sem, 16)
                for n, r in (("b_f", bf_row), ("dt_bias_2", dtb_row), ("a_log_2", alog_row), ("d_skip_2", dskip_row)):
                    act.dma_start(r, i[n].partition_broadcast(P)).then_inc(params.sem, 16)
            project_act(act, pA_lat)
            act.wait_ge(params.sem, 16 * 10)
            act.wait_ge(sem["rope_ang"], 1)
            nc.scalar.activation(trig, turned, ACT.Sin).then_inc(sem["rope_trig"], 1)
            project_act(act, pA_qm)
            norm_act(act, pre_mem, lambda m: (loaded_mem.sem, 16), rounds=False)
            project_act(act, pA_gate)
            norm_act(act, latent, rounds=False)
            round_all_act(act, pre_mem)
            for S in p_mem:
                project_act(act, S)
            round_all_act(act, latent)
            project_act(act, pA_q)
            project_act(act, pA_kv, early=lambda: enter_act(act, attA))
            attend_act(act, attA, attAm)
            attend_act(act, attAm)
            round_all_act(act, ytA)
            nc.scalar.preload_act_table_set("sqrt_and_others")
            project_act(act, pA_out)
            post_act(act, post[0], pA_out, latent.sq(2 * MB), pre[1])
            project_act(act, pB_qkv)
            project_act(act, pB_f)
            act.wait_ge(sem["gates_in"], 1)
            nc.scalar.activation(b_t, b_t, ACT.Exp).then_inc(sem["gates_exp"], 1)
            act.wait_ge(sem["gates_exp"], 1)
            nc.scalar.activation(b_t, b_t, ACT.Ln, bias=one_t[:, :]).then_inc(sem["gates_log"], 1)
            project_act(act, pB_qm)
            project_act(act, pB_gate, early=lambda: enter_act(act, attB))
            attend_act(act, attB, attBm)
            attend_act(act, attBm)
            round_all_act(act, ytB)
            nc.scalar.preload_act_table_set("sqrt_and_others")
            project_act(act, pB_out)
            post_act(act, post[1], pB_out, pre[1].sq(MB), pre[2])
            ssd_act(act)
            project_act(act, pC_qkv)
            project_act(act, pC_zs)
            stick_act(act)
            round_all_act(act, ytC)
            norm_act(act, pre_gate, rounds=False)
            project_act(act, pC_sb)
            round_all_act(act, pre_gate)
            gates_act(act)
            round_all_act(act, ytM)
            nc.scalar.preload_act_table_set("sqrt_and_others")
            project_act(act, pC_out)
            post_act(act, post[2], pC_out, pre_gate.sq(MB))

        @block.vector
        def _(dve):
            link = chain(dve, "dve_self")
            dve.wait_ge(consts.sem, 1)
            norm_dve(dve, pre[0])
            dve.wait_ge(params.sem, 16 * 10)
            link(nc.vector.tensor_copy(pos_f[:, :], pos_i[:, :]))
            link(nc.vector.tensor_tensor(trig[:, 0], pos_f[:, :].unsqueeze(2).to_broadcast([P, MB, HALF]),
                                         inv[:, :].unsqueeze(1).to_broadcast([P, MB, HALF]), ALU.mult))
            rounder = 1.5 * 2.0 ** 23
            for n in range(2):
                link(nc.vector.tensor_scalar(turns_n[:, n], trig[:, 0], float(1 / (2 * np.pi)), 0.25 * n, ALU.mult, ALU.add))
                link(nc.vector.tensor_scalar(turns_n[:, n], turns_n[:, n], rounder, None, ALU.add))
                link(nc.vector.tensor_scalar(turns_n[:, n], turns_n[:, n], rounder, None, ALU.subtract))
                src = trig[:, 0]
                two_pi = 2 * np.pi
                c1 = 6.28125
                c2 = float(np.float32(np.round((two_pi - c1) * 2 ** 20) / 2 ** 20))
                c3 = float(two_pi - c1 - c2)
                for c in (c1, c2, c3):
                    link(nc.vector.scalar_tensor_tensor(turned[:, n], turns_n[:, n], -c, src, ALU.mult, ALU.add))
                    src = turned[:, n]
                if n:
                    link(nc.vector.tensor_scalar(turned[:, n], turned[:, n], float(np.pi / 2), None, ALU.add))
                pi_ = float(np.nextafter(np.float32(np.pi), np.float32(0)))
                link(nc.vector.tensor_scalar(turned[:, n], turned[:, n], pi_, -pi_, ALU.min, ALU.max))
            nc.vector.tensor_copy(done_t[:, :], pos_f[:, 0:1]).then_inc(sem["rope_ang"], 1)
            norm_dve(dve, pre_mem)

            def rotate(x1, x2, y1, y2, c, s, t):
                for n, (x, f) in enumerate(((x1, c), (x2, s), (x2, c), (x1, s))):
                    ins = nc.vector.tensor_tensor(t[n], x, f, ALU.mult)
                link(ins)
                nc.vector.tensor_tensor(y1, t[0], t[1], ALU.subtract)
                return nc.vector.tensor_tensor(y2, t[2], t[3], ALU.add)

            dve.wait_ge(sem["rope_trig"], 1)
            dve.wait_ge(*pA_lat.evac(2 * MB))
            kr = Q_LORA + KV_LORA
            rotate(lat[:, :, kr:kr + HALF], lat[:, :, kr + HALF:kr + ROPE], k_rot[:, :, 0:HALF],
                   k_rot[:, :, HALF:ROPE], trig[:, 1], trig[:, 0], rot_k).then_inc(sem["kr_done"], 1)
            norm_dve(dve, latent)
            dve.wait_ge(*pA_q.evac(3 * MB))
            for m in range(MB):
                v = a_q[:, m, :].rearrange("p (h c) -> p h c", c=QK_A)
                x1, x2 = v[:, :, NOPE:NOPE + HALF], v[:, :, NOPE + HALF:QK_A]
                b = [trig[:, n, m, :].unsqueeze(1).to_broadcast([P, A_H, HALF]) for n in (1, 0)]
                ins = rotate(x1, x2, x1, x2, b[0], b[1], [t[:, m * A_H:(m + 1) * A_H, :] for t in rot])
            ins.then_inc(sem["rope_done"], 1)
            attend_dve(dve, attA)
            attend_dve(dve, attAm)
            norm_dve(dve, ytA)
            post_dve(dve, post[0], (row_in.sem, 16), pre[1])
            dve.wait_ge(*pB_f.evac(MB))
            link(nc.vector.tensor_tensor(b_f, b_f, bf_row.unsqueeze(1).to_broadcast([P, MB, B_H]), ALU.add))
            nc.vector.scalar_tensor_tensor(b_t, b_f, -1.0, b_f, ALU.mult, ALU.min).then_inc(sem["gates_in"], 1)
            dve.wait_ge(sem["gates_log"], 1)
            nc.vector.scalar_tensor_tensor(b_u, b_f, 0.0, b_t, ALU.min, ALU.subtract).then_inc(sem["gates_in"], 1)
            dve.wait_ge(sem["sums"], 1)
            f_sum = sum_bank[:, 0:MB * B_H].rearrange("p (m h) -> p m h", m=MB)
            nc.vector.tensor_scalar(b_F, f_sum, -1.0, None, ALU.mult).then_inc(sem["sums_out"], 1)
            nc.vector.tensor_scalar(b_8F, f_sum, HD ** 0.5, None, ALU.mult).then_inc(sem["sums_out"], 1)
            attend_dve(dve, attB)
            attend_dve(dve, attBm)
            norm_dve(dve, ytB)
            post_dve(dve, post[1], (row_in.sem, 32), pre[2])
            ssd_dve(dve, link)
            stick_dve(dve)
            norm_dve(dve, ytC)
            norm_dve(dve, pre_gate)
            gates_dve(dve)
            norm_dve(dve, ytM)
            post_dve(dve, post[2], (row_in.sem, 64))

        @block.tensor
        def _(pe):
            pe.wait_ge(consts.sem, 1)
            norm_pe(pe, pre[0])
            project_pe(pe, pA_lat, pre[0])
            project_pe(pe, pA_qm)
            project_pe(pe, pA_gate)
            pe.wait_ge(*pA_gate.evac(2 * MB))
            norm_pe(pe, pre_mem)
            project_pe(pe, p_mem[0], pre_mem)
            project_pe(pe, p_mem[1])
            pe.wait_ge(*p_mem[1].evac(MEMB))
            norm_pe(pe, latent)
            project_pe(pe, pA_q, latent)
            project_pe(pe, pA_kv)
            enter_pe(pe, pA_kv, attA)
            attend_pe(pe, attA, attAm)
            pe.wait_ge(*attA.weighed(4 * A_H))
            attend_pe(pe, attAm)
            pe.wait_ge(*attAm.weighed(4 * MEM_H))
            norm_pe(pe, ytA)
            project_pe(pe, pA_out, ytA)
            norm_pe(pe, pre[1])
            project_pe(pe, pB_qkv, pre[1])
            project_pe(pe, pB_f)
            project_pe(pe, pB_qm)
            pe.wait_ge(*pB_f.evac(MB))
            pe.wait_ge(sem["gates_in"], 2)
            for m in range(MB):
                to = sum_bank[:, m * B_H:(m + 1) * B_H]
                for c in range(m + 1):
                    mm = nc.tensor.matmul(to, (tri_le if c == m else ones)[:, :], b_u[:, c, :],
                                          start=c == 0, stop=c == m)
            mm.then_inc(sem["sums"], 1)
            pe.wait_ge(sem["sums_out"], 2)
            project_pe(pe, pB_gate)
            enter_pe(pe, pB_gate, attB)
            attend_pe(pe, attB, attBm)
            pe.wait_ge(*attB.weighed(4 * B_H))
            attend_pe(pe, attBm)
            pe.wait_ge(*attBm.weighed(4 * MEM_H))
            norm_pe(pe, ytB)
            project_pe(pe, pB_out, ytB)
            norm_pe(pe, pre[2])
            pe.wait_ge(*pre[2].normed(2 * MB))
            ssd_pe(pe)
            project_pe(pe, pC_qkv, pre_qkv)
            project_pe(pe, pC_zs)
            pe.wait_ge(*pC_zs.evac(2 * MB))
            stick_pe(pe)
            pe.wait_ge(sem["s_y"], C_H)
            norm_pe(pe, ytC)
            project_pe(pe, pC_sb, ytC)
            pe.wait_ge(*pC_sb.evac(2 * MB))
            norm_pe(pe, pre_gate)
            project_pe(pe, pC_gate, pre_gate)
            norm_pe(pe, ytM, lambda m: (sem["g_done"], 3 * MB + m + 1))
            project_pe(pe, pC_out, ytM)


def kernel(**inputs):
    import concourse.bacc as bacc
    from concourse.bass_utils import run_bass_kernel_spmd

    nc = bacc.Bacc("TRN2", target_bir_lowering=False, num_devices=1)
    arrays, args = {}, {}
    for name, value in inputs.items():
        a = np.ascontiguousarray(value)
        arrays[f"in_{name}"] = a
        args[name] = nc.dram_tensor(f"in_{name}", a.shape, mybir.dt.from_np(a.dtype), kind="ExternalInput").ap()
    out = nc.dram_tensor("out_0", (1, T, D), F32, kind="ExternalOutput").ap()
    build(nc, args, out)
    r = run_bass_kernel_spmd(nc, [arrays], core_ids=[0])
    return r.results[0]["out_0"]
```
